# Optimizing a Trainium2 kernel written in Bass

```python
import jax, jax.numpy as jnp
from jax import lax
import numpy as np

D_MODEL = 1024
BATCH = 1
SEQ = 128
DEPTH = 4
DEC_BATCH = 1
DEC_SEQ = 128
PAST_LEN = 128

GRID_W = 64
MIXER_KINDS = ('attn', 'mlstm', 'gla')
N_MIXERS = 3
EPS = 1e-6
ATT_HEADS = 16
ATT_KV_HEADS = 4
ATT_GROUP = ATT_HEADS // ATT_KV_HEADS
HEAD_DIM = D_MODEL // ATT_HEADS
WINDOW = 128
Q_BLOCK = 128
ROPE_BASE = 10000.0
MLSTM_HEADS = 8
MLSTM_DK = D_MODEL // MLSTM_HEADS
MLSTM_DV = 2 * D_MODEL // MLSTM_HEADS
MLSTM_CHUNK = 64
CONV_W = 3
GLA_HEADS = 4
GLA_DK = D_MODEL // 2 // GLA_HEADS
GLA_DV = D_MODEL // GLA_HEADS
GLA_GATE_RANK = 16
GLA_TAU = 16.0
GLA_CHUNK = 16
N_EXPERTS = 16
N_GROUPS = 4
EXPERTS_PER_GROUP = N_EXPERTS // N_GROUPS
TOP_K = 2
D_EXPERT = D_MODEL // 2

kernel_name = 'hybrid_dit_attn_mlstm_gla_moe_step'

def rmsnorm(x, g):
    xf = x.astype(jnp.float32)
    y = xf * lax.rsqrt(jnp.mean(xf * xf, axis=-1, keepdims=True) + EPS)
    return (y * g.astype(jnp.float32)).astype(x.dtype)

def head_rmsnorm(x, g):
    xf = x.astype(jnp.float32)
    y = xf * lax.rsqrt(jnp.mean(xf * xf, axis=-1, keepdims=True) + EPS)
    return y * g.astype(jnp.float32).reshape(x.shape[2], x.shape[3])

def adaln(cvec, w_mod, b_mod):
    m = jax.nn.silu(cvec) @ w_mod + b_mod
    return [t[:, None, :] for t in jnp.split(m, 6, axis=-1)]

def flip(x):
    return jnp.flip(x, axis=1)

def short_conv(x, w):
    xp = jnp.pad(x, ((0, 0), (1, 1), (0, 0)))
    return xp[:, :-2] * w[0] + xp[:, 1:-1] * w[1] + xp[:, 2:] * w[2]

def axial_rope(x):
    T = x.shape[1]
    rows = T // GRID_W
    row = jnp.repeat(jnp.arange(rows, dtype=jnp.int32), GRID_W)
    col = jnp.tile(jnp.arange(GRID_W, dtype=jnp.int32), rows)
    half = HEAD_DIM // 2
    nf = half // 2
    inv = ROPE_BASE ** (-jnp.arange(nf, dtype=jnp.float32) / nf)
    xf = x.astype(jnp.float32)

    def rot(xa, pos):
        ang = pos.astype(jnp.float32)[:, None] * inv[None, :]
        cos = jnp.cos(ang)[None, :, None, :]
        sin = jnp.sin(ang)[None, :, None, :]
        x1, x2 = xa[..., :nf], xa[..., nf:]
        return jnp.concatenate([x1 * cos - x2 * sin, x2 * cos + x1 * sin], axis=-1)

    return jnp.concatenate([rot(xf[..., :half], row), rot(xf[..., half:], col)], axis=-1).astype(x.dtype)

def attend(qb, k, v, mask, sink):
    s = jnp.einsum('bqkgd,bnkd->bkgqn', qb, k).astype(jnp.float32) * HEAD_DIM ** -0.5
    if mask is not None:
        s = jnp.where(mask, s, -jnp.inf)
    sk = sink.astype(jnp.float32).reshape(1, ATT_KV_HEADS, ATT_GROUP, 1, 1)
    m = jnp.maximum(s.max(axis=-1, keepdims=True), sk)
    p = jnp.exp(s - m)
    den = p.sum(axis=-1, keepdims=True) + jnp.exp(sk - m)
    return jnp.einsum('bkgqn,bnkd->bqkgd', (p / den).astype(v.dtype), v)

def attn_qkv(h, w_qkv):
    B, T, _ = h.shape
    qkv = h @ w_qkv
    qw = ATT_HEADS * HEAD_DIM
    kw = ATT_KV_HEADS * HEAD_DIM
    q = qkv[..., :qw].reshape(B, T, ATT_HEADS, HEAD_DIM)
    k = qkv[..., qw:qw + kw].reshape(B, T, ATT_KV_HEADS, HEAD_DIM)
    v = qkv[..., qw + kw:].reshape(B, T, ATT_KV_HEADS, HEAD_DIM)
    return q, k, v

def q_blocks(q):
    B, T = q.shape[:2]
    nb = T // Q_BLOCK
    return q.reshape(B, nb, Q_BLOCK, ATT_KV_HEADS, ATT_GROUP, HEAD_DIM).transpose(1, 0, 2, 3, 4, 5)

def merge_blocks(out, B, T):
    return out.transpose(1, 0, 2, 3, 4, 5).reshape(B, T, ATT_HEADS * HEAD_DIM)

def attn_context(h, w_qkv, sink, w_o):
    B, T, _ = h.shape
    q, k, v = attn_qkv(h, w_qkv)
    out = lax.map(lambda qb: attend(qb, k, v, None, sink), q_blocks(q))
    return merge_blocks(out, B, T) @ w_o, (k, v)

def attn_latent(h, state, w_qkv, sink, w_o):
    ck, cv = state
    B, T, _ = h.shape
    Lc = ck.shape[1]
    q, k, v = attn_qkv(h, w_qkv)
    q = axial_rope(q)
    k = axial_rope(k)
    pad = ((0, 0), (WINDOW, WINDOW), (0, 0), (0, 0))
    k_pad = jnp.pad(k, pad)
    v_pad = jnp.pad(v, pad)
    span = Q_BLOCK + 2 * WINDOW
    ctx_mask = jnp.ones((Q_BLOCK, Lc), dtype=bool)

    def block(args):
        qb, i = args
        start = i * Q_BLOCK
        kw = lax.dynamic_slice_in_dim(k_pad, start, span, axis=1)
        vw = lax.dynamic_slice_in_dim(v_pad, start, span, axis=1)
        qpos = start + jnp.arange(Q_BLOCK)
        kpos = start - WINDOW + jnp.arange(span)
        win = (jnp.abs(qpos[:, None] - kpos[None, :]) <= WINDOW) & (kpos >= 0)[None, :] & (kpos < T)[None, :]
        mask = jnp.concatenate([ctx_mask, win], axis=1)
        return attend(qb, jnp.concatenate([ck.astype(kw.dtype), kw], axis=1),
                      jnp.concatenate([cv.astype(vw.dtype), vw], axis=1), mask, sink)

    out = lax.map(block, (q_blocks(q), jnp.arange(T // Q_BLOCK)))
    return merge_blocks(out, B, T) @ w_o

def mlstm_scan(q, k, v, log_i, log_f, C0, n0, m0):
    B, T, H, dk = q.shape
    dv = v.shape[-1]
    L = MLSTM_CHUNK
    nc = T // L

    def chunks(x):
        return x.reshape(B, nc, L, *x.shape[2:]).swapaxes(0, 1)

    causal = jnp.tril(jnp.ones((L, L), dtype=bool))

    def step(carry, xs):
        C, n, m = carry
        qc, kc, vc, ic, fc = xs
        b = jnp.cumsum(fc, axis=1)
        dmat = b[:, :, None, :] - b[:, None, :, :] + ic[:, None, :, :]
        dmat = jnp.where(causal[None, :, :, None], dmat, -jnp.inf)
        inter = b + m[:, None, :]
        m_t = jnp.maximum(inter, dmat.max(axis=2))
        w = jnp.exp(dmat - m_t[:, :, None, :])
        qk = jnp.einsum('bthd,bshd->btsh', qc, kc) * w
        sc = jnp.exp(inter - m_t)
        num = sc[..., None] * jnp.einsum('bhvd,bthd->bthv', C, qc) + jnp.einsum('btsh,bshv->bthv', qk, vc)
        den = sc * jnp.einsum('bhd,bthd->bth', n, qc) + qk.sum(axis=2)
        hc = num / jnp.maximum(jnp.abs(den), jnp.exp(-m_t))[..., None]
        b_last = b[:, -1]
        wlog = b_last[:, None, :] - b + ic
        m_new = jnp.maximum(b_last + m, wlog.max(axis=1))
        decay = jnp.exp(b_last + m - m_new)
        ws = jnp.exp(wlog - m_new[:, None, :])
        C_new = decay[..., None, None] * C + jnp.einsum('bsh,bshv,bshd->bhvd', ws, vc, kc)
        n_new = decay[..., None] * n + jnp.einsum('bsh,bshd->bhd', ws, kc)
        return (C_new, n_new, m_new), hc

    xs = (chunks(q), chunks(k), chunks(v), chunks(log_i), chunks(log_f))
    state, hs = lax.scan(step, (C0, n0, m0), xs)
    return hs.swapaxes(0, 1).reshape(B, T, H, dv), state

def mlstm_mixer(h, state, w_in, b_gates, conv_w, norm_g, w_out):
    B, T, _ = h.shape
    f32 = jnp.float32
    qk_w = MLSTM_HEADS * MLSTM_DK
    v_w = MLSTM_HEADS * MLSTM_DV
    p = h @ w_in
    qk = jax.nn.silu(short_conv(p[..., :2 * qk_w], conv_w))
    q = qk[..., :qk_w].reshape(B, T, MLSTM_HEADS, MLSTM_DK).astype(f32)
    k = qk[..., qk_w:].reshape(B, T, MLSTM_HEADS, MLSTM_DK).astype(f32) * MLSTM_DK ** -0.5
    v = p[..., 2 * qk_w:2 * qk_w + v_w].reshape(B, T, MLSTM_HEADS, MLSTM_DV).astype(f32)
    o = jax.nn.sigmoid(p[..., 2 * qk_w + v_w:2 * qk_w + 2 * v_w])
    g = (p[..., 2 * qk_w + 2 * v_w:] + b_gates).astype(f32).reshape(B, T, 2, 2, MLSTM_HEADS)
    C0, n0, m0 = (s.astype(f32) for s in state)
    hf, (Cf, nf, mf) = mlstm_scan(q, k, v, g[:, :, 0, 0], jax.nn.log_sigmoid(g[:, :, 0, 1]),
                                  C0[:, 0], n0[:, 0], m0[:, 0])
    hb, (Cb, nb, mb) = mlstm_scan(flip(q), flip(k), flip(v), flip(g[:, :, 1, 0]),
                                  flip(jax.nn.log_sigmoid(g[:, :, 1, 1])), C0[:, 1], n0[:, 1], m0[:, 1])
    hsum = head_rmsnorm(hf + flip(hb), norm_g).astype(h.dtype).reshape(B, T, v_w)
    y = (o * hsum) @ w_out
    return y, (jnp.stack([Cf, Cb], axis=1), jnp.stack([nf, nb], axis=1), jnp.stack([mf, mb], axis=1))

def gla_scan(q, k, v, log_a, S0):
    B, T, H, dk = q.shape
    dv = v.shape[-1]
    L = GLA_CHUNK
    nc = T // L
    qc = q.reshape(B, nc, L, H, dk)
    kc = k.reshape(B, nc, L, H, dk)
    vc = v.reshape(B, nc, L, H, dv)
    bc = jnp.cumsum(log_a.reshape(B, nc, L, H, dk), axis=2)
    causal = jnp.tril(jnp.ones((L, L), dtype=bool))
    diff = bc[:, :, :, None] - bc[:, :, None, :]
    diff = jnp.where(causal[None, None, :, :, None, None], diff, -jnp.inf)
    A = jnp.einsum('bcthd,bcshd,bctshd->bchts', qc, kc, jnp.exp(diff))
    o_intra = jnp.einsum('bchts,bcshv->bcthv', A, vc)
    b_last = bc[:, :, -1]
    k_dec = kc * jnp.exp(b_last[:, :, None] - bc)
    chunk_kv = jnp.einsum('bcshd,bcshv->bchdv', k_dec, vc)

    def step(S, xs):
        dec, kv = xs
        return jnp.exp(dec)[..., None] * S + kv, S

    S_final, S_prev = lax.scan(step, S0, (b_last.swapaxes(0, 1), chunk_kv.swapaxes(0, 1)))
    o_inter = jnp.einsum('bcthd,cbhdv->bcthv', qc * jnp.exp(bc), S_prev)
    return (o_intra + o_inter).reshape(B, T, H, dv), S_final

def gla_mixer(h, state, w_in, w_a1, w_a2, b_a, norm_g, w_out):
    B, T, _ = h.shape
    f32 = jnp.float32
    kw = GLA_HEADS * GLA_DK
    vw = GLA_HEADS * GLA_DV
    p = h @ w_in
    q = p[..., :kw].reshape(B, T, GLA_HEADS, GLA_DK).astype(f32) * GLA_DK ** -0.5
    k = p[..., kw:2 * kw].reshape(B, T, GLA_HEADS, GLA_DK).astype(f32)
    v = p[..., 2 * kw:2 * kw + vw].reshape(B, T, GLA_HEADS, GLA_DV).astype(f32)
    r = p[..., 2 * kw + vw:]

    def log_gate(d):
        z = (h @ w_a1[d]) @ w_a2[d] + b_a[d]
        return jax.nn.log_sigmoid(z.astype(f32)).reshape(B, T, GLA_HEADS, GLA_DK) / GLA_TAU

    (S0,) = state
    S0 = S0.astype(f32)
    of, Sf = gla_scan(q, k, v, log_gate(0), S0[:, 0])
    ob, Sb = gla_scan(flip(q), flip(k), flip(v), flip(log_gate(1)), S0[:, 1])
    o = head_rmsnorm(of + flip(ob), norm_g).astype(h.dtype).reshape(B, T, vw)
    y = (o * jax.nn.silu(r)) @ w_out
    return y, (jnp.stack([Sf, Sb], axis=1),)

def moe(h, router_w, router_b, wg, wu, wd):
    B, T, D = h.shape
    x = h.reshape(B * T, D)
    scores = jax.nn.sigmoid((x @ router_w).astype(jnp.float32))
    sel = scores + router_b.astype(jnp.float32)
    gscore = lax.top_k(sel.reshape(-1, N_GROUPS, EXPERTS_PER_GROUP), 2)[0].sum(axis=-1)
    gbest = jnp.argmax(gscore, axis=-1)
    in_group = (jnp.arange(N_EXPERTS) // EXPERTS_PER_GROUP)[None, :] == gbest[:, None]
    _, idx = lax.top_k(jnp.where(in_group, sel, -jnp.inf), TOP_K)
    w = jnp.take_along_axis(scores, idx, axis=-1)
    w = w / w.sum(axis=-1, keepdims=True)
    combine = jnp.einsum('nk,nke->ne', w, jax.nn.one_hot(idx, N_EXPERTS, dtype=jnp.float32))
    hid = jax.nn.silu(jnp.einsum('nd,edf->nef', x, wg)) * jnp.einsum('nd,edf->nef', x, wu)
    y = jnp.einsum('nef,efd->nd', hid * combine[..., None].astype(hid.dtype), wd)
    return y.reshape(B, T, D)

def setup_inputs(seed: int = 0) -> dict:
    key = jax.random.key(seed)
    ks = iter(jax.random.split(key, 48))
    f32 = jnp.float32

    def nrm(shape, scale=1.0):
        return jax.random.normal(next(ks), shape, f32) * scale

    D = D_MODEL
    qk_w = MLSTM_HEADS * MLSTM_DK
    v_w = MLSTM_HEADS * MLSTM_DV
    att_cols = (ATT_HEADS + 2 * ATT_KV_HEADS) * HEAD_DIM
    gla_cols = 2 * GLA_HEADS * GLA_DK + 2 * GLA_HEADS * GLA_DV
    mlstm_cols = 2 * qk_w + 2 * v_w + 4 * MLSTM_HEADS
    kv_shape = (DEC_BATCH, PAST_LEN, ATT_KV_HEADS, HEAD_DIM)
    d = {}
    d['x_prompt'] = nrm((BATCH, SEQ, D))
    d['x_sample'] = nrm((DEC_BATCH, DEC_SEQ, D))
    d['cache_k_0'] = nrm(kv_shape)
    d['cache_v_0'] = nrm(kv_shape)
    d['state_mlstm_C_1'] = nrm((DEC_BATCH, 2, MLSTM_HEADS, MLSTM_DV, MLSTM_DK), 0.1)
    d['state_mlstm_n_1'] = nrm((DEC_BATCH, 2, MLSTM_HEADS, MLSTM_DK), 0.1)
    d['state_mlstm_m_1'] = nrm((DEC_BATCH, 2, MLSTM_HEADS), 0.5)
    d['state_gla_S_2'] = nrm((DEC_BATCH, 2, GLA_HEADS, GLA_DK, GLA_DV), 0.1)
    d['cache_k_3'] = nrm(kv_shape)
    d['cache_v_3'] = nrm(kv_shape)
    d['c'] = nrm((DEC_BATCH, D))
    d['c_ctx'] = nrm((D,))
    d['w_mod'] = nrm((DEPTH, D, 6 * D), 0.5 * D ** -0.5)
    d['b_mod'] = nrm((DEPTH, 6 * D), 0.01)
    d['norm1_g'] = 1.0 + nrm((DEPTH, D), 0.1)
    d['norm2_g'] = 1.0 + nrm((DEPTH, D), 0.1)
    d['final_g'] = 1.0 + nrm((D,), 0.1)
    d['router_w'] = nrm((D, N_EXPERTS), D ** -0.5)
    d['router_b'] = nrm((N_EXPERTS,), 0.01)
    d['moe_wg'] = nrm((DEPTH, N_EXPERTS, D, D_EXPERT), D ** -0.5)
    d['moe_wu'] = nrm((DEPTH, N_EXPERTS, D, D_EXPERT), D ** -0.5)
    d['moe_wd'] = nrm((DEPTH, N_EXPERTS, D_EXPERT, D), D_EXPERT ** -0.5)
    d['attn0_w_qkv'] = nrm((D, att_cols), D ** -0.5)
    d['attn0_sink'] = nrm((ATT_HEADS,))
    d['attn0_w_o'] = nrm((ATT_HEADS * HEAD_DIM, D), (ATT_HEADS * HEAD_DIM) ** -0.5)
    d['mlstm1_w_in'] = nrm((D, mlstm_cols), D ** -0.5)
    d['mlstm1_b_gates'] = (nrm((2, 2, MLSTM_HEADS), 0.1) + jnp.array([0.0, 3.0], f32)[None, :, None]).reshape(-1)
    d['mlstm1_conv'] = nrm((CONV_W, 2 * qk_w), 0.2) + jnp.array([0.0, 1.0, 0.0], f32)[:, None]
    d['mlstm1_norm_g'] = 1.0 + nrm((v_w,), 0.1)
    d['mlstm1_w_out'] = nrm((v_w, D), v_w ** -0.5)
    d['gla2_w_in'] = nrm((D, gla_cols), D ** -0.5)
    d['gla2_w_a1'] = nrm((2, D, GLA_GATE_RANK), D ** -0.5)
    d['gla2_w_a2'] = nrm((2, GLA_GATE_RANK, GLA_HEADS * GLA_DK), GLA_GATE_RANK ** -0.5)
    d['gla2_b_a'] = nrm((2, GLA_HEADS * GLA_DK), 0.5)
    d['gla2_norm_g'] = 1.0 + nrm((GLA_HEADS * GLA_DV,), 0.1)
    d['gla2_w_out'] = nrm((GLA_HEADS * GLA_DV, D), (GLA_HEADS * GLA_DV) ** -0.5)
    d['attn3_w_qkv'] = nrm((D, att_cols), D ** -0.5)
    d['attn3_sink'] = nrm((ATT_HEADS,))
    d['attn3_w_o'] = nrm((ATT_HEADS * HEAD_DIM, D), (ATT_HEADS * HEAD_DIM) ** -0.5)
    return d

def reference(x_prompt, x_sample, cache_k_0, cache_v_0, state_mlstm_C_1, state_mlstm_n_1, state_mlstm_m_1,
              state_gla_S_2, cache_k_3, cache_v_3, c, c_ctx, w_mod, b_mod, norm1_g, norm2_g, final_g,
              router_w, router_b, moe_wg, moe_wu, moe_wd, attn0_w_qkv, attn0_sink, attn0_w_o,
              mlstm1_w_in, mlstm1_b_gates, mlstm1_conv, mlstm1_norm_g, mlstm1_w_out,
              gla2_w_in, gla2_w_a1, gla2_w_a2, gla2_b_a, gla2_norm_g, gla2_w_out,
              attn3_w_qkv, attn3_sink, attn3_w_o):
    f32 = jnp.float32
    layer_params = (
        ((attn0_w_qkv, attn0_sink, attn0_w_o), (cache_k_0, cache_v_0)),
        ((mlstm1_w_in, mlstm1_b_gates, mlstm1_conv, mlstm1_norm_g, mlstm1_w_out),
         (state_mlstm_C_1, state_mlstm_n_1, state_mlstm_m_1)),
        ((gla2_w_in, gla2_w_a1, gla2_w_a2, gla2_b_a, gla2_norm_g, gla2_w_out), (state_gla_S_2,)),
        ((attn3_w_qkv, attn3_sink, attn3_w_o), (cache_k_3, cache_v_3)),
    )
    xc, xl = x_prompt, x_sample
    nbc = x_prompt.shape[0]
    new_state = []
    for i in range(DEPTH):
        kind = MIXER_KINDS[i % N_MIXERS]
        params, cache = layer_params[i]
        sc1, ac1, gc1, sc2, ac2, gc2 = adaln(c_ctx[None, :], w_mod[i], b_mod[i])
        sl1, al1, gl1, sl2, al2, gl2 = adaln(c, w_mod[i], b_mod[i])
        hc = rmsnorm(xc, norm1_g[i]) * (1 + ac1) + sc1
        hl = rmsnorm(xl, norm1_g[i]) * (1 + al1) + sl1
        if kind == 'attn':
            yc, st = attn_context(hc, *params)
            yl = attn_latent(hl, cache, *params)
        elif kind == 'mlstm':
            zero = (jnp.zeros((nbc, 2, MLSTM_HEADS, MLSTM_DV, MLSTM_DK), f32),
                    jnp.zeros((nbc, 2, MLSTM_HEADS, MLSTM_DK), f32),
                    jnp.zeros((nbc, 2, MLSTM_HEADS), f32))
            yc, st = mlstm_mixer(hc, zero, *params)
            yl, _ = mlstm_mixer(hl, cache, *params)
        else:
            zero = (jnp.zeros((nbc, 2, GLA_HEADS, GLA_DK, GLA_DV), f32),)
            yc, st = gla_mixer(hc, zero, *params)
            yl, _ = gla_mixer(hl, cache, *params)
        new_state.extend(s.astype(x_prompt.dtype) for s in st)
        xc = xc + gc1 * yc
        xl = xl + gl1 * yl
        hc2 = rmsnorm(xc, norm2_g[i]) * (1 + ac2) + sc2
        hl2 = rmsnorm(xl, norm2_g[i]) * (1 + al2) + sl2
        xc = xc + gc2 * moe(hc2, router_w, router_b, moe_wg[i], moe_wu[i], moe_wd[i])
        xl = xl + gl2 * moe(hl2, router_w, router_b, moe_wg[i], moe_wu[i], moe_wd[i])
    y_prompt = rmsnorm(xc, final_g)
    y_sample = rmsnorm(xl, final_g)
    k0, v0, c1, n1, m1, s2, k3, v3 = new_state
    return (y_prompt, y_sample, k0, v0, c1, n1, m1, s2, k3, v3)


_drawn_inputs = setup_inputs


def setup_inputs(seed=0):
    import zlib

    import numpy as np

    out = dict(_drawn_inputs(seed))
    spreads = {}
    factors = {'state_gla_S_2': 8.0, 'attn0_sink': 8.0, 'attn3_sink': 8.0}
    for name, (base, spread) in spreads.items():
        noise = np.random.default_rng([zlib.crc32(name.encode()), seed]).standard_normal(out[name].shape)
        drawn = base * np.exp(spread * noise) if base else spread * noise
        out[name] = __import__('jax').numpy.asarray(drawn.astype(out[name].dtype))
    for name, factor in factors.items():
        out[name] = (out[name] * factor).astype(out[name].dtype)
    return out
```

```python
from contextlib import ExitStack

import numpy as np
import concourse.bass as bass
from concourse import mybir

F32 = mybir.dt.float32
I32 = mybir.dt.int32
ALU = mybir.AluOpType
ACT = mybir.ActivationFunctionType
AX = mybir.AxisListType

P = 128
D = 1024
T = 128
N2 = 2 * T
KD = D // P
DEPTH = 4
EPS = 1e-6
HEADS, KV, HD = 16, 4, 64
MH, MDK, MDV = 8, 128, 256
GH, GDK, GDV = 4, 128, 256
NE, NG, EPG = 16, 4, 4
FE = 512
SLOTS = 64
RING = 6
GB = 32
NB = T // GB

CONST = {}


def constants():
    cols, at = [], 0

    def add(name, a):
        nonlocal at
        full = np.zeros((P, a.shape[1]), np.float32)
        full[:a.shape[0]] = a
        CONST[name] = (at, at + a.shape[1])
        cols.append(full)
        at += a.shape[1]

    i = np.arange(P)
    add("ident", np.eye(P))
    add("ones", np.ones((P, P)))
    half, nf = HD // 2, HD // 4
    inv = 10000.0 ** (-np.arange(nf, dtype=np.float32) / np.float32(nf))
    f = i % HD
    pos = np.where(f[:, None] < half, (i // 64)[None, :], (i % 64)[None, :]).astype(np.float32)
    ang = pos * inv.astype(np.float32)[f % nf][:, None]
    add("cos", np.cos(ang))
    add("sin", np.sin(ang))
    rot = np.zeros((P, P), np.float32)
    for m in range(P):
        if m % half < nf:
            rot[m + nf, m] = -1.0
        else:
            rot[m - nf, m] = 1.0
    add("rot", rot)
    for j in range(2):
        dup = np.zeros((P, P), np.float32)
        for m in range(P):
            dup[64 * j + m % 64, m] = 1.0
        add(f"dup{j}", dup)
    add("le", (i[:, None] <= i[None, :]))
    add("ge", (i[:, None] >= i[None, :]))
    add("lt", (i[:, None] < i[None, :]))
    add("slot1", np.broadcast_to(1.0 + np.arange(2 * P), (P, 2 * P)))
    win = np.zeros((P, 80))
    win[:, 40] = 1.0
    add("win", win)
    selm = np.zeros((P, 2))
    for j in range(4):
        selm[32 * j, 0] = selm[32 * j + 1, 1] = 1.0
    add("selm", selm)
    add("prio", np.broadcast_to(np.tile(16.0 - np.arange(16), 2), (P, 32)))
    add("gprio", np.broadcast_to(np.tile(4.0 - np.arange(4), 2), (P, 8)))
    add("j1", np.broadcast_to(1.0 + np.arange(8), (P, 8)))
    add("code_e", np.broadcast_to(np.tile(np.arange(16.0), 3), (P, 48)))
    add("code_b", np.broadcast_to(np.repeat(64.0 * np.arange(1, 4), 16), (P, 48)))
    add("eps", np.full((P, 1), EPS))
    return np.concatenate(cols, 1).astype(np.float32)


constants()
NCONST = max(b for _, b in CONST.values())

PR = {"n1": 0, "n2": 32, "fin": 64, "cc": 72, "cl": 80, "mg": 88, "gg": 104, "ba": 112,
      "bm": 128, "conv": 320, "n0": 368}
NPR = 384


def plan_chunks():
    chunks, first = [], {}

    def part(name, items):
        first[name] = len(chunks)
        chunks.extend(items)

    mod = lambda l: [("mod", l, c) for c in range(12)]
    part("mod0", mod(0))
    for l in range(DEPTH):
        if l in (0, 3):
            part(f"mix{l}", [("qkv", l, c) for c in range(3)] + [("wo", l, c) for c in range(2)])
        elif l == 1:
            part("mix1", [("min", l, c) for c in range(12)] + [("c0", l, 0)] + [("mout", l, (c, r)) for c in range(2) for r in range(2)])
        else:
            part("mix2", [("gin", l, c) for c in range(6)] + [("s0", l, 0)] + [("gout", l, c) for c in range(2)])
        if l + 1 < DEPTH:
            part(f"mod{l + 1}", mod(l + 1))
        part(f"moe{l}", [(w, l, e) for e in range(NE) for w in ("wg", "wu", "wd")])
    return chunks, first


CHUNKS, FIRST = plan_chunks()



STEPS = {
    "tensor_step": ["prmT", "a_rot0", "a_dup0", "l_g", "l_at", "l_kt", "l_den", "l_n", "l_nT", "l_rnb",
                    "g_u", "g_at", "g_rnb", "a_rot3", "a_dup3"],
    "vector_step": ["zero_rows", "prm", "a_rope0", "l_abs", "l_rows", "l_ac", "l_rr", "l_rn", "g_am", "g_sm", "g_rn",
                    "a_rope3"],
    "scalar_step": ["l_rowexp", "l_n_sb", "l_nT_sb", "l_root", "g_u_sb", "g_se", "g_root"],
}
STEP = {name: (sem, i + 1) for sem, names in STEPS.items() for i, name in enumerate(names)}
def program(nc, I, O):
    with ExitStack() as ctx:
        def sb(name, shape, dt=F32):
            return ctx.enter_context(nc.sbuf_tensor(name, shape, dt))

        sems = {}

        def S(name):
            name = STEP[name][0] if name in STEP else name
            if name not in sems:
                sems[name] = ctx.enter_context(nc.semaphore(name))
            return sems[name]

        PS = ctx.enter_context(nc.psum_tensor("PS", [P, 8, 512], F32))
        ring = sb("ring", [P, RING, 8, 512])
        CN = sb("consts", [P, NCONST])
        PRM = sb("prm", [P, NPR])
        X = sb("X", [P, KD, N2])
        H = sb("H", [P, KD, N2])
        SQ = sb("SQ", [P, KD, N2])
        RS = sb("RS", [P, 2, N2])
        MC = sb("MC", [P, 2, 96])
        CS = sb("CS", [P, KD, 32])
        RW = sb("RW", [P, KD, NE])
        RB = sb("RB", [P, NE])
        SK = sb("SK", [P, 2, HEADS])
        WGT = sb("WGT", [P, KD, 2, 40])
        BGT = sb("BGT", [40, 2])
        M0 = sb("M0", [40, 2])
        EXI = sb("EXI", [1, 24], I32)
        small = sb("small", [P, 640])
        ARN = 17800
        arena = sb("arena", [P, ARN])

        def shaped(v, shape):
            if len(shape) == 2:
                return v.rearrange("p (a b) -> p a b", a=shape[0])
            if len(shape) == 3:
                return v.rearrange("p (a b c) -> p a b c", a=shape[0], b=shape[1])
            if len(shape) == 4:
                return v.rearrange("p (a b c d) -> p a b c d", a=shape[0], b=shape[1], c=shape[2])
            return v

        def ar(at, *shape):
            n = int(np.prod(shape))
            assert at + n <= ARN, (at, shape)
            return shaped(arena[:, at:at + n], shape)

        def sq(at, *shape):
            return shaped(SQ[:, :, :].rearrange("p a b -> p (a b)")[:, at:at + int(np.prod(shape))], shape)

        def sm(at, *shape):
            return shaped(small[:, at:at + int(np.prod(shape))], shape)

        def c_(name):
            a, b = CONST[name]
            return CN[:, a:b]

        def prm(name, n, off=0):
            return PRM[:, PR[name] + off:PR[name] + off + n]

        def bank(b, lo=0, hi=512):
            return PS[:, b, lo:hi]

        def mod_col(l, v, k, s):
            j = (v * 8 + k) * 2 + s
            return MC[:, l % 2, j:j + 1]

        def last(ap, n):
            return ap.unsqueeze(len(ap.shape)).broadcast_to(list(ap.shape) + [n])

        def mid(ap, n):
            return ap.unsqueeze(1).broadcast_to([ap.shape[0], n, ap.shape[1]])

        ident, ones = c_("ident"), c_("ones")

        XR = ar(0, 2, 1024)
        PT = ar(4096, 3, P)
        HT = ar(0, 2, 1024)
        GX = ar(2048, 512)
        XG = ar(2560, 4, 2, SLOTS)
        SG = ar(3072, 256)
        HID = ar(3328, 256)
        HTS = ar(3584, 2, 2, SLOTS)
        WTS = ar(3840, 2, N2)
        YS = ar(4352, 512)
        PB = ar(4864, 2, SLOTS)
        WB = ar(4992, 2, 2, SLOTS)
        RT = ar(5248, 2048)
        MP = sq(0, 2, 512)

        QT = ar(0, 8, N2)
        KR = ar(2048, 2, N2)
        KDUP = ar(2560, KV, 3, T)
        KC = ar(4096, 512)
        VL = ar(4608, 256)
        CV = ar(4864, 256)
        CK = ar(5120, KV, 2, HD)
        RTMP = ar(5632, 10, T)
        PBUF = ar(6912, 4, 3 * T)
        PTB = ar(8448, 3, 4, T)
        OT = ar(9984, 8, N2)
        AMX, AM2, ANM, ASD, ASUM, AES, AR_ = (sm(0, 4, 3), sm(16, 4, 2), sm(32, 4, 2), sm(40, 4, 2), sm(48, 4, 2),
                                              sm(56, 4, 2), sm(64, 4, 2))

        mQK = ar(0, 16, N2)
        mKW = ar(2048, MH, 2, T)
        mV = ar(4096, 2, 2048)
        mO = ar(8192, 16, N2)
        mW = ar(12288, 2, 2, MH, T)
        mRM = ar(16384, 3, N2)
        mN0 = ar(17152, 16, 40)
        mRAW = sq(0, 4, N2)
        mROW = sq(1024, 4, N2)
        mSC, mEM = sm(0, N2), sm(256, N2)
        mAC = sm(512, 2, 40)
        mQS = H[:, :, :].rearrange("p a b -> p (a b)").rearrange("p (d h t) -> p d h t", d=2, h=MH)
        mTMP = sq(0, 4, T)
        mCO = sq(0, 2, 2, 2, T)
        mHQ = sq(0, 2, 2, N2)
        mWL = sm(592, 16)
        mNS = sm(608, 16)

        gQ, gK = ar(0, 8, T), ar(1024, 8, T)
        gV = ar(2048, 2, 1024)
        gR = ar(4096, 8, N2)
        gLA = ar(6144, 2, 8, T)
        gB = ar(8192, 2, 8, T)
        gAX = ar(10240, 2, 8, T)
        gKI = ar(10240, 2, 8, T)
        gT0, gT1 = ar(12288, 8, T), ar(6144, 8, T)
        gQE = ar(7168, 2, GH, T)
        gQI = ar(13312, 2, 8, T)
        gAT = ar(15360, 8, T)
        gOG = ar(10240, 8, N2)
        gSO = ar(13312, 8, 256)
        gKD = ar(8192, 8, T)
        WA1 = ar(16384, KD, 64)
        WA2 = ar(16896, 512)[0:64]
        gU = sq(1024, N2)[0:64]
        gHQ = sq(0, 2, 2, N2)

        def serial(eng):
            count = {}

            def run(ins, sem):
                sem = STEP[sem][0] if sem in STEP else sem
                ins.then_inc(S(sem), 1)
                count[sem] = count.get(sem, 0) + 1
                eng.wait_ge(S(sem), count[sem])
            return run

        def wait(eng, sem, v):
            if not isinstance(v, int) or v > 0:
                eng.wait_ge(S(sem), v)

        def after(eng, name):
            eng.wait_ge(S(name), STEP[name][1])

        def landed(pe, n, i=0):
            pe.wait_ge(S(f"landed{n % RING}"), 16 * (n // RING + 1) + 16 * i)
            return slot_view(CHUNKS[n][0], n % RING)

        def slot_view(kind, slot):
            v = ring[:, slot].rearrange("p a b -> p (a b)")
            if kind in ("wd", ):
                return v.rearrange("p (k n) -> p k n", k=4)
            if kind == "c0":
                return v.rearrange("p (k n) -> p k n", k=32)
            if kind == "s0":
                return v[:, 0:2048].rearrange("p (k n) -> p k n", k=8)
            return ring[:, slot]

        def used(n):
            kind, l, c = CHUNKS[n]
            a = l // 3
            return {"mod": lambda: ("mod_rows", 12 * l + c + 1),
                    "qkv": lambda: ("a_kv", 2 * a + 2) if c == 2 else ("a_q", 8 * a + 4 * c + 4),
                    "wo": lambda: ("a_y", 8 * a + 4 * c + 4),
                    "min": lambda: [("l_qk", 4 * c + 4), ("l_v", 2 * c - 6), ("l_o", 4 * c - 28)][c // 4],
                    "c0": lambda: ("l_h", MH),
                    "mout": lambda: ("l_y", 4 * c[0] + 4) if c[1] else ("l_y0", c[0] + 1),
                    "gin": lambda: ("g_qk", 4 * c + 4) if c < 2 else ("g_v", 2 * c - 2) if c < 4 else ("g_r", 4 * c - 12),
                    "s0": lambda: ("g_o", GH),
                    "gout": lambda: ("g_y", 4 * c + 4),
                    "wg": lambda: ("up", 2 * (NE * l + c) + 1),
                    "wu": lambda: ("up", 2 * (NE * l + c) + 2),
                    "wd": lambda: ("down", NE * l + c + 1)}[kind]()

        def src_of(kind, l, c):
            def cols(w, j, r=0):
                return w.rearrange("(k p) n -> p k n", p=P)[:, 8 * r:8 * r + 8, 512 * j:512 * j + 512]
            if kind == "mod":
                return cols(I["w_mod"][l], c)
            if kind == "qkv":
                return cols(I[f"attn{l}_w_qkv"], c)
            if kind == "wo":
                return cols(I[f"attn{l}_w_o"], c)
            if kind == "min":
                return cols(I["mlstm1_w_in"], c)
            if kind == "mout":
                return cols(I["mlstm1_w_out"], c[0], c[1])
            if kind == "gin":
                return cols(I["gla2_w_in"], c)
            if kind == "gout":
                return cols(I["gla2_w_out"], c)
            if kind == "c0":
                return I["state_mlstm_C_1"][0].rearrange("d h (j p) k -> p (d h j) k", p=P)
            if kind == "s0":
                return I["state_gla_S_2"][0].rearrange("d h k v -> k (d h) v")
            return expert_weights(kind, l, c)

        def expert_weights(kind, l, e):
            return I["moe_" + kind][l, bass.ds(e, 1)].rearrange("o (k p) n -> p (o k) n", p=P)

        def gla_block(i):
            d, j = i // NB, i % NB
            blk = j if d == 0 else NB - 1 - j
            return (0, blk, 0, GB * (blk + 1)) if d == 0 else (1, blk, GB * blk, T)

        block = ctx.enter_context(nc.Block())

        @block.sync
        def _(sp):
            def load(n):
                kind, l, c = CHUNKS[n]
                if n >= RING:
                    wait(sp, *used(n - RING))
                sp.dma_start(slot_view(kind, n % RING), src_of(kind, l, c)).then_inc(S(f"landed{n % RING}"), 16)

            n = 0
            for l in range(DEPTH):
                while n < FIRST[f"moe{l}"]:
                    load(n)
                    n += 1
                for j in range(6):
                    load(n + j)
                with sp.Fori(1, NE // 2) as i:
                    for j in range(6):
                        kind = CHUNKS[n + j][0]
                        sem, v = used(n + j)
                        step = 4 if sem == "up" else 2
                        sp.wait_ge(S(sem), v - step + step * i)
                        sp.dma_start(slot_view(kind, (n + j) % RING), expert_weights(kind, l, 2 * i + j // 3))\
                          .then_inc(S(f"landed{(n + j) % RING}"), 16)
                n += 3 * NE
                sp.wait_ge(S("table"), l + 1)
                nx = sp.value_load(EXI[0:1, 16:17], min_val=0, max_val=8)
                before = sp.value_load(EXI[0:1, 17:18], min_val=0, max_val=64)
                with sp.If(nx > 0):
                    for j in range(3):
                        wait(sp, *used(n - 3 + j))
                    with sp.Fori(0, nx) as i:
                        e = sp.value_load(EXI[0:1, bass.ds(i, 1)], min_val=0, max_val=NE - 1)
                        sp.wait_ge(S("x_down"), before + i)
                        for j, w in enumerate(("wg", "wu", "wd")):
                            sp.dma_start(slot_view(w, (n - 3 + j) % RING), expert_weights(w, l, e)).then_inc(S(f"x_landed{j}"), 16)
                sp.wait_ge(S("x_down"), before + nx)
            sp.wait_ge(S("y_sb"), 2)
            sp.dma_start(O["y_prompt"][0], XR[:, 0]).then_inc(S("out"), 16)
            sp.dma_start(O["y_sample"][0], XR[:, 1]).then_inc(S("out"), 16)
            sp.wait_ge(S("out"), 16 * (4 + 3 + 2 + 2))
            for j in range(2):
                sp.wait_ge(S(f"out_C{j}"), 16 * MH)

        @block.gpsimd
        def _(pool):
            for t in (WGT[:], CS[:], BGT[:], M0[:], mN0):
                pool.memset(t, 0.0).then_inc(S("pad"), 1)
            pool.wait_ge(S("pad"), 5)
            gates = I["mlstm1_w_in"].rearrange("(k p) n -> p k n", p=P)[:, :, 6144:6176]
            for d in range(2):
                for g in range(2):
                    at = 16 * d + 8 * g
                    pool.dma_start(WGT[:, :, g, 32 * d:32 * d + 8], gates[:, :, at:at + 8]).then_inc(S("load_g"), 16)
                    pool.dma_start(BGT[32 * d:32 * d + 8, g:g + 1],
                                   I["mlstm1_b_gates"][at:at + 8].rearrange("(h o) -> h o", o=1)).then_inc(S("load_g"), 16)
                pool.dma_start(M0[32 * d:32 * d + 8, 1:2], I["state_mlstm_m_1"][0, d].rearrange("(h o) -> h o", o=1)).then_inc(S("load_g"), 16)
            pool.dma_start(RW[:], I["router_w"].rearrange("(k p) n -> p k n", p=P)).then_inc(S("load_rw"), 16)
            after(pool, "prm")
            for d in range(2):
                for h in range(MH):
                    r = 8 * d + h
                    pool.tensor_copy(mN0[:, r, 32 * d + h:32 * d + h + 1], prm("n0", 1, r)).then_inc(S("n0"), 1)
            pool.wait_ge(S("x"), KD * 4)
            pool.wait_ge(S("out"), 80)
            pool.memset(WA1, 0.0).then_inc(S("pad"), 1)
            pool.wait_ge(S("pad"), 6)
            for d in range(2):
                pool.dma_start(WA1[:, :, 32 * d:32 * d + 16], I["gla2_w_a1"][d].rearrange("(k p) n -> p k n", p=P)).then_inc(S("load_a"), 16)
                pool.dma_start(WA2[32 * d:32 * d + 16, :], I["gla2_w_a2"][d]).then_inc(S("load_a"), 16)

        @block.scalar
        def _(act):
            run = serial(act)
            A = nc.scalar.activation

            def load(dst, src, sem):
                act.dma_start(dst, src).then_inc(S(sem), 16)

            load(CN[:, :], I["consts"], "load_c")
            load(XR[:, 0], I["x_prompt"][0], "load_x")
            load(XR[:, 1], I["x_sample"][0], "load_x")
            after(act, "zero_rows")
            for name, src, n in (("cc", I["c_ctx"], 8), ("cl", I["c"][0], 8), ("fin", I["final_g"], 8),
                                 ("mg", I["mlstm1_norm_g"], 16), ("gg", I["gla2_norm_g"], 8)):
                load(PT[PR[name]:PR[name] + n, 0], src.rearrange("(k p) -> k p", p=P), "load_p")
            load(PT[0:32, 0], I["norm1_g"].rearrange("l (k p) -> (l k) p", p=P), "load_p")
            load(PT[32:64, 0], I["norm2_g"].rearrange("l (k p) -> (l k) p", p=P), "load_p")
            load(PT[112:120, 0], I["gla2_b_a"].rearrange("d (k p) -> (d k) p", p=P), "load_p")
            bm = I["b_mod"].rearrange("l (k p) -> (l k) p", p=P)
            load(PT[:, 1], bm[0:128], "load_p")
            load(PT[0:64, 2], bm[128:192], "load_p")
            load(PT[64:112, 2], I["mlstm1_conv"].rearrange("l (k p) -> (l k) p", p=P), "load_p")
            load(PT[112:128, 2], I["state_mlstm_n_1"][0].rearrange("d h k -> (d h) k"), "load_p")
            load(RB[:, :], I["router_b"].partition_broadcast(P), "load_b")
            for a, l in enumerate((0, 3)):
                load(SK[:, a], I[f"attn{l}_sink"].partition_broadcast(P), "load_b")
            after(act, "prm")
            act.wait_ge(S("pad"), 5)
            run(A(CS[:, :, 0], prm("cc", 8), ACT.Silu), "cs")
            run(A(CS[:, :, 1], prm("cl", 8), ACT.Silu), "cs")

            def mod(l):
                for c in range(12):
                    act.wait_ge(S("mod_rows"), 12 * l + c + 1)
                    wait(act, "mod_cols", 12 * l + c - 1)
                    run(A(MP[:, c % 2], bank(c % 2), ACT.Copy), "mod_sb")

            def norm(n):
                mods = 1 + n // 2
                act.wait_ge(S("mod_cols"), 12 * min(mods, DEPTH))
                for k in range(KD):
                    act.wait_ge(S("x"), KD * (n + 1) - KD + k + 1)
                    run(A(SQ[:, k], X[:, k], ACT.Square), "sq")
                act.wait_ge(S("sumsq"), n + 1)
                run(A(RS[:, 0], bank(7, 0, N2), ACT.Sqrt, bias=c_("eps"), scale=1.0 / D), "root")

            def affine(n, l, v):
                act.wait_ge(S("mod"), 3 * (l + 1))
                for k in range(KD):
                    act.wait_ge(S("xn"), KD * n + k + 1)
                    run(A(H[:, k, 0:T], H[:, k, 0:T], ACT.Identity, bias=mod_col(l, v, k, 0), scale=mod_col(l, v + 1, k, 0)), "h0")

            def attention(a, l):
                load(CK[:, :, 0], I[f"cache_k_{l}"][0], "load_ck")
                load(CK[:, :, 1], I[f"cache_k_{l}"][0], "load_ck")
                load(CV, I[f"cache_v_{l}"][0].rearrange("t h d -> t (h d)"), "load_ck")
                for m in range(8):
                    act.wait_ge(S("a_q"), 8 * a + m + 1)
                    run(A(QT[:, m], bank(m % 4, 0, N2), ACT.Copy), "a_q_sb")
                for m in range(2):
                    act.wait_ge(S("a_k"), 2 * a + m + 1)
                    run(A(KR[:, m], bank(m % 4, 0, N2), ACT.Copy), "a_k_sb")
                act.wait_ge(S("a_kv"), 2 * a + 1)
                run(A(KC, bank(2), ACT.Copy), "a_kv_sb")
                act.wait_ge(S("a_kv"), 2 * a + 2)
                run(A(VL, bank(3, 0, 256), ACT.Copy), "a_kv_sb")
                load(O[f"cache_k_{l}"][0].rearrange("t h d -> t (h d)"), KC[:, 0:256], "out")
                load(O[f"cache_v_{l}"][0].rearrange("t h d -> t (h d)"), KC[:, 256:512], "out")
                after(act, f"a_dup{l}")
                kd = PS[:, 4:6].rearrange("p b (j n) -> p (b j) n", j=2)
                run(A(KDUP[:, :, 0], kd[:, :, 0:T], ACT.Copy), "a_kd")
                run(A(KDUP[:, :, 2], kd[:, :, T:N2], ACT.Copy), "a_kd")
                run(A(KDUP[:, :, 1], bank(6).rearrange("p (j n) -> p j n", j=4), ACT.Copy), "a_kd")
                for g in range(KV):
                    n = 4 * a + g
                    act.wait_ge(S("a_neg"), n + 1)
                    wait(act, "a_pt", n)
                    for j in range(4):
                        run(A(PBUF[:, j, 0:T], bank(j, 0, T), ACT.Exp, bias=ANM[:, j, 0:1], scale=HD ** -0.5,
                              accum_out=ASUM[:, j, 0:1]), "a_exp")
                        run(A(PBUF[:, j, T:3 * T], bank(j, T, 3 * T), ACT.Exp, bias=ANM[:, j, 1:2], scale=HD ** -0.5,
                              accum_out=ASUM[:, j, 1:2]), "a_exp")
                    run(A(AES, ASD, ACT.Exp), "a_exp")
                    act.wait_ge(S("a_pt"), n + 1)
                    run(A(PTB[:, 2], bank(6).rearrange("p (j n) -> p j n", j=4), ACT.Copy), "a_ptA")
                    act.wait_ge(S("a_pv"), n + 1)
                    run(A(OT[:, 2 * g:2 * g + 2].rearrange("p m (s t) -> p s m t", s=2),
                          bank(7).rearrange("p (s m t) -> p s m t", s=2, m=2), ACT.Copy), "a_o")

            def mlstm():
                E = mROW[0:40, 2]
                after(act, "l_abs")
                run(A(E, E, ACT.Exp, scale=-1.0), "l_ln")
                run(A(E, E, ACT.Ln, bias=1.0), "l_ln")

                def silu(m):
                    act.wait_ge(S("l_conv"), m + 1)
                    run(A(mQK[:, m], mQK[:, m], ACT.Silu), "l_qk_sb")

                for m in range(16):
                    act.wait_ge(S("l_qk"), m + 1)
                    wait(act, "l_conv", m - 3)
                    run(A(mRAW[:, m % 4], bank(m % 4, 0, N2), ACT.Copy), "l_raw")
                    if m >= 2:
                        silu(m - 2)
                for i in range(8):
                    act.wait_ge(S("l_v"), i + 1)
                    run(A(mV[:, i % 2, 512 * (i // 2):512 * (i // 2) + 512], bank(4 + i % 3), ACT.Copy), "l_v_sb")
                    if i < 2:
                        silu(14 + i)
                for m in range(16):
                    act.wait_ge(S("l_o"), m + 1)
                    run(A(mO[:, m], bank(m % 4, 0, N2), ACT.Sigmoid), "l_o_sb")
                run(A(mSC[0:40], mRM[0:40, 2], ACT.Exp, scale=-1.0), "scalar")
                run(A(mEM[0:40], mRM[0:40, 1], ACT.Exp, scale=-1.0), "l_rowexp")
                for q in range(4):
                    d, hg = q // 2, q % 2
                    act.wait_ge(S("l_w"), 8 * (q + 1))
                    for s in range(2):
                        w = mW[:, s, d, 4 * hg:4 * hg + 4]
                        run(A(w, w, ACT.Exp, scale=-1.0), "l_we")
                n0 = FIRST["mix1"] + 12
                c0 = slot_view("c0", n0 % RING)
                for u in range(8):
                    act.wait_ge(S("l_c0t"), u + 1)
                    run(A(c0[:, 4 * u:4 * u + 4], bank(4 + 3 * (u % 2)).rearrange("p (a b) -> p a b", a=4), ACT.Copy), "l_c0")
                for h in range(MH):
                    act.wait_ge(S("l_c"), h + 1)
                    wait(act, f"out_C{h % 2}", 32 * (h // 2))
                    run(A(mCO[:, h % 2], bank(5 + h % 2).rearrange("p (j d k) -> p j d k", j=2, d=2), ACT.Copy), "l_c_sb")
                    for d in range(2):
                        load(O["C"][0, d, h].rearrange("(j p) k -> p j k", p=P), mCO[:, h % 2, :, d], f"out_C{h % 2}")
                after(act, "l_n")
                run(A(mNS, bank(4, 0, 16), ACT.Copy), "l_n_sb")
                after(act, "l_nT")
                run(A(mROW[0:16, 2, 0:P], PS[0:16, 4, 128:256], ACT.Copy), "l_nT_sb")
                load(O["n"][0].rearrange("d h k -> (d h) k"), mROW[0:16, 2, 0:P], "out")
                for d in range(2):
                    t = T - 1 if d == 0 else 0
                    load(O["m"][0, d].rearrange("(h o) -> h o", o=1), mRM[32 * d:32 * d + 8, 1, t:t + 1], "out")
                for j in range(2):
                    act.wait_ge(S(f"out_C{j}"), 16 * MH)
                for h in range(MH):
                    act.wait_ge(S("l_h"), h + 1)
                    v = bank(h % 4).rearrange("p (j n) -> p j n", j=2)
                    run(A(mQK[:, 2 * h:2 * h + 2], v, ACT.Copy), "scalar")
                    wait(act, "l_ss", h - 1)
                    run(A(mHQ[:, h % 2], v, ACT.Square), "l_hq")
                act.wait_ge(S("l_ss"), MH)
                run(A(mROW[0:8, 0], PS[0:8, 4, 0:N2], ACT.Sqrt, bias=c_("eps")[0:8], scale=1.0 / MDV), "l_root")

            def gla():
                after(act, "g_u")
                run(A(gU, PS[0:64, 4, 0:N2], ACT.Copy), "g_u_sb")

                def qk(m):
                    act.wait_ge(S("g_qk"), m + 1)
                    dst = (gQ if m < 4 else gK)[:, 2 * (m % 4):2 * (m % 4) + 2]
                    run(A(dst, bank(m % 4, 0, N2).rearrange("p (s t) -> p s t", s=2), ACT.Copy,
                          scale=GDK ** -0.5 if m < 4 else 1.0), "g_qk_sb")
                for m in range(8):
                    qk(m)
                for d in range(2):
                    act.wait_ge(S("g_abs"), d + 1)
                    run(A(gAX[:, d], gAX[:, d], ACT.Exp, scale=-1.0), "g_ln")
                    run(A(gAX[:, d], gAX[:, d], ACT.Ln, bias=1.0), "g_ln")
                for i in range(4):
                    act.wait_ge(S("g_v"), i + 1)
                    run(A(gV[:, i % 2, 512 * (i // 2):512 * (i // 2) + 512], bank(i), ACT.Copy), "g_v_sb")
                for m in range(8):
                    act.wait_ge(S("g_r"), m + 1)
                    run(A(gR[:, m], bank(m % 4, 0, N2), ACT.Silu), "g_r_sb")
                for d in range(2):
                    act.wait_ge(S("g_qd"), d + 1)
                    run(A(gQI[:, d], gQI[:, d], ACT.Exp, scale=1.0 / 16), "g_qe")
                for i in range(2 * NB):
                    d, blk, lo, hi = gla_block(i)
                    act.wait_ge(S("g_kd"), i + 1)
                    t = (gT0, gT1)[i % 2][:, :, lo:hi]
                    run(A(t, t, ACT.Exp, scale=1.0 / 16), "g_ke")
                for d in range(2):
                    run(A(gQE[:, d], gB[:, d].rearrange("p (h s) t -> p h s t", s=2)[:, :, 1], ACT.Exp, scale=1.0 / 16), "g_qx")
                act.wait_ge(S("g_sd"), 2)
                run(A(gT0, gT0, ACT.Exp, scale=1.0 / 16), "g_se")
                for h in range(GH):
                    act.wait_ge(S("g_o"), h + 1)
                    v = bank(h).rearrange("p (j n) -> p j n", j=2)
                    run(A(gOG[:, 2 * h:2 * h + 2], v, ACT.Copy), "scalar")
                    wait(act, "g_ss", h - 1)
                    run(A(gHQ[:, h % 2], v, ACT.Square), "g_hq")
                act.wait_ge(S("g_ss"), GH)
                run(A(mROW[0:8, 1], PS[0:8, 6, 0:N2], ACT.Sqrt, bias=c_("eps")[0:8], scale=1.0 / GDV), "g_root")
                for i in range(4):
                    act.wait_ge(S("g_s"), i + 1)
                    run(A(gSO[:, 2 * i:2 * i + 2], bank(i).rearrange("p (a b) -> p a b", a=2), ACT.Copy), "g_s_sb")
                for d in range(2):
                    load(O["S"][0, d].rearrange("h k v -> k h v"), gSO[:, 4 * d:4 * d + 4], "out")

            def moe(l):
                for b in range(4):
                    act.wait_ge(S("ht"), 4 * l + b + 1)
                    run(A(HT[:, b // 2, 512 * (b % 2):512 * (b % 2) + 512], bank(b), ACT.Copy), "ht_sb")
                act.wait_ge(S("logitT"), l + 1)
                run(A(RT[0:NE, 0:N2], PS[0:NE, 5, 0:N2], ACT.Copy), "logitT_sb")
                act.wait_ge(S("logit"), l + 1)
                run(A(RT[:, 256:288], bank(4, 0, 32), ACT.Sigmoid), "score")

                def evac(dst, src, func, sem, value):
                    A(dst, src, func).then_inc(S(sem), 1)
                    act.wait_ge(S(sem), value)

                def gathered(E):
                    act.wait_ge(S("gather"), E + 1)
                    evac(GX, bank(6), ACT.Copy, "gx", E + 1)

                def expert(E, more=True):
                    act.wait_ge(S("up"), 2 * E + 1)
                    evac(SG, bank(4, 0, 256), ACT.Silu, "silu", E + 1)
                    if more:
                        gathered(E + 1)
                    act.wait_ge(S("down"), E + 1)
                    evac(YS, bank(7), ACT.Copy, "ys", E + 1)

                E0 = NE * l
                gathered(E0)
                expert(E0)
                expert(E0 + 1)
                with act.Fori(1, NE // 2 - 1) as i:
                    expert(2 * i + E0)
                    expert(2 * i + (E0 + 1))
                expert(E0 + 14)
                expert(E0 + 15, False)
                act.wait_ge(S("table"), l + 1)
                nx = act.value_load(EXI[0:1, 16:17], min_val=0, max_val=8)
                before = act.value_load(EXI[0:1, 17:18], min_val=0, max_val=64)
                with act.If(nx > 0):
                    with act.Fori(0, nx) as i:
                        act.wait_ge(S("x_gather"), before + i)
                        evac(GX, bank(6), ACT.Copy, "x_gx", before + i)
                        act.wait_ge(S("x_up"), before + i)
                        evac(SG, bank(4, 0, 256), ACT.Silu, "x_silu", before + i)
                        act.wait_ge(S("x_down"), before + i + 1)
                        evac(YS, bank(7), ACT.Copy, "x_ys", before + i)

            mod(0)
            for l in range(DEPTH):
                norm(2 * l)
                affine(2 * l, l, 0)
                (lambda: attention(l // 3, l), mlstm, gla)[l % 3]()
                act.wait_ge(S("out"), (32, 80, 112, 144)[l])
                norm(2 * l + 1)
                affine(2 * l + 1, l, 3)
                if l + 1 < DEPTH:
                    mod(l + 1)
                moe(l)
            norm(2 * DEPTH)
            for k in range(KD):
                act.wait_ge(S("xn"), KD * 2 * DEPTH + k + 1)
                run(A(H[:, k], H[:, k], ACT.Copy, scale=prm("fin", 1, k)), "h0")
            for b in range(4):
                act.wait_ge(S("yT"), b + 1)
                run(A(XR[:, b // 2, 512 * (b % 2):512 * (b % 2) + 512], bank(b), ACT.Copy), "scalar")
                if b % 2:
                    run(act.nop(), "y_sb")

        @block.tensor
        def _(pe):
            mm, tp = pe.matmul, pe.transpose

            def group(out, pairs, sem=None, first=True, final=True):
                pairs = list(pairs)
                for i, (a, b) in enumerate(pairs):
                    ins = mm(out, a, b, start=first and i == 0, stop=final and i == len(pairs) - 1)
                if sem:
                    ins.then_inc(S(sem), 1)
                return ins

            def tile(w, m):
                return [w[:, k, P * m:P * m + P] for k in range(KD)]

            pe.wait_ge(S("load_c"), 16)
            pe.wait_ge(S("load_x"), 32)
            for b in range(4):
                for k in (2 * b, 2 * b + 1):
                    for s in range(2):
                        ins = tp(bank(b, N2 * (k % 2) + T * s, N2 * (k % 2) + T * s + T), XR[:, s, P * k:P * k + P], ident)
                ins.then_inc(S("xT"), 1)
            pe.nop().then_inc(S("x_down"), 1)
            pe.nop().then_inc(S("x_scatter"), 1)
            pe.wait_ge(S("load_p"), 16 * 12)
            for j in range(3):
                ins = tp(bank(4, P * j, P * j + P), PT[:, j], ident)
            ins.then_inc(S("prmT"), 1)
            pe.wait_ge(S("cs"), 2)

            def mod(l):
                def cols(c):
                    pe.wait_ge(S("mod_sb"), 12 * l + c + 1)
                    for j in range(4 * c, 4 * c + 4):
                        ins = mm(bank(6, 2 * j, 2 * j + 2), MP[:, c % 2, P * (j % 4):P * (j % 4) + P], c_("selm"), start=True, stop=True)
                    ins.then_inc(S("mod_cols"), 1)

                if l == 0:
                    pe.wait_ge(S("x"), 8)
                n0 = FIRST[f"mod{l}"]
                for c in range(12):
                    w = landed(pe, n0 + c)
                    if c >= 2:
                        pe.wait_ge(S("mod_sb"), 12 * l + c - 1)
                    for k in range(KD):
                        g = 32 * (k % 4)
                        ins = mm(PS[g:g + 32, c % 2, :], CS[:, k], w[:, k], start=(k < 4), stop=(k >= 4))
                    ins.then_inc(S("mod_rows"), 1)
                    if c:
                        cols(c - 1)
                cols(11)

            def sumsq(n):
                for k in range(KD):
                    pe.wait_ge(S("sq"), KD * n + k + 1)
                    ins = mm(bank(7, 0, N2), ones, SQ[:, k], start=(k == 0), stop=(k == KD - 1))
                ins.then_inc(S("sumsq"), 1)

            def h_ready(n, k=KD - 1):
                pe.wait_ge(S("h0"), KD * n + k + 1)
                pe.wait_ge(S("h1"), KD * n + k + 1)

            def attention(a, l):
                n0 = FIRST[f"mix{l}"]
                for c in range(2):
                    w = landed(pe, n0 + c)
                    for m in range(4 * c, 4 * c + 4):
                        if m >= 4:
                            pe.wait_ge(S("a_q_sb"), 8 * a + m - 3)
                        for k in range(KD):
                            if m == 0:
                                h_ready(2 * l, k)
                            ins = mm(bank(m % 4, 0, N2), w[:, k, P * (m % 4):P * (m % 4) + P], H[:, k], start=(k == 0), stop=(k == KD - 1))
                        ins.then_inc(S("a_q"), 1)
                w = landed(pe, n0 + 2)
                for m in range(2):
                    pe.wait_ge(S("a_q_sb"), 8 * a + 5 + m)
                    group(bank(m, 0, N2), zip(tile(w, m), [H[:, k] for k in range(KD)]), "a_k")
                pe.wait_ge(S("a_q_sb"), 8 * a + 7)
                group(bank(2), [(H[:, k, 0:T], w[:, k]) for k in range(KD)], "a_kv")
                pe.wait_ge(S("a_q_sb"), 8 * a + 8)
                group(bank(3, 0, 256), [(H[:, k, T:N2], w[:, k, 256:512]) for k in range(KD)], "a_kv")
                pe.wait_ge(S("a_k_sb"), 2 * a + 2)
                for m in range(10):
                    src = QT[:, m, T:N2] if m < 8 else KR[:, m - 8, T:N2]
                    ins = mm(bank(4 + m // 4, T * (m % 4), T * (m % 4) + T), c_("rot"), src, start=True, stop=True)
                ins.then_inc(S(f"a_rot{l}"), 1)
                after(pe, f"a_rope{l}")
                pe.wait_ge(S("load_ck"), 48 * (a + 1))
                for j in range(KV):
                    mm(bank(4 + j // 2, N2 * (j % 2), N2 * (j % 2) + N2), c_(f"dup{j % 2}"), KR[:, j // 2], start=True, stop=True)
                for j in range(KV):
                    ins = tp(bank(6, T * j, T * j + T), CK[:, j].rearrange("p a b -> p (a b)"), ident)
                ins.then_inc(S(f"a_dup{l}"), 1)

                def scores(g):
                    if g == 0:
                        pe.wait_ge(S("a_kd"), 3 * (a + 1))
                        pe.wait_ge(S("a_kv_sb"), 2 * (a + 1))
                    else:
                        pe.wait_ge(S("a_exp"), 9 * (4 * a + g))
                    for j in range(4):
                        h = 4 * g + j
                        p0 = HD * (h % 2)
                        mm(bank(j, 0, T), QT[p0:p0 + HD, h // 2, 0:T], KDUP[p0:p0 + HD, g, 0], start=True, stop=True)
                        ins = mm(bank(j, T, 3 * T), QT[p0:p0 + HD, h // 2, T:N2], KDUP[p0:p0 + HD, g, 1:3].rearrange("p a b -> p (a b)"), start=True, stop=True)
                    ins.then_inc(S("a_s"), 1)

                scores(0)
                for g in range(KV):
                    n = 4 * a + g
                    if g + 1 < KV:
                        scores(g + 1)
                    pe.wait_ge(S("a_p"), n + 1)
                    wait(pe, "a_ptV", 2 * n)
                    wait(pe, "a_ptA", n)
                    for part in range(3):
                        for j in range(4):
                            ins = tp(bank(4 + part, T * j, T * j + T), PBUF[:, j, T * part:T * part + T], ident)
                    ins.then_inc(S("a_pt"), 1)
                    pe.wait_ge(S("a_ptV"), 2 * (n + 1))
                    pe.wait_ge(S("a_ptA"), n + 1)
                    wait(pe, "a_o", n)
                    cols = slice(HD * g, HD * g + HD)
                    for half in range(2):
                        p0 = HD * half
                        def probs(part):
                            return PTB[:, part].rearrange("p (m two) t -> p two m t", two=2)[:, half]
                        out = PS[p0:p0 + HD, 7].rearrange("p (s m t) -> p s m t", s=2, m=2)
                        mm(out[:, 0], KC[:, 256 + HD * g:256 + HD * g + HD], probs(0), start=True, stop=True)
                        mm(out[:, 1], CV[:, cols], probs(1), start=True, stop=False)
                        ins = mm(out[:, 1], VL[:, cols], probs(2), start=False, stop=True)
                    ins.then_inc(S("a_pv"), 1)
                pe.wait_ge(S("a_o"), 4 * (a + 1))
                out_proj("a_y", 8 * a, n0 + 3, OT, 2 * l)

            def out_proj(sem, base, n0, src, r):
                for c in range(2):
                    w = landed(pe, n0 + c)
                    for m in range(4 * c, 4 * c + 4):
                        if m >= 4:
                            pe.wait_ge(S("x"), KD * (r + 1) + m - 3)
                        group(bank(m % 4, 0, N2), zip(tile(w, m % 4), [src[:, k] for k in range(KD)]), sem)

            def mlstm():
                n0 = FIRST["mix1"]
                h_ready(2)
                pe.wait_ge(S("load_g"), 16 * 10)
                for g in range(2):
                    ins = group(PS[0:40, 7, N2 * g:N2 * g + N2], [(WGT[:, k, g], H[:, k]) for k in range(KD)])
                ins.then_inc(S("l_g"), 1)
                for c in range(4):
                    w = landed(pe, n0 + c)
                    for m in range(4 * c, 4 * c + 4):
                        wait(pe, "l_raw", m - 3)
                        group(bank(m % 4, 0, N2), zip(tile(w, m % 4), [H[:, k] for k in range(KD)]), "l_qk")
                for c in range(4):
                    w = landed(pe, n0 + 4 + c)
                    for s in range(2):
                        i = 2 * c + s
                        wait(pe, "l_v_sb", i - 2)
                        group(bank(4 + i % 3), [(H[:, k, T * s:T * s + T], w[:, k]) for k in range(KD)], "l_v")
                after(pe, "l_rows")
                for s in range(2):
                    ins = tp(bank(7, 40 * s, 40 * s + 40), mROW[0:40, 0, T * s:T * s + T], ident[0:40, 0:40])
                ins.then_inc(S("l_at"), 1)
                pe.wait_ge(S("l_raw"), 16)
                for c in range(4):
                    w = landed(pe, n0 + 8 + c)
                    for m in range(4 * c, 4 * c + 4):
                        wait(pe, "l_o_sb", m - 3)
                        group(bank(m % 4, 0, N2), zip(tile(w, m % 4), [H[:, k] for k in range(KD)]), "l_o")

                def spread(out, r, rows, parts=40):
                    return mm(out, ident[0:parts, r:r + 1].broadcast_to([parts, P]), rows, start=True, stop=True)

                pe.wait_ge(S("l_v_sb"), 8)
                after(pe, "l_ac")
                for q in range(4):
                    d, hg = q // 2, q % 2
                    wait(pe, "l_w", 8 * (q - 1))
                    for j in range(4):
                        b = 4 + 2 * (q % 2) + j // 2
                        ins = spread(bank(b, N2 * (j % 2), N2 * (j % 2) + N2), 32 * d + 4 * hg + j, mRM[0:40, 0])
                    ins.then_inc(S("l_mb"), 1)
                pe.wait_ge(S("l_o_sb"), 16)
                pe.wait_ge(S("l_qk_sb"), 16)
                for s in range(2):
                    for hg in range(2):
                        for j in range(4):
                            h = 4 * hg + j
                            ins = mm(bank(2 * s + hg, T * j, T * j + T), mQK[:, 8 + h, T * s:T * s + T], mQK[:, h, T * s:T * s + T], start=True, stop=True)
                        ins.then_inc(S("l_st"), 1)
                pe.wait_ge(S("l_w"), 32)
                for h in range(MH):
                    ins = tp(bank(5 + h // 4, T * (h % 4), T * (h % 4) + T), mQK[:, 8 + h, 0:T], ident)
                ins.then_inc(S("l_kt"), 1)
                pe.wait_ge(S("l_at_w"), 8)
                pe.wait_ge(S("n0"), 16)
                for i in range(16):
                    d, h = i // 8, i % 8
                    r = 32 * d + h
                    mm(PS[0:40, 4, 0:N2], c_("win")[:, 40 - r:80 - r], mW[:, :, d, h], start=(i == 0), stop=(i == 15))
                for i in range(16):
                    d, h = i // 8, i % 8
                    ins = mm(PS[0:40, 4, N2:N2 + T], mN0[:, i], mQK[:, h, T:N2], start=(i == 0), stop=(i == 15))
                ins.then_inc(S("l_den"), 1)
                c0 = landed(pe, n0 + 12)
                after(pe, "l_rr")
                for u in range(8):
                    wait(pe, "l_c0", u - 1)
                    for j in range(4):
                        ins = tp(bank(4 + 3 * (u % 2), P * j, P * j + P), c0[:, 4 * u + j], ident)
                    ins.then_inc(S("l_c0t"), 1)
                pe.wait_ge(S("l_stm"), 8)
                for i in range(16):
                    d, h = i // 8, i % 8
                    wait(pe, "l_sc", 2 * (i - 3))
                    spread(bank(i % 4, 0, 3 * T), 32 * d + h, mROW[0:40, 0:2].rearrange("p a b -> p (a b)")[:, 0:3 * T]).then_inc(S("l_rb"), 1)
                pe.wait_ge(S("l_kw"), 16)
                for h in range(MH):
                    wait(pe, "l_c_sb", h - 1)
                    for j in range(2):
                        at = MDV * h + P * j
                        ins = mm(bank(5 + h % 2, N2 * j, N2 * j + N2), mV[:, 0, at:at + P], mKW[:, h].rearrange("p a b -> p (a b)"), start=True, stop=True)
                    ins.then_inc(S("l_c"), 1)
                pe.wait_ge(S("l_c0"), 8)
                for d in range(2):
                    for h in range(MH):
                        ins = mm(bank(4, 8 * d + h, 8 * d + h + 1), mKW[:, h, d], ones[:, 0:1], start=True, stop=True)
                ins.then_inc(S("l_n"), 1)
                after(pe, "l_n_sb")
                tp(PS[0:16, 4, 128:256], mNS, ident).then_inc(S("l_nT"), 1)
                after(pe, "l_nT_sb")
                pe.wait_ge(S("l_sc"), 32)

                def sums(h):
                    pe.wait_ge(S("l_hq"), h + 1)
                    for j in range(2):
                        ins = mm(PS[0:8, 4, 0:N2], c_("win")[:, 40 - h:48 - h], mHQ[:, h % 2, j], start=(h == 0 and j == 0), stop=(h == MH - 1 and j == 1))
                    ins.then_inc(S("l_ss"), 1)

                for h in range(MH):
                    wait(pe, "l_hq", h - 3)
                    for j in range(2):
                        at = MDV * h + P * j
                        for s in range(2):
                            v = mV[:, s, at:at + P]
                            pairs = [(v, mW[:, s, 0, h]), (v, mW[:, s, 1, h])]
                            if s:
                                pairs += [(c0[:, 16 * d + 2 * h + j], mQS[:, d, h]) for d in range(2)]
                            ins = group(bank(h % 4, N2 * j + T * s, N2 * j + T * s + T), pairs)
                    ins.then_inc(S("l_h"), 1)
                    if h:
                        sums(h - 1)
                sums(MH - 1)
                after(pe, "l_rn")
                for h in range(MH):
                    ins = spread(bank((5, 6, 7, 4)[h // 2], N2 * (h % 2), N2 * (h % 2) + N2), h, mROW[0:8, 1], 8)
                ins.then_inc(S("l_rnb"), 1)
                for c in range(2):
                    for r in range(2):
                        w = landed(pe, n0 + 13 + 2 * c + r)
                        for m in range(4):
                            if r == 0:
                                if c:
                                    pe.wait_ge(S("x"), KD * 3 + m + 1)
                                elif m == 0:
                                    pe.wait_ge(S("l_hn"), 8)
                            elif m == 0:
                                pe.wait_ge(S("l_hn"), 16)
                            ins = group(bank(m, 0, N2), zip(tile(w, m), [mQK[:, 8 * r + k] for k in range(KD)]), None, first=(r == 0), final=(r == 1))
                            if r:
                                ins.then_inc(S("l_y"), 1)
                            elif m == 3:
                                ins.then_inc(S("l_y0"), 1)

            def gla():
                n0 = FIRST["mix2"]
                h_ready(4)
                pe.wait_ge(S("load_a"), 64)
                group(PS[0:64, 4, 0:N2], [(WA1[:, k], H[:, k]) for k in range(KD)], "g_u")

                def qk(c):
                    w = landed(pe, n0 + c)
                    for m in range(4):
                        wait(pe, "g_qk_sb", 4 * c + m - 3)
                        group(bank(m, 0, N2), zip(tile(w, m), [H[:, k] for k in range(KD)]), "g_qk")

                qk(0)
                after(pe, "g_u_sb")
                for d in range(2):
                    for h in range(GH):
                        ins = mm(bank(4 + 2 * d + h // 2, N2 * (h % 2), N2 * (h % 2) + N2), WA2[32 * d:32 * d + 16, P * h:P * h + P], gU[32 * d:32 * d + 16], start=True, stop=True)
                    ins.then_inc(S("g_z"), 1)
                qk(1)
                for i in range(4):
                    if i % 2 == 0:
                        w = landed(pe, n0 + 2 + i // 2)
                    pe.wait_ge(S("g_qk_sb"), 5 + i)
                    s = i % 2
                    group(bank(i), [(H[:, k, T * s:T * s + T], w[:, k]) for k in range(KD)], "g_v")
                for c in range(2):
                    w = landed(pe, n0 + 4 + c)
                    for m in range(4 * c, 4 * c + 4):
                        if m < 4:
                            pe.wait_ge(S("g_v_sb"), m + 1)
                        else:
                            pe.wait_ge(S("g_r_sb"), m - 3)
                        group(bank(m % 4, 0, N2), zip(tile(w, m % 4), [H[:, k] for k in range(KD)]), "g_r")
                pe.wait_ge(S("g_r_sb"), 8)
                for i in range(2 * NB):
                    d, blk, lo, hi = gla_block(i)
                    pe.wait_ge(S("g_ki"), i + 1)
                    pe.wait_ge(S("g_qi"), d + 1)
                    for hs in range(8):
                        ins = mm(PS[GB * blk:GB * blk + GB, 2 * d + hs // 4, T * (hs % 4):T * (hs % 4) + T],
                                 gQI[:, d, hs, GB * blk:GB * blk + GB], gKI[:, i % 2, hs], start=True, stop=True)
                    ins.then_inc(S("g_a"), 1)
                after(pe, "g_am")
                for hs in range(8):
                    ins = tp(bank(4 + hs // 4, T * (hs % 4), T * (hs % 4) + T), gT1[:, hs], ident)
                ins.then_inc(S("g_at"), 1)
                s0 = landed(pe, n0 + 6)
                pe.wait_ge(S("g_at_sb"), 2)
                pe.wait_ge(S("g_qxm"), 2)

                def sums(h):
                    pe.wait_ge(S("g_hq"), h + 1)
                    for j in range(2):
                        ins = mm(PS[0:8, 6, 0:N2], c_("win")[:, 40 - h:48 - h], gHQ[:, h % 2, j], start=(h == 0 and j == 0), stop=(h == GH - 1 and j == 1))
                    ins.then_inc(S("g_ss"), 1)

                for h in range(GH):
                    for j in range(2):
                        at = GDV * h + P * j
                        for s in range(2):
                            pairs = [(gV[:, s, at:at + P], gAT[:, 2 * h + s])]
                            if s:
                                pairs += [(s0[:, 4 * d + h, P * j:P * j + P], gQE[:, d, h]) for d in range(2)]
                            ins = group(bank(h, N2 * j + T * s, N2 * j + T * s + T), pairs)
                    ins.then_inc(S("g_o"), 1)
                    if h:
                        sums(h - 1)
                sums(GH - 1)
                after(pe, "g_rn")
                for h in range(GH):
                    ins = mm(bank(4 + h // 2, N2 * (h % 2), N2 * (h % 2) + N2), ident[0:8, h:h + 1].broadcast_to([8, P]), mROW[0:8, 0], start=True, stop=True)
                ins.then_inc(S("g_rnb"), 1)
                after(pe, "g_sm")
                for u in range(2):
                    if u:
                        pe.wait_ge(S("g_kt_sb"), 1)
                    for j in range(4):
                        ins = tp(bank(7, P * j, P * j + P), gT0[:, 4 * u + j], ident)
                    ins.then_inc(S("g_kt"), 1)
                pe.wait_ge(S("g_kt_sb"), 2)
                for i in range(4):
                    pe.wait_ge(S("g_hq"), i + 1)
                    for j in range(2):
                        r = 2 * i + j
                        ins = mm(bank(i, N2 * j, N2 * j + N2), gKD[:, r], gV[:, 0, GDV * (r % 4):GDV * (r % 4) + GDV], start=True, stop=True)
                    ins.then_inc(S("g_s"), 1)
                pe.wait_ge(S("g_on"), 8)
                pe.wait_ge(S("g_s_sb"), 4)
                out_proj("g_y", 0, n0 + 7, gOG, 4)

            def moe(l):
                E0 = NE * l
                n0 = FIRST[f"moe{l}"]
                n = 2 * l + 1
                if l == 0:
                    pe.wait_ge(S("load_rw"), 16)
                for k in range(KD):
                    h_ready(n, k)
                    ins = mm(PS[0:NE, 5, 0:N2], RW[:, k], H[:, k], start=(k == 0), stop=(k == KD - 1))
                ins.then_inc(S("logitT"), 1)
                for s in range(2):
                    for c in range(2):
                        for k in range(4 * c, 4 * c + 4):
                            ins = tp(bank(2 * s + c, P * (k % 4), P * (k % 4) + P), H[:, k, T * s:T * s + T], ident)
                        ins.then_inc(S("ht"), 1)
                pe.wait_ge(S("logitT_sb"), l + 1)
                for s in range(2):
                    ins = tp(bank(4, NE * s, NE * s + NE), RT[0:NE, T * s:T * s + T], ident[0:NE, 0:NE])
                ins.then_inc(S("logit"), 1)
                pe.wait_ge(S("routed"), l + 1)
                M = RT[:, 384:416].rearrange("p (s e) -> p s e", s=2)
                mm(bank(5, 0, NE), c_("lt"), M[:, 0], start=True, stop=True)
                mm(bank(5, NE, 2 * NE), c_("lt"), M[:, 1], start=True, stop=False)
                mm(bank(5, NE, 2 * NE), ones, M[:, 0], start=False, stop=True)
                mm(PS[0:1, 5, 32:48], ones[:, 0:1], M[:, 0], start=True, stop=False)
                mm(PS[0:1, 5, 32:48], ones[:, 0:1], M[:, 1], start=False, stop=True).then_inc(S("rank"), 1)
                pe.wait_ge(S("ht_sb"), 4 * (l + 1))

                def gather(sem):
                    for s in range(2):
                        for dh in range(2):
                            ins = mm(PS[64 * dh:64 * dh + 64, 6, :], PB[:, s], HT[:, s, 512 * dh:512 * dh + 512], start=(s == 0), stop=(s == 1))
                    ins.then_inc(S(sem), 1)

                def turn_w(sem):
                    for s in range(2):
                        ins = tp(bank(4, T * s, T * s + T), WB[:, s].rearrange("p a b -> p (a b)"), ident)
                    ins.then_inc(S(sem), 1)

                def turn_x(sem):
                    for j in range(4):
                        ins = tp(bank(6, P * j, P * j + P), GX[:, P * j:P * j + P], ident)
                    ins.then_inc(S(sem), 1)

                def up(w, b, sem):
                    for k in range(KD):
                        for fh in range(2):
                            ins = mm(PS[64 * fh:64 * fh + 64, b, 0:256], XG[:, k % 4, k // 4], w[:, k, 256 * fh:256 * fh + 256], start=(k == 0), stop=(k == KD - 1))
                    ins.then_inc(S(sem), 1)

                def turn_h(sem):
                    for j in range(2):
                        ins = tp(bank(5, P * j, P * j + P), HID[:, P * j:P * j + P], ident)
                    ins.then_inc(S(sem), 1)

                def down(w, sem):
                    for f in range(4):
                        for dh in range(2):
                            ins = mm(PS[64 * dh:64 * dh + 64, 7, :], HTS[:, f % 2, f // 2], w[:, f, 512 * dh:512 * dh + 512], start=(f == 0), stop=(f == 3))
                    ins.then_inc(S(sem), 1)

                def scatter(w, sem, first=False):
                    for q in range(4):
                        for dh in range(2):
                            t = 4 * dh + q
                            ins = mm(bank(t // 2, N2 * (t % 2), N2 * (t % 2) + N2), YS[64 * dh:64 * dh + 64, P * q:P * q + P],
                                     WTS[64 * dh:64 * dh + 64, w], start=first and t % 2 == 0, stop=True, skip_group_check=True)
                    ins.then_inc(S(sem), 1)

                def prepare(E):
                    pe.wait_ge(S("pw"), 6 * (E + 1))
                    gather("gather")

                def expert(e, E, i, first=False, more=True):
                    base = n0 + 3 * e
                    pe.wait_ge(S("xg"), E + 1)
                    w = landed(pe, base, i)
                    up(w, 4, "up")
                    w = landed(pe, base + 1, i)
                    up(w, 5, "up")
                    if not first:
                        pe.wait_ge(S("ys"), E)
                        scatter((e + 1) % 2, "scatter", first=(e == 1 and isinstance(i, int) and i == 0))
                    if more:
                        prepare(E + 1)
                    pe.wait_ge(S("hid"), E + 1)
                    turn_h("turn_h")
                    if more:
                        turn_w("turn_w")
                        pe.wait_ge(S("gx"), E + 2)
                        turn_x("turn_x")
                    pe.wait_ge(S("hts"), E + 1)
                    if more:
                        pe.wait_ge(S("wts"), E + 2)
                    w = landed(pe, base + 2, i)
                    down(w, "down")

                prepare(E0)
                turn_w("turn_w")
                pe.wait_ge(S("gx"), E0 + 1)
                turn_x("turn_x")
                pe.wait_ge(S("wts"), E0 + 1)
                expert(0, E0, 0, first=True)
                expert(1, E0 + 1, 0)
                with pe.Fori(1, NE // 2 - 1) as i:
                    expert(0, 2 * i + E0, i)
                    expert(1, 2 * i + (E0 + 1), i)
                expert(0, E0 + 14, 7)
                expert(1, E0 + 15, 7, more=False)
                pe.wait_ge(S("ys"), E0 + 16)
                scatter(1, "scatter")
                pe.wait_ge(S("table"), l + 1)
                nx = pe.value_load(EXI[0:1, 16:17], min_val=0, max_val=8)
                before = pe.value_load(EXI[0:1, 17:18], min_val=0, max_val=64)
                with pe.If(nx > 0):
                    with pe.Fori(0, nx) as i:
                        pe.wait_ge(S("x_pw"), before + i)
                        gather("x_gather")
                        turn_w("x_turn_w")
                        pe.wait_ge(S("x_gx"), before + i)
                        turn_x("x_turn_x")
                        pe.wait_ge(S("x_xg"), before + i)
                        pe.wait_ge(S("x_wts"), before + i)
                        for j in range(2):
                            pe.wait_ge(S(f"x_landed{j}"), 16 * before + 16 * i)
                            up(slot_view("wg", (n0 + 45 + j) % RING), 4 + j, ("x_up", "x_up2")[j])
                        pe.wait_ge(S("x_hid"), before + i)
                        turn_h("x_turn_h")
                        pe.wait_ge(S("x_hts"), before + i)
                        pe.wait_ge(S("x_landed2"), 16 * before + 16 * i)
                        down(slot_view("wd", (n0 + 47) % RING), "x_down")
                        pe.wait_ge(S("x_ys"), before + i)
                        scatter(0, "x_scatter")

            mod(0)
            for l in range(DEPTH):
                sumsq(2 * l)
                (lambda: attention(l // 3, l), mlstm, gla)[l % 3]()
                sumsq(2 * l + 1)
                if l + 1 < DEPTH:
                    pe.wait_ge(S("x"), KD * (2 * l + 2))
                    mod(l + 1)
                moe(l)
            sumsq(2 * DEPTH)
            pe.wait_ge(S("h0"), KD * (2 * DEPTH + 1))
            for s in range(2):
                for c in range(2):
                    for k in range(4 * c, 4 * c + 4):
                        ins = tp(bank(2 * s + c, P * (k % 4), P * (k % 4) + P), H[:, k, T * s:T * s + T], ident)
                    ins.then_inc(S("yT"), 1)

        @block.vector
        def _(v):
            run = serial(v)
            tt, ts, stt = v.tensor_tensor, v.tensor_scalar, v.scalar_tensor_tensor

            run(v.memset(PT, 0.0), "zero_rows")
            v.nop().then_inc(S("x_p"), 4)
            for b in range(4):
                v.wait_ge(S("xT"), b + 1)
                for k in (2 * b, 2 * b + 1):
                    run(v.tensor_copy(X[:, k], bank(b, N2 * (k % 2), N2 * (k % 2) + N2)), "x")
            after(v, "prmT")
            run(v.tensor_copy(PRM[:, :], bank(4, 0, NPR)), "prm")
            v.wait_ge(S("load_b"), 48)

            def mod(l):
                v.wait_ge(S("mod_cols"), 12 * (l + 1))
                m = MC[:, l % 2].rearrange("p (j s) -> p j s", s=2)
                run(tt(m, bank(6, 0, 96).rearrange("p (j s) -> p j s", s=2), last(prm("bm", 48, 48 * l), 2), ALU.add), "mod")
                for vec, g in ((1, "n1"), (4, "n2")):
                    mv = m[:, 8 * vec:8 * vec + 8]
                    run(stt(mv, mv, 1.0, last(prm(g, 8, 8 * l), 2), ALU.add, ALU.mult), "mod")

            def norm(n, l=None, vec=None):
                v.wait_ge(S("root"), n + 1)
                run(v.reciprocal(RS[:, 1], RS[:, 0]), "dve")

                def xn(k):
                    run(tt(H[:, k], X[:, k], RS[:, 1], ALU.mult), "xn")

                xn(0)
                for k in range(KD):
                    if k + 1 < KD:
                        xn(k + 1)
                    if l is not None:
                        run(ts(H[:, k, T:N2], H[:, k, T:N2], mod_col(l, vec + 1, k, 1), mod_col(l, vec, k, 1), ALU.mult, ALU.add), "h1")

            def residual(sem, base, l, vec, src):
                for m in range(KD):
                    if sem:
                        v.wait_ge(S(sem), base + m + 1)
                    y = src(m)
                    run(stt(X[:, m, 0:T], y[:, 0:T], mod_col(l, vec, m, 0), X[:, m, 0:T], ALU.mult, ALU.add), "dve")
                    run(stt(X[:, m, T:N2], y[:, T:N2], mod_col(l, vec, m, 1), X[:, m, T:N2], ALU.mult, ALU.add), "x")

            def attention(a, l):
                after(v, f"a_rot{l}")
                run(tt(RTMP[:, 0:4], bank(4).rearrange("p (m t) -> p m t", m=4), mid(c_("sin"), 4), ALU.mult), "dve")
                run(tt(RTMP[:, 4:8], bank(5).rearrange("p (m t) -> p m t", m=4), mid(c_("sin"), 4), ALU.mult), "dve")
                run(tt(RTMP[:, 8:10], bank(6, 0, N2).rearrange("p (m t) -> p m t", m=2), mid(c_("sin"), 2), ALU.mult), "dve")
                for dst, tmp, n in ((QT[:, :, T:N2], RTMP[:, 0:8], 8), (KR[:, :, T:N2], RTMP[:, 8:10], 2)):
                    run(tt(dst, dst, mid(c_("cos"), n), ALU.mult), "dve")
                    run(tt(dst, dst, tmp, ALU.add), "dve" if n == 8 else f"a_rope{l}")
                sink = SK[:, a]
                for g in range(KV):
                    n = 4 * a + g
                    v.wait_ge(S("a_s"), n + 1)
                    run(v.tensor_reduce(AMX.rearrange("p a b -> p (a b)"), PS[:, 0:4, 0:3 * T].rearrange("p j (c t) -> p j c t", c=3), AX.X, ALU.max), "dve")
                    run(tt(AMX[:, :, 1:2], AMX[:, :, 1:2], AMX[:, :, 2:3], ALU.max), "dve")
                    run(stt(AM2, AMX[:, :, 0:2], HD ** -0.5, last(sink[:, 4 * g:4 * g + 4], 2), ALU.mult, ALU.max), "dve")
                    run(tt(ASD, last(sink[:, 4 * g:4 * g + 4], 2), AM2, ALU.subtract), "dve")
                    run(ts(ANM, AM2, -1.0, None, ALU.mult), "a_neg")
                    v.wait_ge(S("a_exp"), 9 * (n + 1))
                    run(tt(AR_, ASUM, AES, ALU.add), "dve")
                    run(v.reciprocal(AR_, AR_), "dve")
                    run(tt(PBUF[:, :, 0:T], PBUF[:, :, 0:T], AR_[:, :, 0:1].broadcast_to([P, 4, T]), ALU.mult), "dve")
                    run(tt(PBUF[:, :, T:3 * T], PBUF[:, :, T:3 * T], AR_[:, :, 1:2].broadcast_to([P, 4, 2 * T]), ALU.mult), "a_p")
                    v.wait_ge(S("a_pt"), n + 1)
                    wait(v, "a_pv", n)
                    for part in range(2):
                        run(v.tensor_copy(PTB[:, part], bank(4 + part).rearrange("p (j t) -> p j t", j=4)), "a_ptV")
                residual("a_y", 8 * a, l, 2, lambda m: bank(m % 4, 0, N2))

            def mlstm():
                R = [mROW[0:40, j] for j in range(4)]
                gi, gf, e, b = R
                after(v, "l_g")
                v.wait_ge(S("load_g"), 160)
                run(ts(gi, PS[0:40, 7, 0:N2], BGT[:, 0:1], None, ALU.add), "dve")
                run(ts(gf, PS[0:40, 7, N2:512], BGT[:, 1:2], None, ALU.add), "dve")
                run(stt(e, gf, -1.0, gf, ALU.mult, ALU.max), "l_abs")
                v.wait_ge(S("l_ln"), 2)
                run(stt(gf, gf, 0.0, e, ALU.min, ALU.subtract), "dve")
                run(v.memset(b, 0.0), "dve")
                run(v.memset(mRM[0:40], 0.0), "dve")
                def both(dst, src, init, op1, ones_=ones):
                    for d in range(2):
                        for s in range(2):
                            rows = slice(32 * d, 32 * d + 8)
                            o = dst[rows, T * s:T * s + T]
                            i = src[rows, T * s:T * s + T]
                            if d:
                                o, i = o[:, ::-1], i[:, ::-1]
                            run(v.tensor_tensor_scan(o, ones[rows], i, 0.0 if init is None else init[rows, s:s + 1], ALU.mult, op1), "dve")
                both(b, gf, None, ALU.add)
                run(tt(gi, gi, b, ALU.subtract), "dve")
                both(mRM[:, 0], gi, M0, ALU.max)
                run(tt(mRM[0:40, 1], mRM[0:40, 0], b, ALU.add), "dve")
                for s in range(2):
                    run(ts(mRM[0:40, 2, T * s:T * s + T], mRM[0:40, 0, T * s:T * s + T], M0[:, s:s + 1], None, ALU.subtract), "dve" if s == 0 else "l_rows")
                for m in range(16):
                    v.wait_ge(S("l_raw"), m + 1)
                    x3 = mRAW[:, m % 4].rearrange("p (s t) -> p s t", s=2)
                    y3 = mQK[:, m].rearrange("p (s t) -> p s t", s=2)
                    w = [prm("conv", 1, 16 * j + m) for j in range(3)]
                    run(ts(y3, x3, w[1], None, ALU.mult), "dve")
                    run(stt(y3[:, :, 1:T], x3[:, :, 0:T - 1], w[0], y3[:, :, 1:T], ALU.mult, ALU.add), "dve")
                    run(stt(y3[:, :, 0:T - 1], x3[:, :, 1:T], w[2], y3[:, :, 0:T - 1], ALU.mult, ALU.add), "l_conv")
                after(v, "l_at")
                run(v.tensor_copy(mAC, bank(7, 0, 80).rearrange("p (s r) -> p s r", s=2)), "l_ac")
                for q in range(4):
                    d, hg = q // 2, q % 2
                    v.wait_ge(S("l_mb"), q + 1)
                    for j in range(4):
                        h = 4 * hg + j
                        r = 32 * d + h
                        for s in range(2):
                            src = bank(4 + 2 * (q % 2) + j // 2, N2 * (j % 2) + T * s, N2 * (j % 2) + T * s + T)
                            run(ts(mW[:, s, d, h], src, mAC[:, s, r:r + 1], 0.0, ALU.subtract, ALU.max), "l_w")
                v.wait_ge(S("l_we"), 8)
                for d in range(2):
                    t = T - 1 if d == 0 else 0
                    run(v.tensor_copy(mWL[:, 8 * d:8 * d + 8], mW[:, 0, d, :, t]), "dve")
                for s in range(2):
                    for hg in range(2):
                        v.wait_ge(S("l_st"), 2 * s + hg + 1)
                        for d in range(2):
                            run(stt(mTMP, bank(2 * s + hg).rearrange("p (j t) -> p j t", j=4), MDK ** -0.5, mid(c_(("le", "ge")[d]), 4), ALU.mult, ALU.mult), "l_stm")
                            w = mW[:, s, d, 4 * hg:4 * hg + 4]
                            run(tt(w, w, mTMP, ALU.mult), "l_at_w")
                after(v, "l_kt")
                for d in range(2):
                    for h in range(MH):
                        run(ts(mKW[:, h, d], bank(5 + h // 4, T * (h % 4), T * (h % 4) + T), mWL[:, 8 * d + h:8 * d + h + 1], MDK ** -0.5, ALU.mult, ALU.mult), "l_kw")
                after(v, "l_den")
                after(v, "l_rowexp")
                run(v.tensor_copy(e, PS[0:40, 4, 0:N2]), "dve")
                run(tt(b[:, 0:T], PS[0:40, 4, N2:N2 + T], mSC[0:40, T:N2], ALU.mult), "dve")
                run(tt(e[:, T:N2], e[:, T:N2], b[:, 0:T], ALU.add), "dve")
                run(stt(b, e, -1.0, e, ALU.mult, ALU.max), "dve")
                run(tt(b, b, mEM[0:40], ALU.max), "dve")
                run(v.reciprocal(gi, b), "dve")
                run(tt(gf[:, 0:T], gi[:, T:N2], mSC[0:40, T:N2], ALU.mult), "l_rr")
                for i in range(16):
                    d, h = i // 8, i % 8
                    v.wait_ge(S("l_rb"), i + 1)
                    w = mW[:, :, d, h]
                    run(tt(w, w, bank(i % 4, 0, N2).rearrange("p (s t) -> p s t", s=2), ALU.mult), "l_sc")
                    run(tt(mQS[:, d, h], mQK[:, h, T:N2], bank(i % 4, N2, 3 * T), ALU.mult), "l_sc")
                after(v, "l_root")
                run(v.reciprocal(mROW[0:8, 1], mROW[0:8, 0]), "l_rn")
                after(v, "l_rnb")
                for m in range(16):
                    h = m // 2
                    hb = bank((5, 6, 7, 4)[h // 2], N2 * (h % 2), N2 * (h % 2) + N2)
                    run(stt(mQK[:, m], mQK[:, m], prm("mg", 1, m), hb, ALU.mult, ALU.mult), "dve")
                    run(tt(mQK[:, m], mQK[:, m], mO[:, m], ALU.mult), "l_hn")
                residual("l_y", 0, 1, 2, lambda m: bank(m % 4, 0, N2))

            def gla():
                for d in range(2):
                    v.wait_ge(S("g_z"), d + 1)
                    for h in range(GH):
                        run(ts(gLA[:, d, 2 * h:2 * h + 2], bank(4 + 2 * d + h // 2, N2 * (h % 2), N2 * (h % 2) + N2).rearrange("p (s t) -> p s t", s=2),
                               prm("ba", 1, 4 * d + h), None, ALU.add), "dve")
                    run(stt(gAX[:, d], gLA[:, d], -1.0, gLA[:, d], ALU.mult, ALU.max), "g_abs")
                for d in range(2):
                    v.wait_ge(S("g_ln"), 2 * d + 2)
                    run(stt(gLA[:, d], gLA[:, d], 0.0, gAX[:, d], ALU.min, ALU.subtract), "dve")
                    for hs in range(8):
                        o, i = gB[:, d, hs], gLA[:, d, hs]
                        if d:
                            o, i = o[:, ::-1], i[:, ::-1]
                        run(v.tensor_tensor_scan(o, ones, i, 0.0, ALU.mult, ALU.add), "dve")
                run(v.memset(gKI, 0.0), "dve")
                for d in range(2):
                    b32 = gB[:, d].rearrange("p a (i t) -> p (a i) t", t=GB)
                    run(tt(gQI[:, d].rearrange("p a (i t) -> p (a i) t", t=GB), b32, b32[:, :, GB // 2:GB // 2 + 1].broadcast_to([P, 8 * NB, GB]), ALU.subtract), "g_qd")

                def diff(i):
                    d, blk, lo, hi = gla_block(i)
                    ref = gB[:, d, :, GB * blk + GB // 2:GB * blk + GB // 2 + 1].broadcast_to([P, 8, hi - lo])
                    run(tt((gT0, gT1)[i % 2][:, :, lo:hi], ref, gB[:, d, :, lo:hi], ALU.subtract), "g_kd")

                diff(0)
                v.wait_ge(S("g_qk_sb"), 8)
                for d in range(2):
                    v.wait_ge(S("g_qe"), d + 1)
                    run(tt(gQI[:, d], gQI[:, d], gQ, ALU.mult), "g_qi")
                for i in range(2 * NB):
                    if i + 1 < 2 * NB:
                        diff(i + 1)
                    d, blk, lo, hi = gla_block(i)
                    wait(v, "g_a", NB if i == NB else i - 1)
                    if i == NB:
                        run(v.memset(gKI, 0.0), "dve")
                    v.wait_ge(S("g_ke"), i + 1)
                    run(tt(gKI[:, i % 2, :, lo:hi], (gT0, gT1)[i % 2][:, :, lo:hi], gK[:, :, lo:hi], ALU.mult), "g_ki")
                v.wait_ge(S("g_a"), 2 * NB)
                for d, mask in ((0, "ge"), (1, "le")):
                    for c in range(2):
                        run(tt((gT1, gKI[:, 0])[d][:, 4 * c:4 * c + 4], bank(2 * d + c).rearrange("p (j t) -> p j t", j=4), mid(c_(mask), 4), ALU.mult), "dve")
                run(tt(gT1, gT1, gKI[:, 0], ALU.add), "g_am")
                v.wait_ge(S("g_qx"), 2)
                q1 = gQ.rearrange("p (h s) t -> p h s t", s=2)[:, :, 1]
                for d in range(2):
                    run(tt(gQE[:, d], gQE[:, d], q1, ALU.mult), "g_qxm")
                kc = gK.rearrange("p (h s) t -> p h s t", s=2)[:, :, 0]
                for d in range(2):
                    bcx = gB[:, d].rearrange("p (h s) t -> p h s t", s=2)[:, :, 0]
                    t = T - 1 if d == 0 else 0
                    run(tt(gT0[:, 4 * d:4 * d + 4], bcx[:, :, t:t + 1].broadcast_to([P, 4, T]), bcx, ALU.subtract), "g_sd")
                after(v, "g_at")
                for c in range(2):
                    run(v.tensor_copy(gAT[:, 4 * c:4 * c + 4], bank(4 + c).rearrange("p (j t) -> p j t", j=4)), "g_at_sb")
                after(v, "g_se")
                for d in range(2):
                    run(tt(gT0[:, 4 * d:4 * d + 4], gT0[:, 4 * d:4 * d + 4], kc, ALU.mult), "dve" if d == 0 else "g_sm")
                after(v, "g_root")
                run(v.reciprocal(mROW[0:8, 0], mROW[0:8, 1]), "g_rn")
                after(v, "g_rnb")
                for m in range(8):
                    hb = bank(4 + m // 4, N2 * (m // 2 % 2), N2 * (m // 2 % 2) + N2)
                    run(stt(gOG[:, m], gOG[:, m], prm("gg", 1, m), hb, ALU.mult, ALU.mult), "dve")
                    run(tt(gOG[:, m], gOG[:, m], gR[:, m], ALU.mult), "g_on")
                for u in range(2):
                    v.wait_ge(S("g_kt"), u + 1)
                    run(v.tensor_copy(gKD[:, 4 * u:4 * u + 4], bank(7).rearrange("p (j t) -> p j t", j=4)), "g_kt_sb")
                residual("g_y", 0, 2, 2, lambda m: bank(m % 4, 0, N2))

            def moe(l):
                def two(at, n=NE):
                    return RT[:, at:at + 2 * n].rearrange("p (s e) -> p s e", s=2)

                def flat(at, n):
                    return RT[:, at:at + n]

                def go(ins, sem="dve"):
                    run(ins, sem)

                sc, sel, M, cmb, rk = two(256), two(288), two(384), two(416), two(448)
                v.wait_ge(S("score"), l + 1)
                go(tt(sel, sc, mid(RB[:, :], 2), ALU.add))
                s4 = RT[:, 288:320].rearrange("p (g a b) -> p g a b", a=2, b=2)
                pr = RT[:, 512:528].rearrange("p (g a) -> p g a", a=2)
                lo = RT[:, 528:544].rearrange("p (g a) -> p g a", a=2)
                go(tt(pr, s4[:, :, :, 0], s4[:, :, :, 1], ALU.max))
                go(tt(lo, s4[:, :, :, 0], s4[:, :, :, 1], ALU.min))
                t1, t2, t3 = flat(544, 8), flat(552, 8), flat(560, 8)
                go(tt(t1, pr[:, :, 0], pr[:, :, 1], ALU.max))
                go(tt(t2, pr[:, :, 0], pr[:, :, 1], ALU.min))
                go(tt(t3, lo[:, :, 0], lo[:, :, 1], ALU.max))
                go(tt(t2, t2, t3, ALU.max))
                go(tt(t1, t1, t2, ALU.add))

                def best(src, prio, n, out, s0):
                    mx, eq = flat(s0, 2), flat(s0 + 8, 2 * n).rearrange("p (s e) -> p s e", s=2)
                    go(v.tensor_reduce(mx, src, AX.X, ALU.max))
                    go(tt(eq, src, last(mx, n), ALU.is_equal))
                    go(tt(eq, eq, prio.rearrange("p (s e) -> p s e", s=2), ALU.mult))
                    go(v.tensor_reduce(mx, eq, AX.X, ALU.max))
                    go(tt(out, eq, last(mx, n), ALU.is_equal))

                gm = flat(572, 8).rearrange("p (s g) -> p s g", s=2)
                best(t1.rearrange("p (s g) -> p s g", s=2), c_("gprio"), NG, gm, 600)
                big = flat(584, 8)
                go(ts(big, flat(572, 8), 1.0, 1e30, ALU.subtract, ALU.mult))
                sg = RT[:, 288:320].rearrange("p (g e) -> p g e", e=EPG)
                go(tt(sg, sg, last(flat(572, 8), EPG), ALU.mult))
                go(tt(sg, sg, last(big, EPG), ALU.add))
                oh1, oh2 = two(640), two(672)
                best(sel, c_("prio"), NE, oh1, 720)
                go(stt(sel, oh1, -2e30, sel, ALU.mult, ALU.add))
                best(sel, c_("prio"), NE, oh2, 720)
                go(tt(M, oh1, oh2, ALU.add), "routed")
                go(tt(cmb, M, sc, ALU.mult))
                ws = flat(800, 2)
                go(v.tensor_reduce(ws, cmb, AX.X, ALU.add))
                go(v.reciprocal(ws, ws))
                go(tt(cmb, cmb, last(ws, NE), ALU.mult))
                v.wait_ge(S("rank"), l + 1)
                go(stt(rk, bank(5, 0, 2 * NE).rearrange("p (s e) -> p s e", s=2), 1.0, M, ALU.add, ALU.mult))
                cnt = RT[0:1, 804:820]
                go(v.tensor_copy(cnt, PS[0:1, 5, 32:48]))

                def slots(e_col, lo, sem):
                    for s in range(2):
                        r, c = e_col(rk, s), e_col(cmb, s)
                        yield ts(PB[:, s], lo, r, None, ALU.is_equal)
                        for y in range(2):
                            yield ts(WB[:, s, y], lo, r, c, ALU.is_equal, ALU.mult)

                S1 = c_("slot1")

                def weights(e, E):
                    wait(v, "turn_w", E)
                    for j, ins in enumerate(slots(lambda t, s: t[:, s, e:e + 1] if isinstance(e, int) else t[:, s, bass.ds(e, 1)], S1[:, 0:SLOTS], "pw")):
                        ins.then_inc(S("pw"), 1)
                        v.wait_ge(S("pw"), 6 * E + j + 1)

                def copy(dst, src, sem, value):
                    v.tensor_copy(dst, src).then_inc(S(sem), 1)
                    v.wait_ge(S(sem), value)

                def wts(E, par):
                    wait(v, "turn_w", E + 1)
                    copy(WTS[:, par], bank(4, 0, N2), "wts", E + 1)

                def xg(E):
                    v.wait_ge(S("turn_x"), E + 1)
                    copy(XG, bank(6).rearrange("p (j h s) -> p j h s", j=4, h=2), "xg", E + 1)

                def expert(e, E, ahead=2):
                    v.wait_ge(S("up"), 2 * E + 2)
                    v.wait_ge(S("silu"), E + 1)
                    tt(HID, SG, bank(5, 0, 256), ALU.mult).then_inc(S("hid"), 1)
                    v.wait_ge(S("hid"), E + 1)
                    v.wait_ge(S("turn_h"), E + 1)
                    copy(HTS, bank(5, 0, 256).rearrange("p (j h s) -> p j h s", j=2, h=2), "hts", E + 1)
                    if ahead:
                        wts(E + 1, (e + 1) % 2)
                        xg(E + 1)

                E0 = NE * l
                weights(0, E0)
                wts(E0, 0)
                xg(E0)
                weights(1, E0 + 1)
                fl, cu = RT[0:1, 832:880], RT[0:1, 880:928]
                for b in range(3):
                    go(ts(RT[0:1, 832 + 16 * b:848 + 16 * b], cnt, 64.0 * (b + 1), None, ALU.is_gt), "dve")
                go(v.tensor_tensor_scan(cu, ones[0:1, 0:48], fl, 0.0, ALU.mult, ALU.add), "dve")
                go(tt(fl, fl, cu, ALU.mult), "dve")
                eq = RT[0:1, 1024:1408].rearrange("p (j i) -> p j i", j=8)
                ec = RT[0:1, 1408:1792].rearrange("p (j i) -> p j i", j=8)
                go(tt(eq, mid(fl, 8), last(c_("j1")[0:1], 48), ALU.is_equal), "dve")
                fx = RT[0:1, 1792:1816]
                for j, code in enumerate(("code_e", "code_b")):
                    go(tt(ec, eq, mid(c_(code)[0:1], 8), ALU.mult), "dve")
                    go(v.tensor_reduce(fx[:, 8 * j:8 * j + 8], ec, AX.X, ALU.add), "dve")
                go(v.tensor_copy(fx[:, 16:17], cu[:, 47:48]), "dve")
                cum = sm(632, 8)[0:1, 0:1]
                if l == 0:
                    go(v.memset(cum, 0.0), "dve")
                go(ts(fx[:, 17:18], cum, 1.0, None, ALU.add), "dve")
                go(tt(cum, cum, cu[:, 47:48], ALU.add), "dve")
                go(v.tensor_copy(EXI[0:1, 0:18], fx[:, 0:18]), "table")

                expert(0, E0)
                weights(2, E0 + 2)
                expert(1, E0 + 1)
                weights(3, E0 + 3)
                with v.Fori(1, NE // 2 - 1) as i:
                    expert(0, 2 * i + E0)
                    weights(2 * i + 2, 2 * i + (E0 + 2))
                    expert(1, 2 * i + (E0 + 1))
                    weights(2 * i + 3, 2 * i + (E0 + 3))
                expert(0, E0 + 14)
                expert(1, E0 + 15, ahead=0)
                nx = v.value_load(EXI[0:1, 16:17], min_val=0, max_val=8)
                before = v.value_load(EXI[0:1, 17:18], min_val=0, max_val=64)
                v.wait_ge(S("scatter"), E0 + 16)
                with v.If(nx > 0):
                    with v.Fori(0, nx) as i:
                        e = v.value_load(EXI[0:1, bass.ds(i, 1)], min_val=0, max_val=NE - 1)
                        lo = v.value_load(EXI[0:1, bass.ds(i + 8, 1)], min_val=64, max_val=192)
                        v.wait_ge(S("x_scatter"), before + i)
                        for j, ins in enumerate(slots(lambda t, s: t[:, s, bass.ds(e, 1)], S1[:, bass.ds(lo, SLOTS)], "x_p")):
                            ins.then_inc(S("x_p" if j < 5 else "x_pw"), 1)
                            if j < 5:
                                v.wait_ge(S("x_p"), 5 * before + 5 * i + j)
                            else:
                                v.wait_ge(S("x_pw"), before + i)
                        v.wait_ge(S("x_turn_w"), before + i)
                        copy(WTS[:, 0], bank(4, 0, N2), "x_wts", before + i)
                        v.wait_ge(S("x_turn_x"), before + i)
                        copy(XG, bank(6).rearrange("p (j h s) -> p j h s", j=4, h=2), "x_xg", before + i)
                        v.wait_ge(S("x_up2"), before + i)
                        v.wait_ge(S("x_silu"), before + i)
                        tt(HID, SG, bank(5, 0, 256), ALU.mult).then_inc(S("x_hid"), 1)
                        v.wait_ge(S("x_hid"), before + i)
                        v.wait_ge(S("x_turn_h"), before + i)
                        copy(HTS, bank(5, 0, 256).rearrange("p (j h s) -> p j h s", j=2, h=2), "x_hts", before + i)
                v.wait_ge(S("x_scatter"), before + nx)
                residual(None, 0, l, 5, lambda m: bank(m // 2, N2 * (m % 2), N2 * (m % 2) + N2))

            mod(0)
            for l in range(DEPTH):
                norm(2 * l, l, 0)
                (lambda: attention(l // 3, l), mlstm, gla)[l % 3]()
                norm(2 * l + 1, l, 3)
                if l + 1 < DEPTH:
                    mod(l + 1)
                moe(l)
            norm(2 * DEPTH)


INS = ["x_prompt", "x_sample", "cache_k_0", "cache_v_0", "state_mlstm_C_1", "state_mlstm_n_1", "state_mlstm_m_1",
       "state_gla_S_2", "cache_k_3", "cache_v_3", "c", "c_ctx", "w_mod", "b_mod", "norm1_g", "norm2_g", "final_g",
       "router_w", "router_b", "moe_wg", "moe_wu", "moe_wd", "attn0_w_qkv", "attn0_sink", "attn0_w_o",
       "mlstm1_w_in", "mlstm1_b_gates", "mlstm1_conv", "mlstm1_norm_g", "mlstm1_w_out", "gla2_w_in", "gla2_w_a1",
       "gla2_w_a2", "gla2_b_a", "gla2_norm_g", "gla2_w_out", "attn3_w_qkv", "attn3_sink", "attn3_w_o"]
OUTS = [("y_prompt", (1, T, D)), ("y_sample", (1, T, D)), ("cache_k_0", (1, T, KV, HD)), ("cache_v_0", (1, T, KV, HD)),
        ("C", (1, 2, MH, MDV, MDK)), ("n", (1, 2, MH, MDK)), ("m", (1, 2, MH)), ("S", (1, 2, GH, GDK, GDV)),
        ("cache_k_3", (1, T, KV, HD)), ("cache_v_3", (1, T, KV, HD))]


def kernel(**inputs):
    import concourse.bacc as bacc
    from concourse.bass_utils import run_bass_kernel_spmd

    nc = bacc.Bacc("TRN2", target_bir_lowering=False, num_devices=1)
    arrays = {f"in_{k}": np.ascontiguousarray(inputs[k]) for k in INS}
    arrays["in_consts"] = constants()
    I = {k[3:]: nc.dram_tensor(k, a.shape, F32, kind="ExternalInput").ap() for k, a in arrays.items()}
    O = {k: nc.dram_tensor(f"out_{k}", s, F32, kind="ExternalOutput").ap() for k, s in OUTS}
    program(nc, I, O)
    r = run_bass_kernel_spmd(nc, [arrays], core_ids=[0])
    return tuple(r.results[0][f"out_{k}"] for k, _ in OUTS)
```

```python
from contextlib import ExitStack

import numpy as np
import concourse.bass as bass
from concourse import mybir

F32 = mybir.dt.float32
I32 = mybir.dt.int32
ALU = mybir.AluOpType
ACT = mybir.ActivationFunctionType
AX = mybir.AxisListType

P = 128
D = 1024
T = 128
N2 = 2 * T
KD = D // P
DEPTH = 4
EPS = 1e-6
HEADS, KV, HD = 16, 4, 64
MH, MDK, MDV = 8, 128, 256
GH, GDK, GDV = 4, 128, 256
NE, NG, EPG = 16, 4, 4
FE = 512
SLOTS = 64
NPAIR = NE // 2
RING = 6
GB = 32
NB = T // GB

CONST = {}


def constants():
    cols, at = [], 0

    def add(name, a):
        nonlocal at
        full = np.zeros((P, a.shape[1]), np.float32)
        full[:a.shape[0]] = a
        CONST[name] = (at, at + a.shape[1])
        cols.append(full)
        at += a.shape[1]

    i = np.arange(P)
    add("ident", np.eye(P))
    add("ones", np.ones((P, P)))
    half, nf = HD // 2, HD // 4
    inv = 10000.0 ** (-np.arange(nf, dtype=np.float32) / np.float32(nf))
    f = i % HD
    pos = np.where(f[:, None] < half, (i // 64)[None, :], (i % 64)[None, :]).astype(np.float32)
    ang = pos * inv.astype(np.float32)[f % nf][:, None]
    add("cos", np.cos(ang))
    add("sin", np.sin(ang))
    rot = np.zeros((P, P), np.float32)
    for m in range(P):
        if m % half < nf:
            rot[m + nf, m] = -1.0
        else:
            rot[m - nf, m] = 1.0
    add("rot", rot)
    for j in range(2):
        dup = np.zeros((P, P), np.float32)
        for m in range(P):
            dup[64 * j + m % 64, m] = 1.0
        add(f"dup{j}", dup)
    add("le", (i[:, None] <= i[None, :]))
    add("ge", (i[:, None] >= i[None, :]))
    add("lt", (i[:, None] < i[None, :]))
    add("slot1", np.broadcast_to(1.0 + np.arange(2 * P), (P, 2 * P)))
    win = np.zeros((P, 80))
    win[:, 40] = 1.0
    add("win", win)
    selm = np.zeros((P, 2))
    for j in range(4):
        selm[32 * j, 0] = selm[32 * j + 1, 1] = 1.0
    add("selm", selm)
    add("prio", np.broadcast_to(np.tile(16.0 - np.arange(16), 2), (P, 32)))
    add("gprio", np.broadcast_to(np.tile(4.0 - np.arange(4), 2), (P, 8)))
    add("j1", np.broadcast_to(1.0 + np.arange(8), (P, 8)))
    add("code_e", np.broadcast_to(np.tile(np.arange(16.0), 3), (P, 48)))
    add("code_b", np.broadcast_to(np.repeat(64.0 * np.arange(1, 4), 16), (P, 48)))
    add("eps", np.full((P, 1), EPS))
    return np.concatenate(cols, 1).astype(np.float32)


constants()
NCONST = max(b for _, b in CONST.values())

PR = {"n1": 0, "n2": 32, "fin": 64, "cc": 72, "cl": 80, "mg": 88, "gg": 104, "ba": 112,
      "bm": 128, "conv": 320, "n0": 368}
NPR = 384


def plan_chunks():
    chunks = []
    mod = lambda l, lo, hi: [("mod", l, c) for c in range(lo, hi)]
    chunks += mod(0, 0, 4)
    chunks += [("qkv", 0, 2)] + mod(0, 4, 8) + [("qkv", 0, 0)] + mod(0, 8, 12) + [("qkv", 0, 1)] + mod(1, 0, 8)
    chunks += [("wo", 0, 0), ("wo", 0, 1)]
    for l in range(DEPTH):
        if l == 1:
            for c in range(12):
                chunks += [("min", 1, c)] + (mod(2, c, c + 1) if c < 8 else [])
            chunks += [("c0", 1, 0)] + [("mout", 1, (c, r)) for c in range(2) for r in range(2)]
        if l == 2:
            for c in range(6):
                chunks += [("gin", 2, c)] + (mod(3, 2 * c, 2 * c + 2) if c < 4 else [])
            chunks += [("s0", 2, 0)] + [("gout", 2, c) for c in range(2)]
        if l == 3:
            chunks += [("qkv", 3, c) for c in (2, 0, 1)] + [("wo", 3, c) for c in range(2)]
        if l + 1 < DEPTH:
            chunks += mod(l + 1, 8, 12)
        chunks += [(w, l, 2 * p + e) for p in range(NPAIR) for w in ("wg", "wu", "wd") for e in range(2)]
    return chunks


CHUNKS = plan_chunks()
POS = {chunk: n for n, chunk in enumerate(CHUNKS)}


def mod_count(l, c):
    return 14 * l + c + 1 + (c > 3) + (c > 9)


WARM = (8, 2, 8, 4, 8, 1)

UNITS = [(0, c) for c in range(4, 12)] + [(1, c) for c in range(4)]

STEPS = {
    "tensor_step": ["prmT", "a_rotk0", "a_dup0", "a_rotA0", "a_rotB0", "l_g", "l_at", "l_kt", "l_den", "l_n", "l_nT", "l_rnb",
                    "g_u", "g_at", "g_rnb", "a_rotk3", "a_dup3", "a_rotA3", "a_rotB3"],
    "vector_step": ["zero_rows", "prm", "a_ropek0", "a_ropeA0", "a_ropeB0", "l_abs", "l_rows", "l_ac", "l_rr", "l_rn", "g_am", "g_sm", "g_rn",
                    "a_ropek3", "a_ropeA3", "a_ropeB3"],
    "scalar_step": ["cs", "l_rowexp", "l_n_sb", "l_nT_sb", "l_root", "g_u_sb", "g_gate", "g_se", "g_root"],
}
STEP = {name: (sem, i + 1) for sem, names in STEPS.items() for i, name in enumerate(names)}
def program(nc, I, O):
    with ExitStack() as ctx:
        def sb(name, shape, dt=F32):
            return ctx.enter_context(nc.sbuf_tensor(name, shape, dt))

        sems = {}

        def S(name):
            name = STEP[name][0] if name in STEP else name
            if name not in sems:
                sems[name] = ctx.enter_context(nc.semaphore(name))
            return sems[name]

        PS = ctx.enter_context(nc.psum_tensor("PS", [P, 8, 512], F32))
        ring = sb("ring", [P, RING, 8, 512])
        CN = sb("consts", [P, NCONST])
        PRM = sb("prm", [P, NPR])
        X = sb("X", [P, KD, N2])
        H = sb("H", [P, KD, N2])
        SQ = sb("SQ", [P, KD, N2])
        RS = sb("RS", [P, 2, N2])
        MC = sb("MC", [P, 2, 96])
        CS = sb("CS", [P, KD, 32])
        RW = sb("RW", [P, KD, NE])
        RB = sb("RB", [P, NE])
        SK = sb("SK", [P, 2, HEADS])
        WGT = sb("WGT", [P, KD, 2, 40])
        BGT = sb("BGT", [40, 2])
        M0 = sb("M0", [40, 2])
        EXI = sb("EXI", [1, 24], I32)
        small = sb("small", [P, 640])
        ARN = 17800
        arena = sb("arena", [P, ARN])

        def shaped(v, shape):
            if len(shape) == 2:
                return v.rearrange("p (a b) -> p a b", a=shape[0])
            if len(shape) == 3:
                return v.rearrange("p (a b c) -> p a b c", a=shape[0], b=shape[1])
            if len(shape) == 4:
                return v.rearrange("p (a b c d) -> p a b c d", a=shape[0], b=shape[1], c=shape[2])
            return v

        def ar(at, *shape):
            n = int(np.prod(shape))
            assert at + n <= ARN, (at, shape)
            return shaped(arena[:, at:at + n], shape)

        def sq(at, *shape):
            return shaped(SQ[:, :, :].rearrange("p a b -> p (a b)")[:, at:at + int(np.prod(shape))], shape)

        def sm(at, *shape):
            return shaped(small[:, at:at + int(np.prod(shape))], shape)

        def c_(name):
            a, b = CONST[name]
            return CN[:, a:b]

        def prm(name, n, off=0):
            return PRM[:, PR[name] + off:PR[name] + off + n]

        def bank(b, lo=0, hi=512):
            return PS[:, b, lo:hi]

        def mod_col(l, v, k, s):
            j = (v * 8 + k) * 2 + s
            return MC[:, l % 2, j:j + 1]

        def last(ap, n):
            return ap.unsqueeze(len(ap.shape)).broadcast_to(list(ap.shape) + [n])

        def mid(ap, n):
            return ap.unsqueeze(1).broadcast_to([ap.shape[0], n, ap.shape[1]])

        ident, ones = c_("ident"), c_("ones")
        BANKS = ((4, 5), (6, 7))

        XR = ar(0, 2, 1024)
        PT = ar(4096, 3, P)
        HT = ar(0, 2, 1024)
        GX = ar(2048, 1024)
        XG = ar(3072, KD, P)
        SG = ar(4096, FE)
        HID = ar(4608, FE)
        HTS = ar(5120, FE // P, P)
        WTS = ar(5632, 2, N2)
        YS = ar(6144, 1024)
        PB = ar(7168, 2, 2, SLOTS)
        WB = ar(7424, 2, 2, SLOTS)
        RT = ar(7680, 1920)
        EXTRA = [ar(9608 + 4096 * e, 8, 512) for e in range(2)]
        MPW = ar(6144, 512)
        MP = [ar(16000, 512), ar(16000, 512), ar(12288, 512), ar(15360, 512)]

        QT = ar(0, 8, N2)
        KR = ar(2048, 2, N2)
        KDUP = ar(2560, KV, 3, T)
        KC = ar(4096, 512)
        VL = ar(4608, 256)
        CV = ar(4864, 256)
        CK = ar(5120, KV, 2, HD)
        RTMP = ar(5632, 10, T)
        PBUF = ar(6912, 4, 3 * T)
        PTB = ar(8448, 3, 4, T)
        OT = ar(9984, 8, N2)
        AMX, AM2, ANM, ASD, ASUM, AES, AR_ = (sm(0, 4, 3), sm(16, 4, 2), sm(32, 4, 2), sm(40, 4, 2), sm(48, 4, 2),
                                              sm(56, 4, 2), sm(64, 4, 2))

        mQK = ar(0, 16, N2)
        mKW = ar(2048, MH, 2, T)
        mV = ar(4096, 2, 2048)
        mO = ar(8192, 16, N2)
        mW = ar(12288, 2, 2, MH, T)
        mRM = ar(16384, 3, N2)
        mN0 = ar(17152, 16, 40)
        mRAW = sq(0, 4, N2)
        mROW = sq(1024, 4, N2)
        mSC, mEM = sm(0, N2), sm(256, N2)
        mAC = sm(512, 2, 40)
        mQS = H[:, :, :].rearrange("p a b -> p (a b)").rearrange("p (d h t) -> p d h t", d=2, h=MH)
        mCO = sq(0, 2, 2, 2, T)
        mHQ = sq(0, 2, 2, N2)
        mWL = sm(592, 16)
        mNS = sm(608, 16)

        gQ, gK = ar(0, 8, T), ar(1024, 8, T)
        gV = ar(2048, 2, 1024)
        gR = ar(4096, 8, N2)
        gLA = ar(6144, 2, 8, T)
        gB = ar(8192, 2, 8, T)
        gAX = ar(10240, 2, 8, T)
        gKI = ar(10240, 2, 8, T)
        gT0, gT1 = ar(12288, 8, T), ar(6144, 8, T)
        gQE = ar(7168, 2, GH, T)
        gQI = ar(13312, 2, 8, T)
        gAT = ar(15360, 8, T)
        gOG = ar(10240, 8, N2)
        gSO = ar(13312, 8, 256)
        gKD = ar(8192, 8, T)
        WA1 = WGT[:, :, :, :].rearrange("p a b c -> p (a b c)")[:, 0:512].rearrange("p (k n) -> p k n", k=KD)
        WA2 = ar(16896, 512)[0:64]
        gU = sq(1024, N2)[0:64]
        gHQ = sq(0, 2, 2, N2)

        def serial(eng):
            count = {}

            def run(ins, sem):
                sem = STEP[sem][0] if sem in STEP else sem
                ins.then_inc(S(sem), 1)
                count[sem] = count.get(sem, 0) + 1
                eng.wait_ge(S(sem), count[sem])
            return run

        def wait(eng, sem, v):
            if not isinstance(v, int) or v > 0:
                eng.wait_ge(S(sem), v)

        def after(eng, name):
            eng.wait_ge(S(name), STEP[name][1])

        def landed(pe, n, i=0):
            pe.wait_ge(S(f"landed{n % RING}"), 16 * (n // RING + 1) + 16 * i)
            return slot_view(CHUNKS[n][0], n % RING)

        def slot_view(kind, slot):
            v = ring[:, slot].rearrange("p a b -> p (a b)")
            if kind in ("wd", ):
                return v.rearrange("p (k n) -> p k n", k=4)
            if kind == "c0":
                return v.rearrange("p (k n) -> p k n", k=32)
            if kind == "s0":
                return v[:, 0:2048].rearrange("p (k n) -> p k n", k=8)
            return ring[:, slot]

        def used(n):
            kind, l, c = CHUNKS[n]
            a = l // 3
            return {"mod": lambda: ("mod_rows", 12 * l + c + 1),
                    "qkv": lambda: ("a_kv", 2 * a + 2) if c == 2 else ("a_q", 8 * a + 4 * c + 4),
                    "wo": lambda: ("a_y", 8 * a + 4 * c + 4),
                    "min": lambda: [("l_qk", 4 * c + 4), ("l_v", 2 * c - 6), ("l_o", 4 * c - 28)][c // 4],
                    "c0": lambda: ("l_h", MH),
                    "mout": lambda: ("l_y", 4 * c[0] + 4) if c[1] else ("l_y0", c[0] + 1),
                    "gin": lambda: ("g_qk", 4 * c + 4) if c < 2 else ("g_v", 2 * c - 2) if c < 4 else ("g_r", 4 * c - 12),
                    "s0": lambda: ("g_o", GH),
                    "gout": lambda: ("g_y", 4 * c + 4),
                    "wg": lambda: ("up", 2 * (NPAIR * l + c // 2) + 1),
                    "wu": lambda: ("up", 2 * (NPAIR * l + c // 2) + 2),
                    "wd": lambda: ("down", NPAIR * l + c // 2 + 1)}[kind]()

        def src_of(kind, l, c):
            def cols(w, j, r=0):
                return w.rearrange("(k p) n -> p k n", p=P)[:, 8 * r:8 * r + 8, 512 * j:512 * j + 512]
            if kind == "mod":
                return cols(I["w_mod"][l], c)
            if kind == "qkv":
                return cols(I[f"attn{l}_w_qkv"], c)
            if kind == "wo":
                return cols(I[f"attn{l}_w_o"], c)
            if kind == "min":
                return cols(I["mlstm1_w_in"], c)
            if kind == "mout":
                return cols(I["mlstm1_w_out"], c[0], c[1])
            if kind == "gin":
                return cols(I["gla2_w_in"], c)
            if kind == "gout":
                return cols(I["gla2_w_out"], c)
            if kind == "c0":
                return I["state_mlstm_C_1"][0].rearrange("d h (j p) k -> p (d h j) k", p=P)
            if kind == "s0":
                return I["state_gla_S_2"][0].rearrange("d h k v -> k (d h) v")
            return expert_weights(kind, l, c)

        def expert_weights(kind, l, e):
            return I["moe_" + kind][l, bass.ds(e, 1)].rearrange("o (p k) n -> p (o k) n", p=P)

        def gla_block(i):
            d, j = i // NB, i % NB
            blk = j if d == 0 else NB - 1 - j
            return (0, blk, 0, GB * (blk + 1)) if d == 0 else (1, blk, GB * blk, T)

        block = ctx.enter_context(nc.Block())

        @block.sync
        def _(sp):
            def load(n):
                kind, l, c = CHUNKS[n]
                if n == 1:
                    sp.wait_ge(S("load_p"), 16 * 12)
                    sp.wait_ge(S("load_x"), 32)
                if n >= RING:
                    wait(sp, *used(n - RING))
                sp.dma_start(slot_view(kind, n % RING), src_of(kind, l, c)).then_inc(S(f"landed{n % RING}"), 16)

            n = 0
            for l in range(DEPTH):
                while n < POS["wg", l, 0]:
                    load(n)
                    n += 1
                for j in range(6):
                    load(n + j)
                sp.wait_ge(S("x"), KD * (2 * l + 2))
                sp.wait_ge(S("out"), (32, 80, 112, 144)[l])

                def weight(j, p, par, i):
                    kind = CHUNKS[n + j][0]
                    sem, count = used(n + j)
                    step = 2 if sem == "up" else 1
                    slot = (n + j) % RING
                    if j < 2:
                        sp.wait_ge(S(f"landed{slot}"), 16 * ((n + j) // RING + par) + 32 * i)
                        dst = EXTRA[j] if par else slot_view(kind, slot)
                    else:
                        sp.wait_ge(S(sem), count - step + step * par + 2 * step * i)
                        dst = slot_view(kind, slot)
                    sp.dma_start(dst, expert_weights(kind, l, 2 * p + j % 2)).then_inc(S(f"landed{slot}"), 16)

                for j in range(6):
                    weight(j, 1, 1, 0)
                with sp.Fori(1, NPAIR // 2) as i:
                    for par in range(2):
                        for j in range(6):
                            weight(j, 2 * i + par, par, i)
                n += 3 * NE
                sp.wait_ge(S("table"), l + 1)
                nx = sp.value_load(EXI[0:1, 16:17], min_val=0, max_val=8)
                before = sp.value_load(EXI[0:1, 17:18], min_val=1, max_val=64)
                with sp.If(nx > 0):
                    for j in range(3):
                        wait(sp, *used(n - 6 + 2 * j))
                    with sp.Fori(0, nx) as i:
                        e = sp.value_load(EXI[0:1, bass.ds(i, 1)], min_val=0, max_val=NE - 1)
                        sp.wait_ge(S("x_down"), before + i)
                        for j, w in enumerate(("wg", "wu", "wd")):
                            sp.dma_start(slot_view(w, (n - 6 + 2 * j) % RING), expert_weights(w, l, e)).then_inc(S(f"x_landed{j}"), 16)
                sp.wait_ge(S("x_down"), before + nx)
            sp.wait_ge(S("y_sb"), 4)
            sp.dma_start(O["y_prompt"][0], XR[:, 0]).then_inc(S("out"), 16)
            sp.dma_start(O["y_sample"][0], XR[:, 1]).then_inc(S("out"), 16)
            sp.wait_ge(S("out"), 16 * (4 + 3 + 2 + 2))
            for j in range(2):
                sp.wait_ge(S(f"out_C{j}"), 16 * MH)

        @block.gpsimd
        def _(pool):
            for t in (WGT[:], CS[:], BGT[:], M0[:]):
                pool.memset(t, 0.0).then_inc(S("pad"), 1)
            pool.wait_ge(S("pad"), 4)
            gates = I["mlstm1_w_in"].rearrange("(k p) n -> p k n", p=P)[:, :, 6144:6176]
            for d in range(2):
                for g in range(2):
                    at = 16 * d + 8 * g
                    pool.dma_start(WGT[:, :, g, 32 * d:32 * d + 8], gates[:, :, at:at + 8]).then_inc(S("load_g"), 16)
                    pool.dma_start(BGT[32 * d:32 * d + 8, g:g + 1],
                                   I["mlstm1_b_gates"][at:at + 8].rearrange("(h o) -> h o", o=1)).then_inc(S("load_g"), 16)
                pool.dma_start(M0[32 * d:32 * d + 8, 1:2], I["state_mlstm_m_1"][0, d].rearrange("(h o) -> h o", o=1)).then_inc(S("load_g"), 16)
            pool.dma_start(RW[:], I["router_w"].rearrange("(k p) n -> p k n", p=P)).then_inc(S("load_g"), 16)
            pool.wait_ge(S("x"), KD * 3)
            pool.memset(mN0, 0.0).then_inc(S("pad"), 1)
            pool.wait_ge(S("pad"), 5)
            for d in range(2):
                for h in range(MH):
                    r = 8 * d + h
                    pool.tensor_copy(mN0[:, r, 32 * d + h:32 * d + h + 1], prm("n0", 1, r)).then_inc(S("n0"), 1)
            pool.wait_ge(S("x"), KD * 4)
            pool.memset(WA1, 0.0).then_inc(S("pad"), 1)
            pool.wait_ge(S("pad"), 6)
            for d in range(2):
                pool.dma_start(WA1[:, :, 32 * d:32 * d + 16], I["gla2_w_a1"][d].rearrange("(k p) n -> p k n", p=P)).then_inc(S("load_a"), 16)
            pool.wait_ge(S("x"), KD * 5)
            pool.wait_ge(S("out"), 80)
            for d in range(2):
                pool.dma_start(WA2[32 * d:32 * d + 16, :], I["gla2_w_a2"][d]).then_inc(S("load_a2"), 16)

        @block.scalar
        def _(act):
            run = serial(act)
            A = nc.scalar.activation

            def load(dst, src, sem):
                act.dma_start(dst, src).then_inc(S(sem), 16)

            act.nop().then_inc(S("x_part"), 1)
            load(CN[:, :], I["consts"], "load_c")
            after(act, "zero_rows")
            for name, src, n in (("cc", I["c_ctx"], 8), ("cl", I["c"][0], 8), ("fin", I["final_g"], 8),
                                 ("mg", I["mlstm1_norm_g"], 16), ("gg", I["gla2_norm_g"], 8)):
                load(PT[PR[name]:PR[name] + n, 0], src.rearrange("(k p) -> k p", p=P), "load_p")
            load(PT[0:32, 0], I["norm1_g"].rearrange("l (k p) -> (l k) p", p=P), "load_p")
            load(PT[32:64, 0], I["norm2_g"].rearrange("l (k p) -> (l k) p", p=P), "load_p")
            load(PT[112:120, 0], I["gla2_b_a"].rearrange("d (k p) -> (d k) p", p=P), "load_p")
            bm = I["b_mod"].rearrange("l (k p) -> (l k) p", p=P)
            load(PT[:, 1], bm[0:128], "load_p")
            load(PT[0:64, 2], bm[128:192], "load_p")
            load(PT[64:112, 2], I["mlstm1_conv"].rearrange("l (k p) -> (l k) p", p=P), "load_p")
            load(PT[112:128, 2], I["state_mlstm_n_1"][0].rearrange("d h k -> (d h) k"), "load_p")
            load(XR[:, 0], I["x_prompt"][0], "load_x")
            load(XR[:, 1], I["x_sample"][0], "load_x")
            load(RB[:, :], I["router_b"].partition_broadcast(P), "load_b")
            for a, l in enumerate((0, 3)):
                load(SK[:, a], I[f"attn{l}_sink"].partition_broadcast(P), "load_b")
            after(act, "prm")
            act.wait_ge(S("pad"), 4)
            run(A(CS[:, :, 0], prm("cc", 8), ACT.Silu), "scalar")
            run(A(CS[:, :, 1], prm("cl", 8), ACT.Silu), "cs")

            def mod(l, c):
                act.wait_ge(S("mod_rows"), 12 * l + c + 1)
                run(A(MPW if l and c >= 8 else MP[l], bank(7), ACT.Copy), "mod_sb")

            eps1 = c_("eps")[0:1]

            def norm(n):
                run(A(sm(636, 1)[0:1], eps1, ACT.Sqrt), "scalar")
                for k in range(KD):
                    act.wait_ge(S("x"), KD * (n + 1) - KD + k + 1)
                    run(A(SQ[:, k], X[:, k], ACT.Square), "sq")
                act.wait_ge(S("sumsq"), n + 1)
                run(A(RS[:, 0], bank(7, 0, N2), ACT.Sqrt, bias=c_("eps"), scale=1.0 / D), "root")

            def affine(n, l, v):
                act.wait_ge(S("mod"), mod_count(l, 3 if v == 0 else 9) + 1)
                for k in range(KD):
                    act.wait_ge(S("xn"), KD * n + k + 1)
                    run(A(H[:, k, 0:T], H[:, k, 0:T], ACT.Identity, bias=mod_col(l, v, k, 0), scale=mod_col(l, v + 1, k, 0)), "h0")

            def attention(a, l):
                load(CK[:, :, 0], I[f"cache_k_{l}"][0], "load_ck")
                load(CK[:, :, 1], I[f"cache_k_{l}"][0], "load_ck")
                load(CV, I[f"cache_v_{l}"][0].rearrange("t h d -> t (h d)"), "load_ck")
                for m in range(2):
                    if l == 0:
                        mod(*UNITS[m])
                    act.wait_ge(S("a_k"), 2 * a + m + 1)
                    run(A(KR[:, m], bank(m, 0, N2), ACT.Copy), "a_k_sb")
                for m in range(2):
                    if l == 0:
                        mod(*UNITS[2 + m])
                    act.wait_ge(S("a_kv"), 2 * a + m + 1)
                    run(A(VL if m else KC, bank(3, 0, 256) if m else bank(2), ACT.Copy), "a_kv_sb")
                load(O[f"cache_k_{l}"][0].rearrange("t h d -> t (h d)"), KC[:, 0:256], "out")
                load(O[f"cache_v_{l}"][0].rearrange("t h d -> t (h d)"), KC[:, 256:512], "out")
                for m in range(8):
                    if l == 0:
                        mod(*UNITS[4 + m])
                    act.wait_ge(S("a_q"), 8 * a + m + 1)
                    run(A(QT[:, m], bank(m % 4, 0, N2), ACT.Copy), "a_q_sb")
                    if m == 2:
                        after(act, f"a_dup{l}")
                        kd = PS[:, 4:6].rearrange("p b (j n) -> p (b j) n", j=2)
                        run(A(KDUP[:, :, 0], kd[:, :, 0:T], ACT.Copy), "a_kd")
                        run(A(KDUP[:, :, 2], kd[:, :, T:N2], ACT.Copy), "a_kd")
                        run(A(KDUP[:, :, 1], bank(6).rearrange("p (j n) -> p j n", j=4), ACT.Copy), "a_kd")

                def probs(g):
                    n = 4 * a + g
                    act.wait_ge(S("a_neg"), n + 1)
                    wait(act, "a_pt", n)
                    for j in range(4):
                        run(A(PBUF[:, j, 0:T], bank(j, 0, T), ACT.Exp, bias=ANM[:, j, 0:1], scale=HD ** -0.5,
                              accum_out=ASUM[:, j, 0:1]), "a_exp")
                        run(A(PBUF[:, j, T:3 * T], bank(j, T, 3 * T), ACT.Exp, bias=ANM[:, j, 1:2], scale=HD ** -0.5,
                              accum_out=ASUM[:, j, 1:2]), "a_exp")
                    run(A(AES, ASD, ACT.Exp), "a_exp")
                    if l == 0:
                        mod(1, 4 + g)

                run(A(sm(636, 1)[0:1], eps1, ACT.Exp), "scalar")
                probs(0)
                for g in range(KV):
                    n = 4 * a + g
                    act.wait_ge(S("a_pt"), n + 1)
                    run(A(PTB[:, 2], bank(6).rearrange("p (j n) -> p j n", j=4), ACT.Copy), "a_ptA")
                    if g + 1 < KV and l:
                        probs(g + 1)
                    act.wait_ge(S("a_pv"), n + 1)
                    run(A(OT[:, 2 * g:2 * g + 2].rearrange("p m (s t) -> p s m t", s=2),
                          bank(7).rearrange("p (s m t) -> p s m t", s=2, m=2), ACT.Copy), "a_o")
                    if g + 1 < KV and not l:
                        probs(g + 1)

            def mlstm():
                E = mROW[0:40, 2]
                after(act, "l_abs")
                run(A(E, E, ACT.Exp, scale=-1.0), "l_ln")
                run(A(E, E, ACT.Ln, bias=1.0), "l_ln")

                def silu(m):
                    act.wait_ge(S("l_conv"), m + 1)
                    run(A(mQK[:, m], mQK[:, m], ACT.Silu), "l_qk_sb")

                for m in range(16):
                    if m % 4 == 0:
                        mod(2, m // 4)
                    act.wait_ge(S("l_qk"), m + 1)
                    wait(act, "l_conv", m - 3)
                    run(A(mRAW[:, m % 4], bank(m % 4, 0, N2), ACT.Copy), "l_raw")
                    if m >= 2:
                        silu(m - 2)
                for i in range(8):
                    if i % 2 == 0:
                        mod(2, 4 + i // 2)
                    act.wait_ge(S("l_v"), i + 1)
                    run(A(mV[:, i % 2, 512 * (i // 2):512 * (i // 2) + 512], bank(4 + i % 2), ACT.Copy), "l_v_sb")
                    if i < 2:
                        silu(14 + i)
                after(act, "l_ac")
                run(A(mSC[0:40], mRM[0:40, 2], ACT.Exp, scale=-1.0), "scalar")
                run(A(mEM[0:40], mRM[0:40, 1], ACT.Exp, scale=-1.0), "l_rowexp")
                for q in range(4):
                    d, hg = q // 2, q % 2
                    act.wait_ge(S("l_mb"), q + 1)
                    for j in range(4):
                        r = 32 * d + 4 * hg + j
                        for s in range(2):
                            src = bank(4 + 2 * (q % 2) + j // 2, N2 * (j % 2) + T * s, N2 * (j % 2) + T * s + T)
                            run(A(mW[:, s, d, 4 * hg + j], src, ACT.Exp, bias=mAC[:, s, r:r + 1], scale=-1.0), "l_w")
                    for m in range(4 * q, 4 * q + 4):
                        act.wait_ge(S("l_o"), m + 1)
                        run(A(mO[:, m], bank(m % 4, 0, N2), ACT.Sigmoid), "l_o_sb")
                c0 = slot_view("c0", POS["c0", 1, 0] % RING)
                for u in range(8):
                    act.wait_ge(S("l_c0t"), u + 1)
                    run(A(c0[:, 4 * u:4 * u + 4], bank(u % 4).rearrange("p (a b) -> p a b", a=4), ACT.Copy), "l_c0")
                for h in range(MH):
                    act.wait_ge(S("l_c"), h + 1)
                    wait(act, f"out_C{h % 2}", 32 * (h // 2))
                    run(A(mCO[:, h % 2], bank(5 + h % 2).rearrange("p (j d k) -> p j d k", j=2, d=2), ACT.Copy), "l_c_sb")
                    for d in range(2):
                        load(O["C"][0, d, h].rearrange("(j p) k -> p j k", p=P), mCO[:, h % 2, :, d], f"out_C{h % 2}")
                after(act, "l_n")
                run(A(mNS, bank(4, 0, 16), ACT.Copy), "l_n_sb")
                after(act, "l_nT")
                run(A(mROW[0:16, 2, 0:P], PS[0:16, 4, 128:256], ACT.Copy), "l_nT_sb")
                load(O["n"][0].rearrange("d h k -> (d h) k"), mROW[0:16, 2, 0:P], "out")
                for d in range(2):
                    t = T - 1 if d == 0 else 0
                    load(O["m"][0, d].rearrange("(h o) -> h o", o=1), mRM[32 * d:32 * d + 8, 1, t:t + 1], "out")
                for j in range(2):
                    act.wait_ge(S(f"out_C{j}"), 16 * MH)
                for h in range(MH):
                    act.wait_ge(S("l_h"), h + 1)
                    v = bank(h % 4).rearrange("p (j n) -> p j n", j=2)
                    run(A(mQK[:, 2 * h:2 * h + 2], v, ACT.Copy), "l_hs")
                    wait(act, "l_ss", h - 1)
                    run(A(mHQ[:, h % 2], v, ACT.Square), "l_hq")
                run(A(sm(636, 1)[0:1], eps1, ACT.Sqrt), "scalar")
                act.wait_ge(S("l_ss"), MH)
                run(A(mROW[0:8, 0], PS[0:8, 4, 0:N2], ACT.Sqrt, bias=c_("eps")[0:8], scale=1.0 / MDV), "l_root")

            def gla():
                after(act, "g_u")
                run(A(gU, PS[0:64, 4, 0:N2], ACT.Copy), "g_u_sb")

                def qk(m):
                    act.wait_ge(S("g_qk"), m + 1)
                    dst = (gQ if m < 4 else gK)[:, 2 * (m % 4):2 * (m % 4) + 2]
                    run(A(dst, bank(m % 4, 0, N2).rearrange("p (s t) -> p s t", s=2), ACT.Copy,
                          scale=GDK ** -0.5 if m < 4 else 1.0), "g_qk_sb")
                for m in range(8):
                    if m % 2 == 0:
                        mod(3, m // 2)
                    qk(m)
                for d in range(2):
                    act.wait_ge(S("g_abs"), d + 1)
                    run(A(gAX[:, d], gAX[:, d], ACT.Exp, scale=-1.0), "g_ln")
                    run(A(gAX[:, d], gAX[:, d], ACT.Ln, bias=1.0), "g_ln")
                for i in range(4):
                    mod(3, 4 + i)
                    act.wait_ge(S("g_v"), i + 1)
                    run(A(gV[:, i % 2, 512 * (i // 2):512 * (i // 2) + 512], bank(i), ACT.Copy), "g_v_sb")
                for d in range(2):
                    act.wait_ge(S("g_qd"), d + 1)
                    run(A(gQI[:, d], gQI[:, d], ACT.Exp, scale=1.0 / 16), "g_qe")
                for i in range(2 * NB):
                    d, blk, lo, hi = gla_block(i)
                    act.wait_ge(S("g_kd"), i + 1)
                    t = (gT0, gT1)[i % 2][:, :, lo:hi]
                    run(A(t, t, ACT.Exp, scale=1.0 / 16), "g_ke")
                    act.wait_ge(S("g_r"), i + 1)
                    run(A(gR[:, i], bank(4 + i % 2, 0, N2), ACT.Copy), "g_r_sb")
                    if i in (3, 4):
                        run(A(gQE[:, i - 3], gB[:, i - 3].rearrange("p (h s) t -> p h s t", s=2)[:, :, 1], ACT.Exp, scale=1.0 / 16), "g_qx")
                run(A(gR, gR, ACT.Silu), "g_gate")
                act.wait_ge(S("g_sd"), 2)
                run(A(gT0, gT0, ACT.Exp, scale=1.0 / 16), "g_se")
                for h in range(GH):
                    act.wait_ge(S("g_o"), h + 1)
                    v = bank(h).rearrange("p (j n) -> p j n", j=2)
                    run(A(gOG[:, 2 * h:2 * h + 2], v, ACT.Copy), "g_os")
                    wait(act, "g_ss", h - 1)
                    run(A(gHQ[:, h % 2], v, ACT.Square), "g_hq")
                run(A(sm(636, 1)[0:1], eps1, ACT.Sqrt), "scalar")
                act.wait_ge(S("g_ss"), GH)
                run(A(mROW[0:8, 1], PS[0:8, 6, 0:N2], ACT.Sqrt, bias=c_("eps")[0:8], scale=1.0 / GDV), "g_root")
                for i in range(4):
                    act.wait_ge(S("g_s"), i + 1)
                    run(A(gSO[:, 2 * i:2 * i + 2], bank(i).rearrange("p (a b) -> p a b", a=2), ACT.Copy), "g_s_sb")
                for d in range(2):
                    load(O["S"][0, d].rearrange("h k v -> k h v"), gSO[:, 4 * d:4 * d + 4], "out")

            def moe(l):
                act.wait_ge(S("logitT"), l + 1)
                run(A(RT[0:NE, 0:N2], PS[0:NE, 5, 0:N2], ACT.Copy), "logitT_sb")
                run(A(RT[0:1, 480:481], eps1, ACT.Sigmoid), "scalar")
                act.wait_ge(S("logit"), l + 1)
                run(A(RT[:, 256:288], bank(4, 0, 32), ACT.Sigmoid), "score")
                for b in range(4):
                    if l + 1 < DEPTH and b < 3:
                        mod(l + 1, 9 + b)
                    act.wait_ge(S("ht"), 4 * l + b + 1)
                    run(A(HT[:, b // 2, 512 * (b % 2):512 * (b % 2) + 512], bank(b), ACT.Copy), "ht_sb")

                def evac(dst, src, func, sem, value):
                    A(dst, src, func).then_inc(S(sem), 1)
                    act.wait_ge(S(sem), value)

                def gx_part(j):
                    return GX.rearrange("s (k q) -> s q k", k=KD)[:, 64 * j:64 * j + 64]

                def gathered(n, banks):
                    act.wait_ge(S("gather"), n + 1)
                    for j in range(2):
                        evac(gx_part(j), bank(banks[j]).rearrange("p (q k) -> p q k", k=KD), ACT.Copy, "gx", 2 * n + j + 1)

                def pair(n, par, more=True):
                    here, there = BANKS[par], BANKS[1 - par]
                    act.wait_ge(S("up"), 2 * n + 1)
                    evac(SG, bank(here[0]), ACT.Silu, "silu", n + 1)
                    if more:
                        gathered(n + 1, there)
                    act.wait_ge(S("down"), n + 1)
                    for j in range(2):
                        evac(YS[:, 512 * j:512 * j + 512], bank(here[j]), ACT.Copy, "ys", 2 * n + j + 1)

                n0 = NPAIR * l
                gathered(n0, BANKS[1])
                pair(n0, 0)
                pair(n0 + 1, 1)
                with act.Fori(1, NPAIR // 2 - 1) as i:
                    pair(2 * i + n0, 0)
                    pair(2 * i + (n0 + 1), 1)
                pair(n0 + 6, 0)
                pair(n0 + 7, 1, False)
                act.wait_ge(S("table"), l + 1)
                nx = act.value_load(EXI[0:1, 16:17], min_val=0, max_val=8)
                before = act.value_load(EXI[0:1, 17:18], min_val=1, max_val=64)
                with act.If(nx > 0):
                    with act.Fori(0, nx) as i:
                        act.wait_ge(S("x_gather"), before + i)
                        evac(gx_part(0)[0:64], PS[0:64, 6].rearrange("p (q k) -> p q k", k=KD), ACT.Copy, "x_part", 2 * before + 2 * i)
                        evac(gx_part(1)[0:64], PS[0:64, 7].rearrange("p (q k) -> p q k", k=KD), ACT.Copy, "x_gx", before + i)
                        act.wait_ge(S("x_up"), before + i)
                        evac(SG[0:64], PS[0:64, 4], ACT.Silu, "x_silu", before + i)
                        act.wait_ge(S("x_down"), before + i + 1)
                        evac(YS[0:64, 0:512], PS[0:64, 4], ACT.Copy, "x_part", 2 * before + 2 * i + 1)
                        evac(YS[0:64, 512:1024], PS[0:64, 5], ACT.Copy, "x_ys", before + i)

            for c in range(4):
                mod(0, c)
            for l in range(DEPTH):
                norm(2 * l)
                affine(2 * l, l, 0)
                (lambda: attention(l // 3, l), mlstm, gla)[l % 3]()
                act.wait_ge(S("out"), (32, 80, 112, 144)[l])
                norm(2 * l + 1)
                if l + 1 < DEPTH:
                    mod(l + 1, 8)
                affine(2 * l + 1, l, 3)
                moe(l)
            norm(2 * DEPTH)
            for k in range(KD):
                act.wait_ge(S("xn"), KD * 2 * DEPTH + k + 1)
                run(A(H[:, k], H[:, k], ACT.Copy, scale=prm("fin", 1, k)), "h0")
            for j in range(4):
                c, s = j // 2, j % 2
                act.wait_ge(S("yT"), j + 1)
                run(A(XR[:, s, 512 * c:512 * c + 512], bank(2 * s + c), ACT.Copy), "y_sb")

        @block.tensor
        def _(pe):
            mm, tp = pe.matmul, pe.transpose

            def group(out, pairs, sem=None, first=True, final=True, fill=None):
                pairs = list(pairs)
                for i, (a, b) in enumerate(pairs):
                    if fill and i == len(pairs) // 2:
                        mod_rows(*fill)
                    ins = mm(out, a, b, start=first and i == 0, stop=final and i == len(pairs) - 1)
                if sem:
                    ins.then_inc(S(sem), 1)
                if fill:
                    mod_cols(*fill)
                return ins

            def tile(w, m):
                return [w[:, k, P * m:P * m + P] for k in range(KD)]

            pe.wait_ge(S("load_c"), 16)
            pe.nop().then_inc(S("x_down"), 1)
            pe.nop().then_inc(S("x_scatter"), 1)
            pe.wait_ge(S("load_p"), 16 * 12)
            for j in range(3):
                ins = tp(bank(4, P * j, P * j + P), PT[:, j], ident)
            ins.then_inc(S("prmT"), 1)
            pe.wait_ge(S("load_x"), 32)
            for b in range(4):
                for k in (2 * b, 2 * b + 1):
                    for s in range(2):
                        ins = tp(bank(b, N2 * (k % 2) + T * s, N2 * (k % 2) + T * s + T), XR[:, s, P * k:P * k + P], ident)
                ins.then_inc(S("xT"), 1)
            after(pe, "cs")

            def mod_rows(l, c):
                w = landed(pe, POS["mod", l, c])
                if l or c:
                    before = (l, c - 1) if c else (l - 1, 11)
                    pe.wait_ge(S("mod"), mod_count(*before))
                for k in range(KD):
                    g = 32 * (k % 4)
                    ins = mm(PS[g:g + 32, 7, :], CS[:, k], w[:, k], start=(k < 4), stop=(k >= 4))
                ins.then_inc(S("mod_rows"), 1)

            def mod_cols(l, c):
                pe.wait_ge(S("mod_sb"), 12 * l + c + 1)
                rows = MPW if l and c >= 8 else MP[l]
                for j in range(4):
                    ins = mm(bank(7, 2 * j, 2 * j + 2), rows[:, P * j:P * j + P], c_("selm"), start=True, stop=True)
                ins.then_inc(S("mod_cols"), 1)

            def sumsq(n):
                pe.wait_ge(S("mod"), mod_count(0, 3) if n == 0 else mod_count((n + 1) // 2, 7) if n % 2 and n < 7 else mod_count(min(n // 2, 3), 11))
                for k in range(KD):
                    pe.wait_ge(S("sq"), KD * n + k + 1)
                    ins = mm(bank(7, 0, N2), ones, SQ[:, k], start=(k == 0), stop=(k == KD - 1))
                ins.then_inc(S("sumsq"), 1)

            def warm(n):
                for _ in range(n):
                    mm(bank(6, 0, N2), ident, c_("slot1"), start=True, stop=True)

            def h_ready(n, k=KD - 1):
                pe.wait_ge(S("h0"), KD * n + k + 1)
                pe.wait_ge(S("h1"), KD * n + k + 1)

            def attention(a, l):
                fill = UNITS if l == 0 else [None] * 12
                w = landed(pe, POS["qkv", l, 2])
                for m in range(2):
                    for k in range(KD):
                        if m == 0:
                            h_ready(2 * l, k)
                        if fill[m] and k == KD // 2:
                            mod_rows(*fill[m])
                        ins = mm(bank(m, 0, N2), w[:, k, P * m:P * m + P], H[:, k], start=(k == 0), stop=(k == KD - 1))
                    ins.then_inc(S("a_k"), 1)
                    if fill[m]:
                        mod_cols(*fill[m])
                group(bank(2), [(H[:, k, 0:T], w[:, k]) for k in range(KD)], "a_kv", fill=fill[2])
                group(bank(3, 0, 256), [(H[:, k, T:N2], w[:, k, 256:512]) for k in range(KD)], "a_kv", fill=fill[3])

                def rotate(b, tiles, name):
                    for j, src in enumerate(tiles):
                        ins = mm(bank(b, T * j, T * j + T), c_("rot"), src[:, T:N2], start=True, stop=True)
                    ins.then_inc(S(f"{name}{l}"), 1)

                for m in range(8):
                    if m % 4 == 0:
                        w = landed(pe, POS["qkv", l, m // 4])
                    pe.wait_ge(*((S("a_k_sb"), 2 * a + m + 1) if m < 2 else (S("a_kv_sb"), 2 * a + m - 1) if m < 4 else (S("a_q_sb"), 8 * a + m - 3)))
                    group(bank(m % 4, 0, N2), zip(tile(w, m % 4), [H[:, k] for k in range(KD)]), "a_q", fill=fill[4 + m])
                    if m == 0:
                        pe.wait_ge(S("a_k_sb"), 2 * a + 2)
                        rotate(6, [KR[:, j] for j in range(2)], "a_rotk")
                    if m == 1:
                        after(pe, f"a_ropek{l}")
                        pe.wait_ge(S("load_ck"), 48 * (a + 1))
                        for j in range(KV):
                            mm(bank(4 + j // 2, N2 * (j % 2), N2 * (j % 2) + N2), c_(f"dup{j % 2}"), KR[:, j // 2], start=True, stop=True)
                        for j in range(KV):
                            ins = tp(bank(6, T * j, T * j + T), CK[:, j].rearrange("p a b -> p (a b)"), ident)
                        ins.then_inc(S(f"a_dup{l}"), 1)
                    if m == 5:
                        pe.wait_ge(S("a_kd"), 3 * (a + 1))
                        pe.wait_ge(S("a_q_sb"), 8 * a + 4)
                        rotate(4, [QT[:, j] for j in range(4)], "a_rotA")
                pe.wait_ge(S("a_q_sb"), 8 * (a + 1))
                rotate(5, [QT[:, j] for j in range(4, 8)], "a_rotB")

                def scores(g):
                    if g % 2 == 0:
                        after(pe, f"a_rope{'AB'[g // 2]}{l}")
                    if g:
                        pe.wait_ge(S("a_exp"), 9 * (4 * a + g))
                    for j in range(4):
                        h = 4 * g + j
                        p0 = HD * (h % 2)
                        mm(bank(j, 0, T), QT[p0:p0 + HD, h // 2, 0:T], KDUP[p0:p0 + HD, g, 0], start=True, stop=True)
                        ins = mm(bank(j, T, 3 * T), QT[p0:p0 + HD, h // 2, T:N2], KDUP[p0:p0 + HD, g, 1:3].rearrange("p a b -> p (a b)"), start=True, stop=True)
                    ins.then_inc(S("a_s"), 1)

                scores(0)
                for g in range(KV):
                    n = 4 * a + g
                    if l == 0:
                        wait(pe, "a_o", n)
                        mod_rows(1, 4 + g)
                    if g + 1 < KV:
                        scores(g + 1)
                    if l == 0:
                        mod_cols(1, 4 + g)
                    pe.wait_ge(S("a_p"), n + 1)
                    wait(pe, "a_ptV", 2 * n)
                    wait(pe, "a_ptA", n)
                    for part in range(3):
                        for j in range(4):
                            ins = tp(bank(4 + part, T * j, T * j + T), PBUF[:, j, T * part:T * part + T], ident)
                    ins.then_inc(S("a_pt"), 1)
                    if l == 0:
                        pe.wait_ge(S("mod"), mod_count(1, 4 + g))
                    pe.wait_ge(S("a_ptV"), 2 * (n + 1))
                    pe.wait_ge(S("a_ptA"), n + 1)
                    wait(pe, "a_o", n)
                    cols = slice(HD * g, HD * g + HD)
                    for half in range(2):
                        p0 = HD * half
                        def probs(part):
                            return PTB[:, part].rearrange("p (m two) t -> p two m t", two=2)[:, half]
                        out = PS[p0:p0 + HD, 7].rearrange("p (s m t) -> p s m t", s=2, m=2)
                        mm(out[:, 0], KC[:, 256 + HD * g:256 + HD * g + HD], probs(0), start=True, stop=True)
                        mm(out[:, 1], CV[:, cols], probs(1), start=True, stop=False)
                        ins = mm(out[:, 1], VL[:, cols], probs(2), start=False, stop=True)
                    ins.then_inc(S("a_pv"), 1)
                pe.wait_ge(S("a_o"), 4 * (a + 1))
                out_proj("a_y", 8 * a, POS["wo", l, 0], OT, 2 * l)

            def out_proj(sem, base, n0, src, r):
                for c in range(2):
                    w = landed(pe, n0 + c)
                    for m in range(4 * c, 4 * c + 4):
                        if m >= 4:
                            pe.wait_ge(S("x"), KD * (r + 1) + m - 3)
                        group(bank(m % 4, 0, N2), zip(tile(w, m % 4), [src[:, k] for k in range(KD)]), sem)

            def mlstm():
                pe.wait_ge(S("load_g"), 16 * 11)
                for g in range(2):
                    for k in range(KD):
                        if g == 0:
                            h_ready(2, k)
                        ins = mm(PS[0:40, 7, N2 * g:N2 * g + N2], WGT[:, k, g], H[:, k], start=(k == 0), stop=(k == KD - 1))
                ins.then_inc(S("l_g"), 1)
                for c in range(4):
                    w = landed(pe, POS["min", 1, c])
                    for m in range(4 * c, 4 * c + 4):
                        wait(pe, "l_raw", m - 3)
                        if m == 0:
                            after(pe, "l_abs")
                        group(bank(m % 4, 0, N2), zip(tile(w, m % 4), [H[:, k] for k in range(KD)]), "l_qk", fill=(2, c) if m % 4 == 0 else None)
                for c in range(4):
                    w = landed(pe, POS["min", 1, 4 + c])
                    for s in range(2):
                        i = 2 * c + s
                        wait(pe, "l_v_sb", i - 1)
                        group(bank(4 + i % 2), [(H[:, k, T * s:T * s + T], w[:, k]) for k in range(KD)], "l_v", fill=(2, 4 + c) if s == 0 else None)
                after(pe, "l_rows")
                for s in range(2):
                    ins = tp(bank(6, 40 * s, 40 * s + 40), mROW[0:40, 0, T * s:T * s + T], ident[0:40, 0:40])
                ins.then_inc(S("l_at"), 1)
                def spread(out, r, rows, parts=40):
                    return mm(out, ident[0:parts, r:r + 1].broadcast_to([parts, P]), rows, start=True, stop=True)

                pe.wait_ge(S("l_raw"), 16)
                pe.wait_ge(S("l_v_sb"), 8)
                pe.wait_ge(S("mod"), mod_count(2, 7))
                after(pe, "l_ac")
                for q in range(4):
                    d, hg = q // 2, q % 2
                    wait(pe, "l_w", 8 * (q - 1))
                    for j in range(4):
                        b = 4 + 2 * (q % 2) + j // 2
                        ins = spread(bank(b, N2 * (j % 2), N2 * (j % 2) + N2), 32 * d + 4 * hg + j, mRM[0:40, 0])
                    ins.then_inc(S("l_mb"), 1)
                    w = landed(pe, POS["min", 1, 8 + q])
                    for m in range(4 * q, 4 * q + 4):
                        wait(pe, "l_o_sb", m - 3)
                        group(bank(m % 4, 0, N2), zip(tile(w, m % 4), [H[:, k] for k in range(KD)]), "l_o")
                pe.wait_ge(S("l_o_sb"), 16)
                pe.wait_ge(S("l_qk_sb"), 16)
                for s in range(2):
                    for hg in range(2):
                        for j in range(4):
                            h = 4 * hg + j
                            ins = mm(bank(2 * s + hg, T * j, T * j + T), mQK[:, 8 + h, T * s:T * s + T], mQK[:, h, T * s:T * s + T], start=True, stop=True)
                        ins.then_inc(S("l_st"), 1)
                pe.wait_ge(S("l_w"), 32)
                for h in range(MH):
                    ins = tp(bank(5 + h // 4, T * (h % 4), T * (h % 4) + T), mQK[:, 8 + h, 0:T], ident)
                ins.then_inc(S("l_kt"), 1)
                pe.wait_ge(S("l_at_w"), 8)
                pe.wait_ge(S("n0"), 16)
                for i in range(16):
                    d, h = i // 8, i % 8
                    r = 32 * d + h
                    mm(PS[0:40, 4, 0:N2], c_("win")[:, 40 - r:80 - r], mW[:, :, d, h], start=(i == 0), stop=(i == 15))
                for i in range(16):
                    d, h = i // 8, i % 8
                    ins = mm(PS[0:40, 4, N2:N2 + T], mN0[:, i], mQK[:, h, T:N2], start=(i == 0), stop=(i == 15))
                ins.then_inc(S("l_den"), 1)
                c0 = landed(pe, POS["c0", 1, 0])
                for u in range(8):
                    wait(pe, "l_c0", u - 3)
                    for j in range(4):
                        ins = tp(bank(u % 4, P * j, P * j + P), c0[:, 4 * u + j], ident)
                    ins.then_inc(S("l_c0t"), 1)
                pe.wait_ge(S("l_c0"), 8)
                after(pe, "l_rr")
                for i in range(16):
                    d, h = i // 8, i % 8
                    wait(pe, "l_sc", 2 * (i - 3))
                    spread(bank(i % 4, 0, 3 * T), 32 * d + h, mROW[0:40, 0:2].rearrange("p a b -> p (a b)")[:, 0:3 * T]).then_inc(S("l_rb"), 1)
                pe.wait_ge(S("l_kw"), 16)
                for h in range(MH):
                    wait(pe, "l_c_sb", h - 1)
                    for j in range(2):
                        at = MDV * h + P * j
                        ins = mm(bank(5 + h % 2, N2 * j, N2 * j + N2), mV[:, 0, at:at + P], mKW[:, h].rearrange("p a b -> p (a b)"), start=True, stop=True)
                    ins.then_inc(S("l_c"), 1)
                pe.wait_ge(S("l_c0"), 8)
                for d in range(2):
                    for h in range(MH):
                        ins = mm(bank(4, 8 * d + h, 8 * d + h + 1), mKW[:, h, d], ones[:, 0:1], start=True, stop=True)
                ins.then_inc(S("l_n"), 1)
                after(pe, "l_n_sb")
                tp(PS[0:16, 4, 128:256], mNS, ident).then_inc(S("l_nT"), 1)
                after(pe, "l_nT_sb")
                pe.wait_ge(S("l_sc"), 32)

                def sums(h):
                    pe.wait_ge(S("l_hq"), h + 1)
                    for j in range(2):
                        ins = mm(PS[0:8, 4, 0:N2], c_("win")[:, 40 - h:48 - h], mHQ[:, h % 2, j], start=(h == 0 and j == 0), stop=(h == MH - 1 and j == 1))
                    ins.then_inc(S("l_ss"), 1)

                for h in range(MH):
                    wait(pe, "l_hq", h - 3)
                    for j in range(2):
                        at = MDV * h + P * j
                        for s in range(2):
                            v = mV[:, s, at:at + P]
                            pairs = [(v, mW[:, s, 0, h]), (v, mW[:, s, 1, h])]
                            if s:
                                pairs += [(c0[:, 16 * d + 2 * h + j], mQS[:, d, h]) for d in range(2)]
                            ins = group(bank(h % 4, N2 * j + T * s, N2 * j + T * s + T), pairs)
                    ins.then_inc(S("l_h"), 1)
                    if h:
                        sums(h - 1)
                sums(MH - 1)
                after(pe, "l_rn")
                for h in range(MH):
                    ins = spread(bank((5, 6, 7, 4)[h // 2], N2 * (h % 2), N2 * (h % 2) + N2), h, mROW[0:8, 1], 8)
                ins.then_inc(S("l_rnb"), 1)
                for c in range(2):
                    for r in range(2):
                        w = landed(pe, POS["mout", 1, (c, r)])
                        for m in range(4):
                            if r == 0:
                                if c:
                                    pe.wait_ge(S("x"), KD * 3 + m + 1)
                                elif m == 0:
                                    pe.wait_ge(S("l_hn"), 4)
                            elif m == 0:
                                pe.wait_ge(S("l_hn"), 8)
                            ins = group(bank(m, 0, N2), zip(tile(w, m), [mQK[:, 8 * r + k] for k in range(KD)]), None, first=(r == 0), final=(r == 1))
                            if r:
                                ins.then_inc(S("l_y"), 1)
                            elif m == 3:
                                ins.then_inc(S("l_y0"), 1)

            def gla():
                pe.wait_ge(S("load_a"), 32)
                for k in range(KD):
                    h_ready(4, k)
                    ins = mm(PS[0:64, 4, 0:N2], WA1[:, k], H[:, k], start=(k == 0), stop=(k == KD - 1))
                ins.then_inc(S("g_u"), 1)

                def qk(c):
                    w = landed(pe, POS["gin", 2, c])
                    for m in range(4):
                        wait(pe, "g_qk_sb", 4 * c + m - 3)
                        group(bank(m, 0, N2), zip(tile(w, m), [H[:, k] for k in range(KD)]), "g_qk", fill=(3, 2 * c + m // 2) if m % 2 == 0 else None)

                def gates(lo, hi):
                    for n in range(lo, hi):
                        d, h = n // 4, n % 4
                        ins = mm(bank(4 + n // 2 % 3, N2 * (n % 2), N2 * (n % 2) + N2), WA2[32 * d:32 * d + 16, P * h:P * h + P], gU[32 * d:32 * d + 16], start=True, stop=True)
                        if h == 3:
                            ins.then_inc(S("g_z"), 1)

                qk(0)
                after(pe, "g_u_sb")
                pe.wait_ge(S("load_a2"), 32)
                gates(0, 6)
                qk(1)
                pe.wait_ge(S("g_abs"), 1)
                gates(6, 8)
                for i in range(4):
                    if i % 2 == 0:
                        w = landed(pe, POS["gin", 2, 2 + i // 2])
                    pe.wait_ge(S("g_qk_sb"), 5 + i)
                    s = i % 2
                    group(bank(i), [(H[:, k, T * s:T * s + T], w[:, k]) for k in range(KD)], "g_v", fill=(3, 4 + i))
                pe.wait_ge(S("g_abs"), 2)
                for i in range(2 * NB):
                    if i % 4 == 0:
                        w = landed(pe, POS["gin", 2, 4 + i // 4])
                    wait(pe, "g_r_sb", i - 1)
                    group(bank(4 + i % 2, 0, N2), zip(tile(w, i % 4), [H[:, k] for k in range(KD)]), "g_r")
                    d, blk, lo, hi = gla_block(i)
                    pe.wait_ge(S("g_v_sb"), 4)
                    pe.wait_ge(S("g_ki"), i + 1)
                    pe.wait_ge(S("g_qi"), d + 1)
                    for hs in range(8):
                        ins = mm(PS[GB * blk:GB * blk + GB, 2 * d + hs // 4, T * (hs % 4):T * (hs % 4) + T],
                                 gQI[:, d, hs, GB * blk:GB * blk + GB], gKI[:, i % 2, hs], start=True, stop=True)
                    ins.then_inc(S("g_a"), 1)
                pe.wait_ge(S("g_r_sb"), 8)
                pe.wait_ge(S("mod"), mod_count(3, 7))
                after(pe, "g_am")
                for hs in range(8):
                    ins = tp(bank(4 + hs // 4, T * (hs % 4), T * (hs % 4) + T), gT1[:, hs], ident)
                ins.then_inc(S("g_at"), 1)
                s0 = landed(pe, POS["s0", 2, 0])
                pe.wait_ge(S("g_at_sb"), 2)
                pe.wait_ge(S("g_qxm"), 2)

                def sums(h):
                    pe.wait_ge(S("g_hq"), h + 1)
                    for j in range(2):
                        ins = mm(PS[0:8, 6, 0:N2], c_("win")[:, 40 - h:48 - h], gHQ[:, h % 2, j], start=(h == 0 and j == 0), stop=(h == GH - 1 and j == 1))
                    ins.then_inc(S("g_ss"), 1)

                for h in range(GH):
                    for j in range(2):
                        at = GDV * h + P * j
                        for s in range(2):
                            pairs = [(gV[:, s, at:at + P], gAT[:, 2 * h + s])]
                            if s:
                                pairs += [(s0[:, 4 * d + h, P * j:P * j + P], gQE[:, d, h]) for d in range(2)]
                            ins = group(bank(h, N2 * j + T * s, N2 * j + T * s + T), pairs)
                    ins.then_inc(S("g_o"), 1)
                    if h:
                        sums(h - 1)
                sums(GH - 1)
                after(pe, "g_rn")
                for h in range(GH):
                    ins = mm(bank(4 + h // 2, N2 * (h % 2), N2 * (h % 2) + N2), ident[0:8, h:h + 1].broadcast_to([8, P]), mROW[0:8, 0], start=True, stop=True)
                ins.then_inc(S("g_rnb"), 1)
                after(pe, "g_sm")
                for u in range(2):
                    if u:
                        pe.wait_ge(S("g_kt_sb"), 1)
                    for j in range(4):
                        ins = tp(bank(7, P * j, P * j + P), gT0[:, 4 * u + j], ident)
                    ins.then_inc(S("g_kt"), 1)
                pe.wait_ge(S("g_kt_sb"), 2)
                for i in range(4):
                    pe.wait_ge(S("g_hq"), i + 1)
                    for j in range(2):
                        r = 2 * i + j
                        ins = mm(bank(i, N2 * j, N2 * j + N2), gKD[:, r], gV[:, 0, GDV * (r % 4):GDV * (r % 4) + GDV], start=True, stop=True)
                    ins.then_inc(S("g_s"), 1)
                pe.wait_ge(S("g_on"), 4)
                pe.wait_ge(S("g_s_sb"), 4)
                out_proj("g_y", 0, POS["gout", 2, 0], gOG, 4)

            def moe(l):
                n0 = POS["wg", l, 0]
                n = 2 * l + 1
                if l == 0:
                    pe.wait_ge(S("load_g"), 16 * 11)
                for k in range(KD):
                    h_ready(n, k)
                    ins = mm(PS[0:NE, 5, 0:N2], RW[:, k], H[:, k], start=(k == 0), stop=(k == KD - 1))
                ins.then_inc(S("logitT"), 1)
                for s in range(2):
                    for c in range(2):
                        for k in range(4 * c, 4 * c + 4):
                            ins = tp(bank(2 * s + c, P * (k % 4), P * (k % 4) + P), H[:, k, T * s:T * s + T], ident)
                        ins.then_inc(S("ht"), 1)
                pe.wait_ge(S("logitT_sb"), l + 1)
                for s in range(2):
                    ins = tp(bank(4, NE * s, NE * s + NE), RT[0:NE, T * s:T * s + T], ident[0:NE, 0:NE])
                ins.then_inc(S("logit"), 1)
                if l + 1 < DEPTH:
                    for c in range(9, 12):
                        mod_rows(l + 1, c)
                        mod_cols(l + 1, c)
                warm(WARM[3] if l + 1 < DEPTH else WARM[4])
                pe.wait_ge(S("routed"), l + 1)
                M = RT[:, 384:416].rearrange("p (s e) -> p s e", s=2)
                mm(bank(5, 0, NE), c_("lt"), M[:, 0], start=True, stop=True)
                mm(bank(5, NE, 2 * NE), c_("lt"), M[:, 1], start=True, stop=False)
                mm(bank(5, NE, 2 * NE), ones, M[:, 0], start=False, stop=True)
                mm(PS[0:1, 5, 32:48], ones[:, 0:1], M[:, 0], start=True, stop=False)
                mm(PS[0:1, 5, 32:48], ones[:, 0:1], M[:, 1], start=False, stop=True).then_inc(S("rank"), 1)
                pe.wait_ge(S("ht_sb"), 4 * (l + 1))

                def gather(banks, sem, rows=P):
                    for j in range(2):
                        for s in range(2):
                            ins = mm(PS[0:rows, banks[j], :], PB[:, s].rearrange("p e t -> p (e t)")[:, 0:rows], HT[:, s, 512 * j:512 * j + 512], start=(s == 0), stop=(s == 1))
                    ins.then_inc(S(sem), 1)

                def turn_w(b, sem, rows=P):
                    for s in range(2):
                        ins = tp(PS[0:rows, b, T * s:T * s + T], WB[:, s].rearrange("p e t -> p (e t)")[:, 0:rows], ident)
                    ins.then_inc(S(sem), 1)

                def turn_x(banks, sem):
                    for k in range(KD):
                        ins = tp(bank(banks[k // 4], P * (k % 4), P * (k % 4) + P), GX[:, P * k:P * k + P], ident)
                    ins.then_inc(S(sem), 1)

                def up(ws, b, sem):
                    for k in range(KD):
                        for e, w in enumerate(ws):
                            ins = mm(PS[64 * e:64 * e + 64, b, :], XG[:, k, 64 * e:64 * e + 64], w[:, k], start=(k == 0), stop=(k == KD - 1))
                    ins.then_inc(S(sem), 1)

                def turn_h(b, sem):
                    for f in range(4):
                        ins = tp(bank(b, P * f, P * f + P), HID[:, P * f:P * f + P], ident)
                    ins.then_inc(S(sem), 1)

                def down(ws, banks, sem):
                    for j in range(2):
                        for f in range(4):
                            for e, w in enumerate(ws):
                                ins = mm(PS[64 * e:64 * e + 64, banks[j], :], HTS[:, f, 64 * e:64 * e + 64], w[:, f, 512 * j:512 * j + 512], start=(f == 0), stop=(f == 3))
                    ins.then_inc(S(sem), 1)

                def scatter(par, sem, first=False, rows=P):
                    for t in range(8):
                        ins = mm(bank(t // 2, N2 * (t % 2), N2 * (t % 2) + N2), YS[0:rows, P * t:P * t + P], WTS[0:rows, par],
                                 start=first and t % 2 == 0, stop=True, skip_group_check=True)
                    ins.then_inc(S(sem), 1)

                def pair(n, par, i, first=False, more=True):
                    here, there = BANKS[par], BANKS[1 - par]
                    pe.wait_ge(S("xg"), 2 * n + 2)
                    for g in range(2):
                        ws = [landed(pe, n0 + 2 * g + e, i) for e in range(2)]
                        up(EXTRA if g == 0 and par else ws, here[g], "up")
                    if not first:
                        pe.wait_ge(S("ys"), 2 * n)
                        scatter(1 - par, "scatter", first=(isinstance(i, int) and i == 1))
                    if more:
                        pe.wait_ge(S("pw"), 8 * n + 16)
                        gather(there, "gather")
                    pe.wait_ge(S("hid"), n + 1)
                    turn_h(here[0], "turn_h")
                    if more:
                        turn_w(here[1], "turn_w")
                        pe.wait_ge(S("gx"), 2 * n + 4)
                        turn_x(there, "turn_x")
                    pe.wait_ge(S("hts"), n + 1)
                    if more:
                        pe.wait_ge(S("wts"), n + 2)
                    down([landed(pe, n0 + 4 + e, i) for e in range(2)], here, "down")

                q0 = NPAIR * l
                if l + 1 < DEPTH:
                    pe.wait_ge(S("mod"), mod_count(l + 1, 11))
                warm(WARM[5])
                pe.wait_ge(S("pw"), 8 * q0 + 4)
                gather(BANKS[1], "gather")
                pe.wait_ge(S("pw"), 8 * (q0 + 1))
                turn_w(BANKS[0][0], "turn_w")
                pe.wait_ge(S("gx"), 2 * q0 + 2)
                turn_x(BANKS[1], "turn_x")
                pe.wait_ge(S("wts"), q0 + 1)
                pair(q0, 0, 0, first=True)
                pair(q0 + 1, 1, 1)
                with pe.Fori(1, NPAIR // 2 - 1) as i:
                    pair(2 * i + q0, 0, 2 * i)
                    pair(2 * i + (q0 + 1), 1, 2 * i + 1)
                pair(q0 + 6, 0, 6)
                pair(q0 + 7, 1, 7, more=False)
                pe.wait_ge(S("ys"), 2 * (q0 + 8))
                scatter(1, "scatter")
                pe.wait_ge(S("table"), l + 1)
                nx = pe.value_load(EXI[0:1, 16:17], min_val=0, max_val=8)
                before = pe.value_load(EXI[0:1, 17:18], min_val=1, max_val=64)
                with pe.If(nx > 0):
                    with pe.Fori(0, nx) as i:
                        pe.wait_ge(S("x_pw"), before + i)
                        gather((6, 7), "x_gather", 64)
                        turn_w(5, "x_turn_w", 64)
                        pe.wait_ge(S("x_gx"), before + i)
                        turn_x((6, 7), "x_turn_x")
                        pe.wait_ge(S("x_xg"), before + i)
                        pe.wait_ge(S("x_wts"), before + i)
                        for j in range(2):
                            pe.wait_ge(S(f"x_landed{j}"), 16 * before + 16 * i)
                            up([slot_view("wg", (n0 + 42 + 2 * j) % RING)], 4 + j, ("x_up", "x_up2")[j])
                        pe.wait_ge(S("x_hid"), before + i)
                        turn_h(6, "x_turn_h")
                        pe.wait_ge(S("x_hts"), before + i)
                        pe.wait_ge(S("x_landed2"), 16 * before + 16 * i)
                        down([slot_view("wd", (n0 + 46) % RING)], (4, 5), "x_down")
                        pe.wait_ge(S("x_ys"), before + i)
                        scatter(0, "x_scatter", rows=64)

            for c in range(4):
                if c == 0:
                    pe.wait_ge(S("x"), 8)
                mod_rows(0, c)
                mod_cols(0, c)
            for l in range(DEPTH):
                sumsq(2 * l)
                warm(WARM[0])
                (lambda: attention(l // 3, l), mlstm, gla)[l % 3]()
                sumsq(2 * l + 1)
                if l + 1 < DEPTH:
                    pe.wait_ge(S("root"), 2 * l + 2)
                    mod_rows(l + 1, 8)
                    mod_cols(l + 1, 8)
                    warm(WARM[1])
                else:
                    warm(WARM[2])
                pe.wait_ge(S("x"), KD * (2 * l + 2))
                moe(l)
            sumsq(2 * DEPTH)
            for c in range(2):
                pe.wait_ge(S("h0"), KD * 2 * DEPTH + 4 * c + 4)
                for s in range(2):
                    for k in range(4 * c, 4 * c + 4):
                        ins = tp(bank(2 * s + c, P * (k % 4), P * (k % 4) + P), H[:, k, T * s:T * s + T], ident)
                    ins.then_inc(S("yT"), 1)

        @block.vector
        def _(v):
            run = serial(v)
            tt, ts, stt = v.tensor_tensor, v.tensor_scalar, v.scalar_tensor_tensor

            run(v.memset(PT, 0.0), "zero_rows")
            v.nop().then_inc(S("x_p"), 3)
            after(v, "prmT")
            run(v.tensor_copy(PRM[:, :], bank(4, 0, NPR)), "prm")
            for b in range(4):
                v.wait_ge(S("xT"), b + 1)
                for k in (2 * b, 2 * b + 1):
                    run(v.tensor_copy(X[:, k], bank(b, N2 * (k % 2), N2 * (k % 2) + N2)), "x")
            v.wait_ge(S("load_b"), 48)

            def mod(l, c):
                v.wait_ge(S("mod_cols"), 12 * l + c + 1)
                m = MC[:, l % 2].rearrange("p (j s) -> p j s", s=2)
                run(tt(m[:, 4 * c:4 * c + 4], bank(7, 0, 8).rearrange("p (j s) -> p j s", s=2), last(prm("bm", 4, 48 * l + 4 * c), 2), ALU.add), "mod")
                if c in (3, 9):
                    vec, g = (1, "n1") if c == 3 else (4, "n2")
                    mv = m[:, 8 * vec:8 * vec + 8]
                    run(stt(mv, mv, 1.0, last(prm(g, 8, 8 * l), 2), ALU.add, ALU.mult), "mod")

            def norm(n, l=None, vec=None):
                v.wait_ge(S("x"), KD * (n + 1))
                v.wait_ge(S("root"), n + 1)
                run(v.reciprocal(RS[:, 1], RS[:, 0]), "dve")

                def xn(k):
                    tt(H[:, k], X[:, k], RS[:, 1], ALU.mult).then_inc(S("xn"), 1)

                xn(0)
                for k in range(KD):
                    if k + 1 < KD:
                        xn(k + 1)
                    if l is not None:
                        v.wait_ge(S("xn"), KD * n + k + 1)
                        ts(H[:, k, T:N2], H[:, k, T:N2], mod_col(l, vec + 1, k, 1), mod_col(l, vec, k, 1), ALU.mult, ALU.add).then_inc(S("h1"), 1)

            def residual(sem, base, l, vec, src):
                for m in range(KD):
                    if sem:
                        v.wait_ge(S(sem), base + m + 1)
                    y = src(m)
                    stt(X[:, m, 0:T], y[:, 0:T], mod_col(l, vec, m, 0), X[:, m, 0:T], ALU.mult, ALU.add)
                    stt(X[:, m, T:N2], y[:, T:N2], mod_col(l, vec, m, 1), X[:, m, T:N2], ALU.mult, ALU.add).then_inc(S("x"), 1)

            def attention(a, l):
                def rope(dst, b, tmp, name):
                    n = dst.shape[1]
                    after(v, f"a_rot{name}{l}")
                    run(tt(tmp, bank(b, 0, T * n).rearrange("p (m t) -> p m t", m=n), mid(c_("sin"), n), ALU.mult), "dve")
                    run(tt(dst, dst, mid(c_("cos"), n), ALU.mult), "dve")
                    run(tt(dst, dst, tmp, ALU.add), f"a_rope{name}{l}")

                def mods(lo, hi):
                    if l == 0:
                        for u in UNITS[lo:hi]:
                            mod(*u)

                mods(0, 5)
                rope(KR[:, :, T:N2], 6, RTMP[:, 8:10], "k")
                mods(5, 10)
                rope(QT[:, 0:4, T:N2], 4, RTMP[:, 0:4], "A")
                mods(10, 12)
                rope(QT[:, 4:8, T:N2], 5, RTMP[:, 4:8], "B")
                sink = SK[:, a]

                def maxima(g):
                    v.wait_ge(S("a_s"), 4 * a + g + 1)
                    run(v.tensor_reduce(AMX.rearrange("p a b -> p (a b)"), PS[:, 0:4, 0:3 * T].rearrange("p j (c t) -> p j c t", c=3), AX.X, ALU.max), "dve")
                    run(tt(AMX[:, :, 1:2], AMX[:, :, 1:2], AMX[:, :, 2:3], ALU.max), "dve")
                    run(stt(AM2, AMX[:, :, 0:2], HD ** -0.5, last(sink[:, 4 * g:4 * g + 4], 2), ALU.mult, ALU.max), "dve")
                    run(tt(ASD, last(sink[:, 4 * g:4 * g + 4], 2), AM2, ALU.subtract), "dve")
                    run(ts(ANM, AM2, -1.0, None, ALU.mult), "a_neg")

                maxima(0)
                for g in range(KV):
                    n = 4 * a + g
                    v.wait_ge(S("a_exp"), 9 * (n + 1))
                    run(tt(AR_, ASUM, AES, ALU.add), "dve")
                    run(v.reciprocal(AR_, AR_), "dve")
                    run(tt(PBUF[:, :, 0:T], PBUF[:, :, 0:T], AR_[:, :, 0:1].broadcast_to([P, 4, T]), ALU.mult), "dve")
                    run(tt(PBUF[:, :, T:3 * T], PBUF[:, :, T:3 * T], AR_[:, :, 1:2].broadcast_to([P, 4, 2 * T]), ALU.mult), "a_p")
                    if l == 0:
                        mod(1, 4 + g)
                    if g + 1 < KV:
                        maxima(g + 1)
                    v.wait_ge(S("a_pt"), n + 1)
                    wait(v, "a_pv", n)
                    for part in range(2):
                        run(v.tensor_copy(PTB[:, part], bank(4 + part).rearrange("p (j t) -> p j t", j=4)), "a_ptV")
                residual("a_y", 8 * a, l, 2, lambda m: bank(m % 4, 0, N2))

            def mlstm():
                R = [mROW[0:40, j] for j in range(4)]
                gi, gf, e, b = R
                after(v, "l_g")
                v.wait_ge(S("load_g"), 16 * 11)
                run(ts(gi, PS[0:40, 7, 0:N2], BGT[:, 0:1], None, ALU.add), "dve")
                run(ts(gf, PS[0:40, 7, N2:512], BGT[:, 1:2], None, ALU.add), "dve")
                run(stt(e, gf, -1.0, gf, ALU.mult, ALU.max), "l_abs")
                v.wait_ge(S("l_ln"), 2)
                run(stt(gf, gf, 0.0, e, ALU.min, ALU.subtract), "dve")
                run(v.memset(b, 0.0), "dve")
                run(v.memset(mRM[0:40], 0.0), "dve")
                def both(dst, src, init, op1, ones_=ones):
                    for d in range(2):
                        for s in range(2):
                            rows = slice(32 * d, 32 * d + 8)
                            o = dst[rows, T * s:T * s + T]
                            i = src[rows, T * s:T * s + T]
                            if d:
                                o, i = o[:, ::-1], i[:, ::-1]
                            run(v.tensor_tensor_scan(o, ones[rows], i, 0.0 if init is None else init[rows, s:s + 1], ALU.mult, op1), "dve")
                both(b, gf, None, ALU.add)
                run(tt(gi, gi, b, ALU.subtract), "dve")
                both(mRM[:, 0], gi, M0, ALU.max)
                run(tt(mRM[0:40, 1], mRM[0:40, 0], b, ALU.add), "dve")
                for s in range(2):
                    run(ts(mRM[0:40, 2, T * s:T * s + T], mRM[0:40, 0, T * s:T * s + T], M0[:, s:s + 1], None, ALU.subtract), "dve" if s == 0 else "l_rows")
                for m in range(16):
                    if m % 4 == 0:
                        mod(2, m // 4)
                    v.wait_ge(S("l_raw"), m + 1)
                    x3 = mRAW[:, m % 4].rearrange("p (s t) -> p s t", s=2)
                    y3 = mQK[:, m].rearrange("p (s t) -> p s t", s=2)
                    w = [prm("conv", 1, 16 * j + m) for j in range(3)]
                    run(ts(y3, x3, w[1], None, ALU.mult), "dve")
                    run(stt(y3[:, :, 1:T], x3[:, :, 0:T - 1], w[0], y3[:, :, 1:T], ALU.mult, ALU.add), "dve")
                    run(stt(y3[:, :, 0:T - 1], x3[:, :, 1:T], w[2], y3[:, :, 0:T - 1], ALU.mult, ALU.add), "l_conv")
                for c in range(4, 8):
                    mod(2, c)
                after(v, "l_at")
                run(v.tensor_copy(mAC, bank(6, 0, 80).rearrange("p (s r) -> p s r", s=2)), "l_ac")
                for q in range(4):
                    d, hg = q // 2, q % 2
                    v.wait_ge(S("l_w"), 8 * (q + 1))
                    for s in range(2):
                        w = mW[:, s, d, 4 * hg:4 * hg + 4]
                        run(stt(w, w, 1.0, mid(c_(("le", "ge")[d]), 4), ALU.min, ALU.mult), "dve")
                for d in range(2):
                    t = T - 1 if d == 0 else 0
                    run(v.tensor_copy(mWL[:, 8 * d:8 * d + 8], mW[:, 0, d, :, t]), "dve")
                for s in range(2):
                    for hg in range(2):
                        v.wait_ge(S("l_st"), 2 * s + hg + 1)
                        for d in range(2):
                            w = mW[:, s, d, 4 * hg:4 * hg + 4]
                            run(stt(w, bank(2 * s + hg).rearrange("p (j t) -> p j t", j=4), MDK ** -0.5, w, ALU.mult, ALU.mult), "l_at_w")
                after(v, "l_kt")
                for d in range(2):
                    for h in range(MH):
                        run(ts(mKW[:, h, d], bank(5 + h // 4, T * (h % 4), T * (h % 4) + T), mWL[:, 8 * d + h:8 * d + h + 1], MDK ** -0.5, ALU.mult, ALU.mult), "l_kw")
                after(v, "l_den")
                after(v, "l_rowexp")
                run(v.tensor_copy(e, PS[0:40, 4, 0:N2]), "dve")
                run(tt(b[:, 0:T], PS[0:40, 4, N2:N2 + T], mSC[0:40, T:N2], ALU.mult), "dve")
                run(tt(e[:, T:N2], e[:, T:N2], b[:, 0:T], ALU.add), "dve")
                run(stt(b, e, -1.0, e, ALU.mult, ALU.max), "dve")
                run(tt(b, b, mEM[0:40], ALU.max), "dve")
                run(v.reciprocal(gi, b), "dve")
                run(tt(gf[:, 0:T], gi[:, T:N2], mSC[0:40, T:N2], ALU.mult), "l_rr")
                for i in range(16):
                    d, h = i // 8, i % 8
                    v.wait_ge(S("l_rb"), i + 1)
                    w = mW[:, :, d, h]
                    run(tt(w, w, bank(i % 4, 0, N2).rearrange("p (s t) -> p s t", s=2), ALU.mult), "l_sc")
                    run(tt(mQS[:, d, h], mQK[:, h, T:N2], bank(i % 4, N2, 3 * T), ALU.mult), "l_sc")
                for m in range(16):
                    v.wait_ge(S("l_hs"), m // 2 + 1)
                    run(stt(mQK[:, m], mQK[:, m], prm("mg", 1, m), mO[:, m], ALU.mult, ALU.mult), "dve")
                after(v, "l_root")
                run(v.reciprocal(mROW[0:8, 1], mROW[0:8, 0]), "l_rn")
                after(v, "l_rnb")
                for h in range(MH):
                    hb = bank((5, 6, 7, 4)[h // 2], N2 * (h % 2), N2 * (h % 2) + N2)
                    run(tt(mQK[:, 2 * h:2 * h + 2], mQK[:, 2 * h:2 * h + 2], mid(hb, 2), ALU.mult), "l_hn")
                residual("l_y", 0, 1, 2, lambda m: bank(m % 4, 0, N2))

            def gla():
                for d in range(2):
                    for c in range(2 * d, 2 * d + 2):
                        mod(3, c)
                    v.wait_ge(S("g_z"), d + 1)
                    for h in range(GH):
                        run(ts(gLA[:, d, 2 * h:2 * h + 2], bank(4 + (4 * d + h) // 2 % 3, N2 * (h % 2), N2 * (h % 2) + N2).rearrange("p (s t) -> p s t", s=2),
                               prm("ba", 1, 4 * d + h), None, ALU.add), "dve")
                    run(stt(gAX[:, d], gLA[:, d], -1.0, gLA[:, d], ALU.mult, ALU.max), "g_abs")
                for d in range(2):
                    v.wait_ge(S("g_ln"), 2 * d + 2)
                    run(stt(gLA[:, d], gLA[:, d], 0.0, gAX[:, d], ALU.min, ALU.subtract), "dve")
                    for hs in range(8):
                        o, i = gB[:, d, hs], gLA[:, d, hs]
                        if d:
                            o, i = o[:, ::-1], i[:, ::-1]
                        run(v.tensor_tensor_scan(o, ones, i, 0.0, ALU.mult, ALU.add), "dve")
                    mod(3, 4 + d)
                run(v.memset(gKI, 0.0), "dve")
                for d in range(2):
                    b32 = gB[:, d].rearrange("p a (i t) -> p (a i) t", t=GB)
                    run(tt(gQI[:, d].rearrange("p a (i t) -> p (a i) t", t=GB), b32, b32[:, :, GB // 2:GB // 2 + 1].broadcast_to([P, 8 * NB, GB]), ALU.subtract), "g_qd")

                def diff(i):
                    d, blk, lo, hi = gla_block(i)
                    ref = gB[:, d, :, GB * blk + GB // 2:GB * blk + GB // 2 + 1].broadcast_to([P, 8, hi - lo])
                    run(tt((gT0, gT1)[i % 2][:, :, lo:hi], ref, gB[:, d, :, lo:hi], ALU.subtract), "g_kd")

                mod(3, 6)
                diff(0)
                mod(3, 7)
                v.wait_ge(S("g_qk_sb"), 8)
                for d in range(2):
                    v.wait_ge(S("g_qe"), d + 1)
                    run(tt(gQI[:, d], gQI[:, d], gQ, ALU.mult), "g_qi")
                for i in range(2 * NB):
                    if i + 1 < 2 * NB:
                        diff(i + 1)
                    d, blk, lo, hi = gla_block(i)
                    wait(v, "g_a", NB if i == NB else i - 1)
                    if i == NB:
                        run(v.memset(gKI, 0.0), "dve")
                    v.wait_ge(S("g_ke"), i + 1)
                    run(tt(gKI[:, i % 2, :, lo:hi], (gT0, gT1)[i % 2][:, :, lo:hi], gK[:, :, lo:hi], ALU.mult), "g_ki")
                    if i in (5, 6):
                        v.wait_ge(S("g_qx"), i - 4)
                        q1 = gQ.rearrange("p (h s) t -> p h s t", s=2)[:, :, 1]
                        run(tt(gQE[:, i - 5], gQE[:, i - 5], q1, ALU.mult), "g_qxm")
                v.wait_ge(S("g_a"), 2 * NB)
                for d, mask in ((0, "ge"), (1, "le")):
                    for c in range(2):
                        run(tt((gT1, gKI[:, 0])[d][:, 4 * c:4 * c + 4], bank(2 * d + c).rearrange("p (j t) -> p j t", j=4), mid(c_(mask), 4), ALU.mult), "dve")
                run(tt(gT1, gT1, gKI[:, 0], ALU.add), "g_am")
                after(v, "g_at")
                for c in range(2):
                    run(v.tensor_copy(gAT[:, 4 * c:4 * c + 4], bank(4 + c).rearrange("p (j t) -> p j t", j=4)), "g_at_sb")
                kc = gK.rearrange("p (h s) t -> p h s t", s=2)[:, :, 0]
                for d in range(2):
                    bcx = gB[:, d].rearrange("p (h s) t -> p h s t", s=2)[:, :, 0]
                    t = T - 1 if d == 0 else 0
                    run(tt(gT0[:, 4 * d:4 * d + 4], bcx[:, :, t:t + 1].broadcast_to([P, 4, T]), bcx, ALU.subtract), "g_sd")
                after(v, "g_se")
                for d in range(2):
                    run(tt(gT0[:, 4 * d:4 * d + 4], gT0[:, 4 * d:4 * d + 4], kc, ALU.mult), "dve" if d == 0 else "g_sm")
                after(v, "g_gate")
                for m in range(8):
                    v.wait_ge(S("g_os"), m // 2 + 1)
                    run(stt(gOG[:, m], gOG[:, m], prm("gg", 1, m), gR[:, m], ALU.mult, ALU.mult), "dve")
                after(v, "g_root")
                run(v.reciprocal(mROW[0:8, 0], mROW[0:8, 1]), "g_rn")
                after(v, "g_rnb")
                for h in range(GH):
                    hb = bank(4 + h // 2, N2 * (h % 2), N2 * (h % 2) + N2)
                    run(tt(gOG[:, 2 * h:2 * h + 2], gOG[:, 2 * h:2 * h + 2], mid(hb, 2), ALU.mult), "g_on")
                for u in range(2):
                    v.wait_ge(S("g_kt"), u + 1)
                    run(v.tensor_copy(gKD[:, 4 * u:4 * u + 4], bank(7).rearrange("p (j t) -> p j t", j=4)), "g_kt_sb")
                residual("g_y", 0, 2, 2, lambda m: bank(m % 4, 0, N2))

            def moe(l):
                def two(at, n=NE):
                    return RT[:, at:at + 2 * n].rearrange("p (s e) -> p s e", s=2)

                def flat(at, n):
                    return RT[:, at:at + n]

                def go(ins, sem="dve"):
                    run(ins, sem)

                sc, sel, M, cmb, rk = two(256), two(288), two(384), two(416), two(448)
                v.wait_ge(S("score"), l + 1)
                go(tt(sel, sc, mid(RB[:, :], 2), ALU.add))
                s4 = RT[:, 288:320].rearrange("p (g a b) -> p g a b", a=2, b=2)
                pr = RT[:, 512:528].rearrange("p (g a) -> p g a", a=2)
                lo = RT[:, 528:544].rearrange("p (g a) -> p g a", a=2)
                go(tt(pr, s4[:, :, :, 0], s4[:, :, :, 1], ALU.max))
                go(tt(lo, s4[:, :, :, 0], s4[:, :, :, 1], ALU.min))
                t1, t2, t3 = flat(544, 8), flat(552, 8), flat(560, 8)
                go(tt(t1, pr[:, :, 0], pr[:, :, 1], ALU.max))
                go(tt(t2, pr[:, :, 0], pr[:, :, 1], ALU.min))
                go(tt(t3, lo[:, :, 0], lo[:, :, 1], ALU.max))
                go(tt(t2, t2, t3, ALU.max))
                go(tt(t1, t1, t2, ALU.add))

                if l + 1 < DEPTH:
                    mod(l + 1, 9)

                def best(src, prio, n, out, s0):
                    mx, eq = flat(s0, 2), flat(s0 + 8, 2 * n).rearrange("p (s e) -> p s e", s=2)
                    go(v.tensor_reduce(mx, src, AX.X, ALU.max))
                    go(tt(eq, src, last(mx, n), ALU.is_equal))
                    go(tt(eq, eq, prio.rearrange("p (s e) -> p s e", s=2), ALU.mult))
                    go(v.tensor_reduce(mx, eq, AX.X, ALU.max))
                    go(tt(out, eq, last(mx, n), ALU.is_equal))

                gm = flat(572, 8).rearrange("p (s g) -> p s g", s=2)
                best(t1.rearrange("p (s g) -> p s g", s=2), c_("gprio"), NG, gm, 600)
                big = flat(584, 8)
                go(ts(big, flat(572, 8), 1.0, 1e30, ALU.subtract, ALU.mult))
                sg = RT[:, 288:320].rearrange("p (g e) -> p g e", e=EPG)
                go(tt(sg, sg, last(flat(572, 8), EPG), ALU.mult))
                go(tt(sg, sg, last(big, EPG), ALU.add))
                oh1, oh2 = two(640), two(672)
                best(sel, c_("prio"), NE, oh1, 720)
                if l + 1 < DEPTH:
                    mod(l + 1, 10)
                go(stt(sel, oh1, -2e30, sel, ALU.mult, ALU.add))
                best(sel, c_("prio"), NE, oh2, 720)
                go(tt(M, oh1, oh2, ALU.add), "routed")
                if l + 1 < DEPTH:
                    mod(l + 1, 11)
                go(tt(cmb, M, sc, ALU.mult))
                ws = flat(800, 2)
                go(v.tensor_reduce(ws, cmb, AX.X, ALU.add))
                go(v.reciprocal(ws, ws))
                go(tt(cmb, cmb, last(ws, NE), ALU.mult))
                v.wait_ge(S("rank"), l + 1)
                go(stt(rk, bank(5, 0, 2 * NE).rearrange("p (s e) -> p s e", s=2), 1.0, M, ALU.add, ALU.mult))
                cnt = RT[0:1, 804:820]
                go(v.tensor_copy(cnt, PS[0:1, 5, 32:48]))

                S1 = c_("slot1")

                def slots(e, s, y, lo, weighted):
                    r, c = [t[:, s, e:e + 1] if isinstance(e, int) else t[:, s, bass.ds(e, 1)] for t in (rk, cmb)]
                    if weighted:
                        return ts(WB[:, s, y], lo, r, c, ALU.is_equal, ALU.mult)
                    return ts(PB[:, s, y], lo, r, None, ALU.is_equal)

                def weights(p, n):
                    wait(v, "turn_w", n)
                    for j in range(8):
                        slots(2 * p + j // 2 % 2, j % 2, j // 2 % 2, S1[:, 0:SLOTS], j >= 4).then_inc(S("pw"), 1)
                    v.wait_ge(S("pw"), 8 * n + 8)

                def copy(dst, src, sem, value):
                    v.tensor_copy(dst, src).then_inc(S(sem), 1)
                    v.wait_ge(S(sem), value)

                def by_k(hid):
                    return hid.rearrange("s (k q) -> s q k", k=FE // P)

                def row(x):
                    return x.rearrange("s (q k) -> s q k", k=FE // P)

                def wts(n, par, b):
                    v.wait_ge(S("turn_w"), n + 1)
                    copy(WTS[:, par], bank(b, 0, N2), "wts", n + 1)

                def xg(n, banks):
                    v.wait_ge(S("turn_x"), n + 1)
                    for j in range(2):
                        copy(XG[:, 4 * j:4 * j + 4], bank(banks[j]).rearrange("p (k t) -> p k t", k=4), "xg", 2 * n + j + 1)

                def pair(n, par, more=True):
                    here, there = BANKS[par], BANKS[1 - par]
                    v.wait_ge(S("up"), 2 * n + 2)
                    v.wait_ge(S("silu"), n + 1)
                    tt(by_k(HID), row(SG), row(bank(here[1])), ALU.mult).then_inc(S("hid"), 1)
                    v.wait_ge(S("hid"), n + 1)
                    v.wait_ge(S("turn_h"), n + 1)
                    copy(HTS, bank(here[0]).rearrange("p (f t) -> p f t", f=4), "hts", n + 1)
                    if more:
                        wts(n + 1, 1 - par, here[1])
                        xg(n + 1, there)

                n0 = NPAIR * l
                weights(0, n0)
                wts(n0, 0, BANKS[0][0])
                xg(n0, BANKS[1])
                weights(1, n0 + 1)
                fl, cu = RT[0:1, 832:880], RT[0:1, 880:928]
                for b in range(3):
                    go(ts(RT[0:1, 832 + 16 * b:848 + 16 * b], cnt, 64.0 * (b + 1), None, ALU.is_gt), "dve")
                go(v.tensor_tensor_scan(cu, ones[0:1, 0:48], fl, 0.0, ALU.mult, ALU.add), "dve")
                go(tt(fl, fl, cu, ALU.mult), "dve")
                eq = RT[0:1, 1024:1408].rearrange("p (j i) -> p j i", j=8)
                ec = RT[0:1, 1408:1792].rearrange("p (j i) -> p j i", j=8)
                go(tt(eq, mid(fl, 8), last(c_("j1")[0:1], 48), ALU.is_equal), "dve")
                fx = RT[0:1, 1792:1816]
                for j, code in enumerate(("code_e", "code_b")):
                    go(tt(ec, eq, mid(c_(code)[0:1], 8), ALU.mult), "dve")
                    go(v.tensor_reduce(fx[:, 8 * j:8 * j + 8], ec, AX.X, ALU.add), "dve")
                go(v.tensor_copy(fx[:, 16:17], cu[:, 47:48]), "dve")
                cum = sm(632, 8)[0:1, 0:1]
                if l == 0:
                    go(v.memset(cum, 0.0), "dve")
                go(ts(fx[:, 17:18], cum, 1.0, None, ALU.add), "dve")
                go(tt(cum, cum, cu[:, 47:48], ALU.add), "dve")
                go(v.tensor_copy(EXI[0:1, 0:18], fx[:, 0:18]), "table")

                pair(n0, 0)
                weights(2, n0 + 2)
                pair(n0 + 1, 1)
                weights(3, n0 + 3)
                with v.Fori(1, NPAIR // 2 - 1) as i:
                    pair(2 * i + n0, 0)
                    weights(2 * i + 2, 2 * i + (n0 + 2))
                    pair(2 * i + (n0 + 1), 1)
                    weights(2 * i + 3, 2 * i + (n0 + 3))
                pair(n0 + 6, 0)
                pair(n0 + 7, 1, False)
                nx = v.value_load(EXI[0:1, 16:17], min_val=0, max_val=8)
                before = v.value_load(EXI[0:1, 17:18], min_val=1, max_val=64)
                v.wait_ge(S("scatter"), n0 + 8)
                with v.If(nx > 0):
                    with v.Fori(0, nx) as i:
                        e = v.value_load(EXI[0:1, bass.ds(i, 1)], min_val=0, max_val=NE - 1)
                        lo = v.value_load(EXI[0:1, bass.ds(i + 8, 1)], min_val=64, max_val=192)
                        v.wait_ge(S("x_scatter"), before + i)
                        for j in range(4):
                            ins = slots(e, j % 2, 0, S1[:, bass.ds(lo, SLOTS)], j >= 2).then_inc(S("x_p" if j < 3 else "x_pw"), 1)
                            if j < 3:
                                v.wait_ge(S("x_p"), 4 * before + 4 * i + j)
                            else:
                                v.wait_ge(S("x_pw"), before + i)
                        v.wait_ge(S("x_turn_w"), before + i)
                        copy(WTS[0:64, 0], PS[0:64, 5, 0:N2], "x_wts", before + i)
                        v.wait_ge(S("x_turn_x"), before + i)
                        for j, (sem, count) in enumerate((("x_p", 4 * before + 4 * i + 3), ("x_xg", before + i))):
                            copy(XG[:, 4 * j:4 * j + 4, 0:64], bank(6 + j).rearrange("p (k t) -> p k t", k=4)[:, :, 0:64], sem, count)
                        v.wait_ge(S("x_up2"), before + i)
                        v.wait_ge(S("x_silu"), before + i)
                        tt(by_k(HID[0:64]), row(SG[0:64]), row(PS[0:64, 5]), ALU.mult).then_inc(S("x_hid"), 1)
                        v.wait_ge(S("x_hid"), before + i)
                        v.wait_ge(S("x_turn_h"), before + i)
                        copy(HTS[:, :, 0:64], bank(6).rearrange("p (f t) -> p f t", f=4)[:, :, 0:64], "x_hts", before + i)
                v.wait_ge(S("x_scatter"), before + nx)
                residual(None, 0, l, 5, lambda m: bank(m // 2, N2 * (m % 2), N2 * (m % 2) + N2))

            for c in range(4):
                mod(0, c)
            for l in range(DEPTH):
                norm(2 * l, l, 0)
                (lambda: attention(l // 3, l), mlstm, gla)[l % 3]()
                norm(2 * l + 1, l, 3)
                if l + 1 < DEPTH:
                    mod(l + 1, 8)
                moe(l)
            norm(2 * DEPTH)


INS = ["x_prompt", "x_sample", "cache_k_0", "cache_v_0", "state_mlstm_C_1", "state_mlstm_n_1", "state_mlstm_m_1",
       "state_gla_S_2", "cache_k_3", "cache_v_3", "c", "c_ctx", "w_mod", "b_mod", "norm1_g", "norm2_g", "final_g",
       "router_w", "router_b", "moe_wg", "moe_wu", "moe_wd", "attn0_w_qkv", "attn0_sink", "attn0_w_o",
       "mlstm1_w_in", "mlstm1_b_gates", "mlstm1_conv", "mlstm1_norm_g", "mlstm1_w_out", "gla2_w_in", "gla2_w_a1",
       "gla2_w_a2", "gla2_b_a", "gla2_norm_g", "gla2_w_out", "attn3_w_qkv", "attn3_sink", "attn3_w_o"]
OUTS = [("y_prompt", (1, T, D)), ("y_sample", (1, T, D)), ("cache_k_0", (1, T, KV, HD)), ("cache_v_0", (1, T, KV, HD)),
        ("C", (1, 2, MH, MDV, MDK)), ("n", (1, 2, MH, MDK)), ("m", (1, 2, MH)), ("S", (1, 2, GH, GDK, GDV)),
        ("cache_k_3", (1, T, KV, HD)), ("cache_v_3", (1, T, KV, HD))]


def kernel(**inputs):
    import concourse.bacc as bacc
    from concourse.bass_utils import run_bass_kernel_spmd

    nc = bacc.Bacc("TRN2", target_bir_lowering=False, num_devices=1)
    arrays = {f"in_{k}": np.ascontiguousarray(inputs[k]) for k in INS}
    arrays["in_consts"] = constants()
    I = {k[3:]: nc.dram_tensor(k, a.shape, F32, kind="ExternalInput").ap() for k, a in arrays.items()}
    O = {k: nc.dram_tensor(f"out_{k}", s, F32, kind="ExternalOutput").ap() for k, s in OUTS}
    program(nc, I, O)
    r = run_bass_kernel_spmd(nc, [arrays], core_ids=[0])
    return tuple(r.results[0][f"out_{k}"] for k, _ in OUTS)
```
